# Optimizing a Trainium2 kernel written in Bass

```python
import math
import jax, jax.numpy as jnp
from jax import lax
import numpy as np

D_MODEL = 2048
BATCH = 1
SEQ = 1024
DEPTH = 2
DEC_BATCH = 8
DEC_SEQ = 1
PAST_LEN = 8192
PAGE_SIZE = 128

N_A_LAYERS = DEPTH // 2
N_B_LAYERS = DEPTH - N_A_LAYERS
LRU_WIDTH = D_MODEL
LRU_BLOCKS = 8
LRU_BLOCK_W = LRU_WIDTH // LRU_BLOCKS
CONV_W = 4
LRU_C = 8.0
HEAD_DIM = 64
N_Q_HEADS = D_MODEL // HEAD_DIM
N_KV_HEADS = 8
GROUP = N_Q_HEADS // N_KV_HEADS
ATT_WIDTH = N_Q_HEADS * HEAD_DIM
KV_WIDTH = N_KV_HEADS * HEAD_DIM
WINDOW = 128
BLOCK = WINDOW
N_BUCKETS = 32
MAX_DISTANCE = 128
RMS_EPS = 1e-6
NEG_INF = -1e30

kernel_name = "yoco_rglru_swa_sink_decoder_step"

def rmsnorm(x, g):
    xf = x.astype(jnp.float32)
    y = xf * lax.rsqrt(jnp.mean(xf * xf, axis=-1, keepdims=True) + RMS_EPS) * g.astype(jnp.float32)
    return y.astype(x.dtype)

def rel_buckets(dist):
    n = jnp.maximum(dist, 0)
    max_exact = N_BUCKETS // 2
    nf = jnp.maximum(n, 1).astype(jnp.float32)
    large = max_exact + (jnp.log(nf / max_exact) / math.log(MAX_DISTANCE / max_exact)
                         * (N_BUCKETS - max_exact)).astype(jnp.int32)
    large = jnp.minimum(large, N_BUCKETS - 1)
    return jnp.where(n < max_exact, n, large)

def rel_bias(dist, table):
    b = table.astype(jnp.float32)[rel_buckets(dist)]
    b = jnp.transpose(b, (2, 0, 1))
    return b.reshape(N_KV_HEADS, GROUP, b.shape[1], b.shape[2])

def lru_combine(left, right):
    a_l, b_l = left
    a_r, b_r = right
    return a_l * a_r, a_r * b_l + b_r

def rglru_layer(x, conv_prev, h0, g_pre, g_post, w_in, conv_w, conv_b, w_r, b_r, w_i, b_i, lam, w_out):
    B, T, _ = x.shape
    xn = rmsnorm(x, g_pre)
    u, gate = jnp.split(xn @ w_in, 2, axis=-1)
    ext = jnp.concatenate([conv_prev.astype(u.dtype), u], axis=1)
    conv = conv_b
    for tap in range(CONV_W):
        conv = conv + ext[:, tap:tap + T] * conv_w[tap]
    new_conv = ext[:, T:]
    ub = conv.reshape(B, T, LRU_BLOCKS, LRU_BLOCK_W)
    r = jax.nn.sigmoid(jnp.einsum('btnc,ncd->btnd', ub, w_r).reshape(B, T, LRU_WIDTH) + b_r)
    i = jax.nn.sigmoid(jnp.einsum('btnc,ncd->btnd', ub, w_i).reshape(B, T, LRU_WIDTH) + b_i)
    log_a = -LRU_C * r.astype(jnp.float32) * jax.nn.softplus(-lam.astype(jnp.float32))
    a = jnp.exp(log_a)
    mult = jnp.sqrt(-jnp.expm1(2.0 * log_a))
    bterm = mult * (i * conv).astype(jnp.float32)
    bterm = bterm.at[:, 0].add(a[:, 0] * h0.astype(jnp.float32))
    _, h = lax.associative_scan(lru_combine, (a, bterm), axis=1)
    y = h.astype(x.dtype) * jax.nn.silu(gate)
    out = y @ w_out
    return x + rmsnorm(out, g_post), new_conv, h[:, -1]

def shared_kv(x, g_kv, w_kv):
    B, T, _ = x.shape
    k, v = jnp.split(rmsnorm(x, g_kv) @ w_kv, 2, axis=-1)
    return (k.reshape(B, T, N_KV_HEADS, HEAD_DIM), v.reshape(B, T, N_KV_HEADS, HEAD_DIM))

def sink_attend(q, k, v, dist, valid, sinks, table):
    s = jnp.einsum('...qhgd,...khd->...hgqk', q, k).astype(jnp.float32) * (1.0 / math.sqrt(HEAD_DIM))
    s = s + rel_bias(dist, table)
    s = jnp.where(valid, s, NEG_INF)
    sk = sinks.astype(jnp.float32).reshape(N_KV_HEADS, GROUP, 1, 1)
    m = jnp.maximum(jnp.max(s, axis=-1, keepdims=True), sk)
    p = jnp.exp(s - m)
    p = p / (jnp.sum(p, axis=-1, keepdims=True) + jnp.exp(sk - m))
    o = jnp.einsum('...hgqk,...khd->...qhgd', p, v.astype(jnp.float32))
    return o.astype(q.dtype)

def banded_attention(q, k, v, sinks, table):
    B, T = q.shape[0], q.shape[1]
    nblk = T // BLOCK
    qb = q.reshape(B, nblk, BLOCK, N_KV_HEADS, GROUP, HEAD_DIM)
    pad = jnp.zeros((B, BLOCK, N_KV_HEADS, HEAD_DIM), k.dtype)
    kp = jnp.concatenate([pad, k], axis=1).reshape(B, nblk + 1, BLOCK, N_KV_HEADS, HEAD_DIM)
    vp = jnp.concatenate([pad, v], axis=1).reshape(B, nblk + 1, BLOCK, N_KV_HEADS, HEAD_DIM)
    kb = jnp.concatenate([kp[:, :-1], kp[:, 1:]], axis=2)
    vb = jnp.concatenate([vp[:, :-1], vp[:, 1:]], axis=2)
    qi = jnp.arange(BLOCK)[:, None]
    kj = jnp.arange(2 * BLOCK)[None, :]
    dist = qi + BLOCK - kj
    blk = jnp.arange(nblk)[:, None, None]
    valid = (dist >= 0) & (dist < WINDOW) & ((blk * BLOCK - BLOCK + kj) >= 0)
    o = sink_attend(qb, kb, vb, dist, valid[:, None, None], sinks, table)
    return o.reshape(B, T, N_KV_HEADS, GROUP, HEAD_DIM)

def cached_attention(q, k_new, v_new, k_past, v_past, sinks, table):
    T = q.shape[1]
    w_rows = k_past.shape[1]
    k_all = jnp.concatenate([k_past.astype(k_new.dtype), k_new], axis=1)
    v_all = jnp.concatenate([v_past.astype(v_new.dtype), v_new], axis=1)
    kpos = jnp.concatenate([PAST_LEN - w_rows + jnp.arange(w_rows), PAST_LEN + jnp.arange(T)])
    qpos = PAST_LEN + jnp.arange(T)
    dist = qpos[:, None] - kpos[None, :]
    valid = (dist >= 0) & (dist < WINDOW)
    return sink_attend(q, k_all, v_all, dist, valid[None, None], sinks, table)

def swa_layer(x, k, v, k_past, v_past, g_pre, g_post, w_qg, sinks, w_out, table):
    B, T, _ = x.shape
    xn = rmsnorm(x, g_pre)
    q, gate = jnp.split(xn @ w_qg, 2, axis=-1)
    q = q.reshape(B, T, N_KV_HEADS, GROUP, HEAD_DIM)
    if k_past is None:
        o = banded_attention(q, k, v, sinks, table)
    else:
        o = cached_attention(q, k, v, k_past, v_past, sinks, table)
    y = o.reshape(B, T, ATT_WIDTH) * jax.nn.silu(gate)
    return x + rmsnorm(y @ w_out, g_post)

def trunk(x, conv_prev, h_prev, k_past, v_past,
          a_norm_pre, a_norm_post, a_w_in, a_conv_w, a_conv_b, a_w_r, a_b_r, a_w_i, a_b_i,
          a_lambda, a_w_out, kv_norm, w_kv, b_norm_pre, b_norm_post, b_w_qg, b_sinks, b_w_out,
          rel_bias_table):
    conv_out, h_out = [], []
    k = v = None
    for layer in range(DEPTH):
        if layer < N_A_LAYERS:
            i = layer
            x, c, h = rglru_layer(x, conv_prev[i], h_prev[i], a_norm_pre[i], a_norm_post[i],
                                  a_w_in[i], a_conv_w[i], a_conv_b[i], a_w_r[i], a_b_r[i],
                                  a_w_i[i], a_b_i[i], a_lambda[i], a_w_out[i])
            conv_out.append(c)
            h_out.append(h)
        else:
            j = layer - N_A_LAYERS
            if j == 0:
                k, v = shared_kv(x, kv_norm, w_kv)
            x = swa_layer(x, k, v, k_past, v_past, b_norm_pre[j], b_norm_post[j], b_w_qg[j],
                          b_sinks[j], b_w_out[j], rel_bias_table)
    return x, jnp.stack(conv_out), jnp.stack(h_out), k, v

def setup_inputs(seed: int = 0) -> dict:
    key = jax.random.key(seed)
    ks = jax.random.split(key, 32)

    def nrm(k, shape, scale):
        return jax.random.normal(k, shape, jnp.float32) * scale

    win_rows = min(WINDOW, PAST_LEN)
    u = jax.random.uniform(ks[10], (N_A_LAYERS, LRU_WIDTH), jnp.float32, 0.9, 0.999)
    s = u ** (1.0 / LRU_C)
    a_lambda = jnp.log(s) - jnp.log1p(-s)
    return {
        "x_prompt": nrm(ks[0], (BATCH, SEQ, D_MODEL), 1.0),
        "x_sample": nrm(ks[1], (DEC_BATCH, DEC_SEQ, D_MODEL), 1.0),
        "state_conv": nrm(ks[2], (N_A_LAYERS, DEC_BATCH, CONV_W - 1, LRU_WIDTH), 1.0),
        "state_h": nrm(ks[3], (N_A_LAYERS, DEC_BATCH, LRU_WIDTH), 0.5),
        "cache_k": nrm(ks[4], (DEC_BATCH, win_rows, N_KV_HEADS, HEAD_DIM), 1.0),
        "cache_v": nrm(ks[5], (DEC_BATCH, win_rows, N_KV_HEADS, HEAD_DIM), 1.0),
        "a_norm_pre": 1.0 + nrm(ks[6], (N_A_LAYERS, D_MODEL), 0.05),
        "a_norm_post": 1.0 + nrm(ks[7], (N_A_LAYERS, D_MODEL), 0.05),
        "a_w_in": nrm(ks[8], (N_A_LAYERS, D_MODEL, 2 * LRU_WIDTH), D_MODEL ** -0.5),
        "a_conv_w": nrm(ks[9], (N_A_LAYERS, CONV_W, LRU_WIDTH), CONV_W ** -0.5),
        "a_conv_b": nrm(ks[11], (N_A_LAYERS, LRU_WIDTH), 0.02),
        "a_w_r": nrm(ks[12], (N_A_LAYERS, LRU_BLOCKS, LRU_BLOCK_W, LRU_BLOCK_W), LRU_BLOCK_W ** -0.5),
        "a_b_r": nrm(ks[13], (N_A_LAYERS, LRU_WIDTH), 0.02),
        "a_w_i": nrm(ks[14], (N_A_LAYERS, LRU_BLOCKS, LRU_BLOCK_W, LRU_BLOCK_W), LRU_BLOCK_W ** -0.5),
        "a_b_i": nrm(ks[15], (N_A_LAYERS, LRU_WIDTH), 0.02),
        "a_lambda": a_lambda,
        "a_w_out": nrm(ks[16], (N_A_LAYERS, LRU_WIDTH, D_MODEL), LRU_WIDTH ** -0.5),
        "kv_norm": 1.0 + nrm(ks[17], (D_MODEL,), 0.05),
        "w_kv": nrm(ks[18], (D_MODEL, 2 * KV_WIDTH), D_MODEL ** -0.5),
        "b_norm_pre": 1.0 + nrm(ks[19], (N_B_LAYERS, D_MODEL), 0.05),
        "b_norm_post": 1.0 + nrm(ks[20], (N_B_LAYERS, D_MODEL), 0.05),
        "b_w_qg": nrm(ks[21], (N_B_LAYERS, D_MODEL, 2 * ATT_WIDTH), D_MODEL ** -0.5),
        "b_sinks": nrm(ks[22], (N_B_LAYERS, N_Q_HEADS), 1.0),
        "b_w_out": nrm(ks[23], (N_B_LAYERS, ATT_WIDTH, D_MODEL), ATT_WIDTH ** -0.5),
        "rel_bias_table": nrm(ks[24], (N_BUCKETS, N_Q_HEADS), 0.5),
    }

def reference(x_prompt, x_sample, state_conv, state_h, cache_k, cache_v,
              a_norm_pre, a_norm_post, a_w_in, a_conv_w, a_conv_b, a_w_r, a_b_r, a_w_i, a_b_i,
              a_lambda, a_w_out, kv_norm, w_kv, b_norm_pre, b_norm_post, b_w_qg, b_sinks, b_w_out,
              rel_bias_table):
    weights = (a_norm_pre, a_norm_post, a_w_in, a_conv_w, a_conv_b, a_w_r, a_b_r, a_w_i, a_b_i,
               a_lambda, a_w_out, kv_norm, w_kv, b_norm_pre, b_norm_post, b_w_qg, b_sinks, b_w_out,
               rel_bias_table)
    B = x_prompt.shape[0]
    conv0 = jnp.zeros((N_A_LAYERS, B, CONV_W - 1, LRU_WIDTH), x_prompt.dtype)
    h0 = jnp.zeros((N_A_LAYERS, B, LRU_WIDTH), jnp.float32)
    y_prompt, p_conv, p_h, p_k, p_v = trunk(x_prompt, conv0, h0, None, None, *weights)
    keep = min(WINDOW, x_prompt.shape[1])
    p_k = p_k[:, -keep:]
    p_v = p_v[:, -keep:]
    y_sample, s_conv, s_h, s_k, s_v = trunk(x_sample, state_conv, state_h, cache_k, cache_v, *weights)
    return (y_prompt, y_sample, p_conv, p_h, p_k, p_v, s_conv, s_h, s_k, s_v)


_drawn_inputs = setup_inputs


def setup_inputs(seed=0):
    import zlib

    import numpy as np

    out = dict(_drawn_inputs(seed))
    spreads = {}
    factors = {'a_b_r': 8.0, 'a_b_i': 7.35, 'b_sinks': 7.483}
    for name, (base, spread) in spreads.items():
        noise = np.random.default_rng([zlib.crc32(name.encode()), seed]).standard_normal(out[name].shape)
        drawn = base * np.exp(spread * noise) if base else spread * noise
        out[name] = __import__('jax').numpy.asarray(drawn.astype(out[name].dtype))
    for name, factor in factors.items():
        out[name] = (out[name] * factor).astype(out[name].dtype)
    return out
```

```python
from contextlib import ExitStack

import concourse.bass as bass
import concourse.mybir as mybir
import numpy as np

F32 = mybir.dt.float32
F32R = mybir.dt.float32r
ALU = mybir.AluOpType
ACT = mybir.ActivationFunctionType
AXX = mybir.AxisListType.X

P = 128
D = 2048
SEQ = 1024
NB = 8
NT = SEQ + NB
GROUPS = 3
TG = NT // GROUPS
KT = D // P
QK = 4
NQ = KT // QK
BLK = 128
NBLK = SEQ // BLK
HD = 64
NH = D // HD
NKV = 8
KVW = NKV * HD
CONV = 4
NBUCKET = 32
MAXDIST = 128
EPS = 1e-6
NEG = -1e30
BW = 3 * BLK
LRU_C = 8.0
TINY = 2.0 ** -113

R_GPRE, R_GPOST, R_CW, R_CB, R_BR, R_BI, R_LAM, R_GKV, R_BPRE, R_BPOST, R_SC, R_SH = 0, 1, 2, 6, 7, 8, 9, 10, 11, 12, 13, 37
NROW = R_SH + NB
NOC = 20

A_ITERS, B_ITERS = 8, 4
A_SPLITS = 4 * NQ + 2
O_ITERS = KT // 2


def bucket_one_hot():
    n = np.arange(MAXDIST)
    exact = NBUCKET // 2
    nf = np.maximum(n, 1).astype(np.float32)
    large = exact + (np.log(nf / np.float32(exact)) / np.float32(np.log(MAXDIST / exact)) * np.float32(NBUCKET - exact)).astype(np.int32)
    b = np.where(n < exact, n, np.minimum(large, NBUCKET - 1))
    row = np.zeros((NBUCKET + 1, BW + P), np.float32)
    row[NBUCKET, :BW] = NEG
    for j in range(BLK, 2 * BLK):
        row[b[2 * BLK - 1 - j], j] = 1.0
        row[NBUCKET, j] = 0.0
    for r in range(P):
        row[b[0 if r == 0 else P - r], BW + r] = 1.0
    return row


def build(nc, t):
    ctx = ExitStack()
    with ctx:
        program(nc, t, ctx)


def program(nc, t, ctx):
    def sb(name, shape, dt=F32, where=ctx):
        return where.enter_context(nc.sbuf_tensor(name, shape, dt))

    def dram(name, shape):
        return nc.dram_tensor(name, shape, F32, kind="Internal").ap()

    def sem(name):
        return ctx.enter_context(nc.semaphore(name))

    x_t = dram("x_t", (KT, P, NT))
    y_t = dram("y_t", (KT, P, NT))
    o_t = dram("o_t", (KT, P, NT))
    x1_t = dram("x1_t", (KT, P, NT))
    bias_row = dram("bias_row", (NH, BW))
    bias_blk = dram("bias_blk", (NH, BLK, 2 * BLK))

    xsp = sb("xsp", [P, KT, 2, NT], F32R)
    wsp = sb("wsp", [P, NQ, 2, QK, P], F32R)
    raw = sb("raw", [P, NQ, QK, P])
    rstd = sb("rstd", [P, NT])
    prm = sb("prm", [P, KT, NROW])
    hbr = sb("hbr", [P, KT])
    hbi = sb("hbi", [P, KT])
    sp2 = sb("sp2", [P, KT])
    ident = sb("ident", [P, P])
    ones = sb("ones", [P, P])
    z = ExitStack()
    ocols = sb("ocols", [P, KT, NOC], where=z)
    z.close()
    qs = sb("qs", [P, KT, 2, NB])
    gsm = sb("gsm", [P, KT, NB])
    bsm = sb("bsm", [P, NH])
    skp = sb("skp", [1, NH])
    nsk = sb("nsk", [P, NH])

    z = ExitStack()
    xr = sb("xr", [P, 3, D], where=z)
    st = sb("st", [P, 2, KT, P], where=z)
    dg = sb("dg", [P, 2, P], where=z)
    ohx = sb("ohx", [NBUCKET + 1, BW + P], where=z)
    tab = sb("tab", [NBUCKET + 1, 2, NH], where=z)
    sxs = sb("sxs", [P, 2, 16], where=z)
    spt = sb("spt", [P, 4, KT], where=z)
    z.close()
    z = ExitStack()
    u = sb("u", [P, 4 + NT], where=z)
    cv = sb("cv", [P, 2, NT], where=z)
    gs = sb("gs", [P, NT], where=z)
    h = sb("h", [P, 2, NT], where=z)
    rc = sb("rc", [P, 2, NT], where=z)
    csp = sb("csp", [P, 2, 2, 2, TG], F32R, where=z)
    z.close()
    z = ExitStack()
    acc = sb("acc", [P, NT], where=z)
    stg = sb("stg", [P, 4, 2, NT], where=z)
    rows = sb("rows", [NOC, D], where=z)
    z.close()
    z = ExitStack()
    k1 = sb("k1", [P, NT], where=z)
    k2 = sb("k2", [P, NT], where=z)
    vn = sb("vn", [P, NBLK, P], where=z)
    q = sb("q", [P, 2, NT], where=z)
    gb = sb("gb", [P, NT], where=z)
    bb = sb("bb", [P, 2, 2, 2 * BLK], where=z)
    pp = sb("pp", [P, 2, 2, 2 * BLK], where=z)
    pt = sb("pt", [P, 2, 2, 2 * BLK], where=z)
    kvo = sb("kvo", [P, 3, P], where=z)
    mx = sb("mx", [P, 6, 2], where=z)
    z.close()
    z = ExitStack()
    kc = sb("kc", [P, 4, NB, P], where=z)
    vc = sb("vc", [P, 4, NB, P], where=z)
    kst = sb("kst", [P, NB, P], where=z)
    sa = sb("sa", [P, 2, P], where=z)
    sbm = sb("sbm", [P, 2, P], where=z)
    skr = sb("skr", [1, 256], where=z)
    sx = sb("sx", [P, 6, 2], where=z)
    z.close()

    ps = ctx.enter_context(nc.psum_tensor("ps", [P, 8, 512], F32))
    SETS = (0, 3)
    X0, X1 = 6, 7

    S = {n: sem(n) for n in (
        "held const_in par_in tab_in x_in0 x_in1 x_in2 x_turned par_turned x_staged x_squared x_hi x_lo xt_out0 xt_out1 "
        "dve_step act_step bias_mm bias_sb bias_out blk_out root_in root_done diag diag_mm rstd_ready tab_ready "
        "raw0 raw1 raw2 raw3 w_gained w_hi w_split w_used psum_read ri_done r_read i_read i_turned cv_ready conv_hi conv_lo gs_ready gt_ready "
        "sig_done rc_ready root chain_done y_ready y_out0 y_out1 o_staged o_sq o_out0 o_out1 acc_ready norm_mm "
        "stage_in0 stage_in1 stage_in2 stage_in3 stage_hi stage_used x1_ready x1_scaled x1_sum x1_sq x1_out0 x1_out1 x1_out2 x1_out3 "
        "oc_ready oc_turned oc_sb state_out q_ready s_done s_read negm p_exp p_ready p_turned pt_ready o_done o_read "
        "b_in0 b_in1 vt_ready v_turned kv_ready kv_out yb_out0 yb_out1 fin_ready fin_turned fin_sb fin_out0 fin_out1 ys_out "
        "smp_in smp_pe smp_act smp_dve smp_split ones_ready b_used stage_free").split()}
    RAW = [S[f"raw{i}"] for i in range(NQ)]

    CREDIT = NQ
    Q_O1 = 16 * A_ITERS
    Q_B = Q_O1 + 64
    Q_O2 = Q_B + 160
    Q_END = Q_O2 + 64
    C_O1, C_B, C_O2 = Q_O1 // NQ, Q_B // NQ, Q_O2 // NQ
    W_O1 = A_SPLITS * A_ITERS
    W_B = W_O1 + 64
    W_O2 = W_B + 160

    def grp(g):
        return slice(g * TG, (g + 1) * TG)

    def hold(eng, s, v):
        eng.wait_ge(s, v)
        eng.sem_inc(S["held"], 1)

    def chunk_done(eng, c):
        eng.wait_ge(S["w_used"], c * NQ + NQ + CREDIT)

    class Chain:

        def __init__(self, eng, s, base=0, per=0, i=0):
            self.eng, self.s, self.base, self.per, self.i, self.n = eng, s, base, per, i, 0

        def step(self, op):
            op.then_inc(self.s, 1)
            self.n += 1

        def wait(self):
            self.eng.wait_ge(self.s, self.i * self.per + (self.base + self.n))

        def link(self, op):
            self.step(op)
            self.wait()

        def end(self, iters=1):
            assert not self.per or self.n == self.per, self.n
            return self.base + (self.per * iters if self.per else self.n)

    w_in = t["a_w_in"][0].rearrange("(k p) n -> p k n", p=P)
    w_r = t["a_w_r"][0].rearrange("n (k p) c -> n p k c", p=P)
    w_i = t["a_w_i"][0].rearrange("n (k p) c -> n p k c", p=P)
    w_oa = t["a_w_out"][0].rearrange("(k p) n -> p k n", p=P)
    w_kv = t["w_kv"].rearrange("(k p) n -> p k n", p=P)
    w_qg = t["b_w_qg"][0].rearrange("(k p) n -> p k n", p=P)
    w_ob = t["b_w_out"][0].rearrange("(k p) n -> p k n", p=P)

    B_CHUNKS = [("k", 0), ("v", 0), ("q", 0), ("q", 1), ("g", 0), ("q", 2), ("g", 1), ("q", 3), ("g", 2), ("g", 3)]
    ATT_AT = [3, 4, 6, 8]
    Q_CHUNK, G_CHUNK = [2, 3, 5, 7], [4, 6, 8, 9]
    NBC = len(B_CHUNKS)

    block = ctx.enter_context(nc.Block())

    @block.sync
    def _(sp):
        sp.dma_start(ident[:], t["ident"]).then_inc(S["const_in"], 16)
        par = [(R_GPRE, t["a_norm_pre"]), (R_GPOST, t["a_norm_post"]), (R_CW, t["a_conv_w"][0]),
               (R_CB, t["a_conv_b"]), (R_BR, t["a_b_r"]), (R_BI, t["a_b_i"]), (R_LAM, t["a_lambda"]),
               (R_GKV, t["kv_norm"].rearrange("(a n) -> a n", a=1)), (R_BPRE, t["b_norm_pre"]),
               (R_BPOST, t["b_norm_post"]), (R_SC, t["state_conv"][0].rearrange("b w n -> (b w) n")),
               (R_SH, t["state_h"][0])]
        for r, src in par:
            sp.dma_start(xr[r:r + src.shape[0], 2, :], src).then_inc(S["par_in"], 16)
        sp.dma_start(ohx[:], t["onehot"]).then_inc(S["tab_in"], 16)
        sp.dma_start(tab[0:NBUCKET, 0, :], t["rel_bias_table"]).then_inc(S["tab_in"], 16)
        sp.dma_start(nsk[:], bass.AP(t["b_sinks"].tensor, 0, [[0, P], [1, NH]])).then_inc(S["tab_in"], 16)
        sp.dma_start(skp[:], t["b_sinks"]).then_inc(S["tab_in"], 16)
        xs = t["x_sample"].rearrange("b o n -> (b o) n")
        for n in range(9):
            slot = n % 3
            if n == 2:
                sp.wait_ge(S["par_turned"], 2)
            elif n > 2:
                sp.wait_ge(S["x_squared"], n - 2)
            if n < 8:
                sp.dma_start(xr[:, slot, :], t["x_prompt"][0, n * P:(n + 1) * P, :]).then_inc(S[f"x_in{slot}"], 16)
            else:
                sp.dma_start(xr[0:NB, slot, :], xs).then_inc(S[f"x_in{slot}"], 16)
        sp.dma_start(t["sample_conv"][0, :, 0:2, :], t["state_conv"][0, :, 1:3, :]).then_inc(S["state_out"], 16)

        def quarter(slot, src, split_before):
            sp.wait_ge(S["w_split"], split_before + 1 + CREDIT)
            sp.dma_start(raw[:, slot, :, :], src).then_inc(RAW[slot], 16)

        def chunk(w, col, base):
            for j in range(NQ):
                quarter(j, w[:, j * QK:(j + 1) * QK, bass.ds(col, P)], base + j - NQ)

        def stage(s, n, free, srcs):
            for sm, v in free:
                sp.wait_ge(sm, v)
            for r, src in enumerate(srcs):
                sp.dma_start(stg[:, s, r, 0:src.shape[-1]], src).then_inc(S[f"stage_in{s}"], 16)

        def tile(a, k, cols=NT):
            return a[bass.ds(k, 1), :, 0:cols].rearrange("o p n -> (o p) n")

        sp.wait_ge(S["bias_out"], 16)
        sp.dma_start(bias_blk[:, :, :], bass.AP(bias_row.tensor, BLK - 1, [[BW, NH], [-1, BLK], [1, 2 * BLK]]))\
            .then_inc(S["blk_out"], 16)

        with sp.Fori(0, A_ITERS) as i:
            b = i * A_SPLITS
            for n, off in enumerate((0, P, D)):
                for j in range(NQ):
                    quarter(j, w_in[:, j * QK:(j + 1) * QK, bass.ds(i * 256 + off, P)], b + n * NQ + j - NQ)
            for slot, w in ((0, w_r), (1, w_i)):
                sp.wait_ge(S["w_split"], b + 2 * NQ + slot + 1 + CREDIT)
                sp.dma_start(raw[:, slot, :, :].rearrange("p a b -> p (a b)").rearrange("p (k c) -> p k c", k=2),
                             w[bass.ds(i, 1)].rearrange("o p k c -> p (o k) c")).then_inc(RAW[slot], 16)
            for j, last in enumerate((12, 13, 10, 11)):
                quarter(j, w_in[:, j * QK:(j + 1) * QK, bass.ds(i * 256 + D + P, P)], b + last)
        chunk(w_oa, 0, W_O1)
        sp.wait_ge(S["y_out0"], 16 * A_ITERS + 16)
        sp.wait_ge(S["y_out1"], 16 * A_ITERS + 16)
        with sp.Fori(0, 4) as i:
            for s in range(4):
                stage(s, i, [(S["stage_used"], i * 4 + s + 1)], [tile(y_t, i * 4 + s)])
        chunk(w_oa, P, W_O1 + NQ)
        with sp.Fori(1, O_ITERS) as i:
            for m in range(2):
                chunk(w_oa, i * 256 + m * P, i * 8 + m * NQ + W_O1)
        chunk(w_kv, 0, W_B)
        sp.wait_ge(S["o_sq"], KT + 2)
        sp.wait_ge(S["o_out0"], 16 * O_ITERS + 16)
        sp.wait_ge(S["o_out1"], 16 * O_ITERS + 16)
        sp.wait_ge(S["xt_out0"], 16 * 5)
        sp.wait_ge(S["xt_out1"], 16 * 4)
        with sp.Fori(0, 4) as i:
            for s in range(4):
                stage(s, i, [(S["stage_used"], i * 4 + s + 17), (S[f"x1_out{s}"], i * 16 + 16)], [tile(o_t, i * 4 + s), tile(x_t, i * 4 + s)])

        def group(i, first):
            b = i * 40 + W_B
            for c, (what, j) in enumerate(B_CHUNKS):
                if what == "q":
                    sp.wait_ge(S["b_used"], i * 4 + j + 1)
                    sp.dma_start(bb[:, j % 2, :, :], bias_blk[bass.ds(i * 8 + j * 2, 2)].rearrange("h q k -> q h k"))\
                        .then_inc(S[f"b_in{j % 2}"], 16)
                if first and c == 0:
                    continue
                w, off = {"k": (w_kv, i * P), "v": (w_kv, i * P + KVW), "q": (w_qg, i * 512 + j * P),
                          "g": (w_qg, i * 512 + j * P + D)}[what]
                chunk(w, off, b + c * NQ)

        sp.wait_ge(S["blk_out"], 16)
        group(0, True)
        with sp.Fori(1, B_ITERS) as i:
            group(i, False)
        chunk(w_ob, 0, W_O2)
        sp.wait_ge(S["yb_out0"], 32 * B_ITERS + 16)
        sp.wait_ge(S["yb_out1"], 32 * B_ITERS + 16)
        sp.wait_ge(S["kv_out"], 64 * B_ITERS + 64)
        for cache, new, dst in ((t["cache_k"], t["sample_k"], kc), (t["cache_v"], t["sample_v"], vc)):
            cr = cache.rearrange("b r h d -> b r (h d)").rearrange("b r (c n) -> b c r n", c=4)
            nr = new.rearrange("b o h d -> b (o h d)").rearrange("b (c n) -> b c n", c=4)
            for b in range(NB):
                sp.dma_start(dst[1:P, :, b, :], cr[b, :, 1:P, :].rearrange("c r n -> r c n")).then_inc(S["smp_in"], 16)
                sp.dma_start(dst[0:1, :, b, :], nr[b:b + 1]).then_inc(S["smp_in"], 16)
        sp.wait_ge(S["smp_split"], 2)
        with sp.Fori(0, 4) as i:
            for s in range(4):
                stage(s, i, [(S["stage_used"], i * 4 + s + 33)], [tile(y_t, i * 4 + s, SEQ)])
        chunk(w_ob, P, W_O2 + NQ)
        with sp.Fori(1, O_ITERS) as i:
            for m in range(2):
                chunk(w_ob, i * 256 + m * P, i * 8 + m * NQ + W_O2)
        sp.wait_ge(S["o_sq"], 2 * KT + 2)
        sp.wait_ge(S["o_out0"], 32 * O_ITERS + 16)
        sp.wait_ge(S["o_out1"], 32 * O_ITERS + 16)
        with sp.Fori(0, 4) as i:
            for s in range(4):
                stage(s, i, [(S["fin_turned"], i * 4 + s + 1)], [tile(o_t, i * 4 + s), tile(x1_t, i * 4 + s)])
        sp.wait_ge(S["state_out"], 16 * 5)
        sp.wait_ge(S["kv_out"], 64 * B_ITERS + 64)
        sp.wait_ge(S["fin_out0"], 16 * 9)
        sp.wait_ge(S["fin_out1"], 16 * 9)
        sp.wait_ge(S["ys_out"], 16)
        for s in range(4):
            sp.wait_ge(S[f"x1_out{s}"], 80)

    @block.gpsimd
    def _(pool):
        pool.sem_inc(S["w_split"], CREDIT)
        pool.memset(ones[:], 1.0).then_inc(S["ones_ready"], 1)

        def split(slot, loads, free, count, gain, k0, also=None, gained=None):
            hold(pool, RAW[slot], loads * 16)
            hold(pool, S["w_used"], free + 1 + CREDIT)
            if also is not None:
                hold(pool, S["ri_done"], also)
            hi, lo, w = wsp[:, slot, 0], wsp[:, slot, 1], raw[:, slot]
            if gain is None:
                pool.tensor_copy(hi, w).then_inc(S["w_hi"], 1)
                hold(pool, S["w_hi"], count)
                pool.tensor_tensor(lo, w, hi.bitcast(F32), ALU.subtract).then_inc(S["w_split"], 1)
                return
            for k in range(QK):
                op = pool.tensor_scalar(w[:, k], w[:, k], prm[:, k0 + k, gain:gain + 1], 1.0, ALU.mult, ALU.mult)
            op.then_inc(S["w_gained"], 1)
            hold(pool, S["w_gained"], gained)
            for k in range(QK):
                op = pool.tensor_scalar(hi[:, k], w[:, k], 1.0, 1.0, ALU.mult, ALU.mult)
            op.then_inc(S["w_hi"], 1)
            hold(pool, S["w_hi"], count)
            pool.tensor_tensor(lo, w, hi.bitcast(F32), ALU.subtract).then_inc(S["w_split"], 1)

        pool.wait_ge(S["par_turned"], 2)
        with pool.Fori(0, A_ITERS) as i:
            n = i * A_SPLITS
            for c in range(3):
                for j in range(NQ):
                    split(j, i * (5 if j < 2 else 4) + c + 1, i * 16 + c * NQ + j - NQ, n + c * NQ + j + 1, R_GPRE, j * QK,
                          gained=i * 16 + c * NQ + j + 1)
            for slot in range(2):
                split(slot, i * 5 + 4, i * 16 + 8 + slot, n + 12 + slot + 1, None, 0)
            for j in range(NQ):
                per = 5 if j < 2 else 4
                split(j, i * per + per, i * 16 + 8 + j, n + 14 + j + 1, R_GPRE, j * QK,
                      also=(i * 12 + 12) if j < 2 else None, gained=i * 16 + 12 + j + 1)

        def out_phase(loads, qb, wb):
            with pool.Fori(0, O_ITERS) as i:
                for m in range(2):
                    for j in range(NQ):
                        split(j, i * 2 + m + 1 + loads[j], i * 8 + m * NQ + j - NQ + qb, i * 8 + m * NQ + j + 1 + wb, None, 0)

        loads = [5 * A_ITERS, 5 * A_ITERS, 4 * A_ITERS, 4 * A_ITERS]
        out_phase(loads, Q_O1, W_O1)
        loads = [n + KT for n in loads]
        with pool.Fori(0, B_ITERS) as i:
            for c in range(NBC):
                for j in range(NQ):
                    split(j, i * NBC + c + 1 + loads[j], i * 40 + c * NQ + j - NQ + Q_B, i * 40 + c * NQ + j + 1 + W_B,
                          R_GKV if c < 2 else R_BPRE, j * QK, gained=16 * A_ITERS + i * 40 + c * NQ + j + 1)
        loads = [n + NBC * B_ITERS for n in loads]
        out_phase(loads, Q_O2, W_O2)

    @block.tensor
    def _(pe):
        pe.sem_inc(S["w_used"], CREDIT)
        pe.wait_ge(S["const_in"], 16)
        pe.wait_ge(S["par_in"], 16 * 12)
        for k in range(KT):
            op = pe.transpose(ps[:, X0 + k // 8, (k % 8) * NROW:(k % 8 + 1) * NROW], xr[0:NROW, 2, k * P:(k + 1) * P],
                              ident[0:NROW, 0:NROW])
        op.then_inc(S["x_turned"], 1)
        for n in range(9):
            w = P if n < 8 else NB
            pe.wait_ge(S[f"x_in{n % 3}"], 16 * (n // 3 + 1))
            for j in range(NQ):
                if n >= 2:
                    pe.wait_ge(S["x_staged"], (n - 2) * NQ + j + 1)
                elif n == 1:
                    pe.wait_ge(S["par_turned"], 2)
                for k in range(QK):
                    op = pe.transpose(ps[:, 4 * (n % 2) + j, k * P:k * P + w],
                                      xr[0:w, n % 3, (j * QK + k) * P:(j * QK + k + 1) * P], ident[0:w, 0:w])
                op.then_inc(S["x_turned"], 1)
        pe.wait_ge(S["tab_ready"], 1)
        pe.wait_ge(S["tab_in"], 64)
        pe.wait_ge(S["x_staged"], 9 * NQ)
        pe.matmul(ps[0:NH, 4, 0:BW], tab[:, 0, :], ohx[:, 0:BW], start=True, stop=True)
        pe.matmul(ps[:, 5, 0:NH], ohx[:, BW:BW + P], tab[:, 1, :], start=True, stop=True).then_inc(S["bias_mm"], 1)
        pe.wait_ge(S["ones_ready"], 1)
        for n in range(9):
            w = P if n < 8 else NB
            pe.wait_ge(S["diag"], n + 1)
            pe.matmul(ps[:, (0, 1, 6)[n // 4], (n % 4) * P:(n % 4) * P + w], ones[0:w, :], dg[0:w, n % 2, 0:w],
                      start=True, stop=True).then_inc(S["diag_mm"], 1)

        def gemm(c, w0, which, ready, parts=None):
            b0 = SETS[which]
            pe.wait_ge(S["psum_read"], c + 1)
            for j in range(NQ):
                if ready is not None:
                    pe.wait_ge(S["stage_used"], ready + (j + 1) * QK + CREDIT)
                pe.wait_ge(S["w_split"], w0 + j + 1 + CREDIT)
                for k in range(QK):
                    kk = j * QK + k
                    for n, (wh, xh) in enumerate(((0, 0), (0, 1), (1, 0))):
                        for g in range(GROUPS):
                            op = pe.matmul(ps[:, b0 + g, 0:TG], wsp[:, j, wh, k, :], xsp[:, kk, xh, grp(g)],
                                           start=(kk == 0 and n == 0), stop=(kk == KT - 1 and n == 2))
                    if k == QK - 1:
                        op.then_inc(S["w_used"], 1)
                    if k % 2 == 1 and parts:
                        for f in parts.get(j * 2 + k // 2, ()):
                            f()

        pe.wait_ge(S["x_lo"], 9)
        pe.wait_ge(S["rstd_ready"], 1)
        with pe.Fori(0, A_ITERS) as i:
            w0, c0 = i * A_SPLITS, i * 4
            gemm(c0, w0, 0, None)
            gemm(c0 + 1, w0 + 4, 1, None)
            gemm(c0 + 2, w0 + 8, 0, None)
            pe.wait_ge(S["w_split"], w0 + 14 + CREDIT)
            for g in range(GROUPS):
                pe.wait_ge(S["conv_lo"], i * 3 + g + 1)
                for m in range(2):
                    for gate in range(2):
                        pe.wait_ge(S["r_read" if gate == 0 else "i_read"], i * 6 + g * 2 + m + 1)
                        n = 0
                        for k in range(2):
                            for wh, xh in ((0, 0), (0, 1), (1, 0)):
                                col = k * 256 + m * P
                                w = wsp[:, gate, wh].rearrange("p a b -> p (a b)")[:, col:col + P]
                                op = pe.matmul(ps[:, X0 + gate, 0:TG], w, csp[:, g % 2, xh, k, :],
                                               start=(n == 0), stop=(n == 5))
                                n += 1
                        op.then_inc(S["ri_done"], 1)
            gemm(c0 + 3, w0 + 14, 1, None)

        def out_phase(c_base, w_base, ready):
            with pe.Fori(0, O_ITERS) as i:
                for m in range(2):
                    gemm(i * 2 + m + c_base, i * 8 + m * NQ + w_base, m, ready)

        def norm_sum(count, reads):
            pe.wait_ge(S["psum_read"], reads)
            pe.wait_ge(S["acc_ready"], count)
            for g in range(GROUPS):
                op = pe.matmul(ps[:, 5 + g, 0:TG], ones[:], acc[:, grp(g)], start=True, stop=True)
            op.then_inc(S["norm_mm"], 1)

        out_phase(C_O1, W_O1, 0)
        pe.wait_ge(S["psum_read"], C_B + 2)
        pe.wait_ge(S["oc_ready"], 1)
        for k in range(KT):
            op = pe.transpose(ps[0:NOC, k // 4, (k % 4) * P:(k % 4 + 1) * P], ocols[:, k, :], ident[:])
        op.then_inc(S["oc_turned"], 1)
        norm_sum(1, C_B + 2)
        pe.wait_ge(S["oc_sb"], 1)
        pe.wait_ge(S["rstd_ready"], 2)

        def scores(i, j, b, bank):
            n = i * 32 + j * NBLK + b
            pe.wait_ge(S["s_read"], n + 1)
            if b == 0:
                pe.wait_ge(S["psum_read"], i * NBC + Q_CHUNK[j] + C_B + 3)
            e, lo = j // 2, max(b - 1, 0) * BLK
            for hf in range(2):
                keys, r = (k1 if hf == e else k2), slice(hf * HD, hf * HD + HD)
                op = pe.matmul(ps[:, bank + hf, (BLK if b == 0 else 0):2 * BLK], q[r, j % 2, b * BLK:(b + 1) * BLK],
                               keys[r, lo:(b + 1) * BLK], start=True, stop=True)
            op.then_inc(S["s_done"], 1)

        def turn(i, j, b):
            n = i * 32 + j * NBLK + b
            pe.wait_ge(S["p_ready"], n + 1)
            pe.wait_ge(S["pt_ready"], n + 1)
            if b == 0 and j == 0:
                pe.wait_ge(S["kv_ready"], i + 1)
            for hf in range(2):
                for kt in range(1 if b == 0 else 0, 2):
                    op = pe.transpose(ps[:, X0, (hf * 2 + kt) * P:(hf * 2 + kt + 1) * P],
                                      pp[:, b % 2, hf, kt * P:(kt + 1) * P], ident[:])
            op.then_inc(S["p_turned"], 1)

        def mix(i, j, b):
            n = i * 32 + j * NBLK + b
            pe.wait_ge(S["pt_ready"], n + 2)
            pe.wait_ge(S["o_read"], n + 1)
            first = 1 if b == 0 else 0
            for hf in range(2):
                for kt in range(first, 2):
                    op = pe.matmul(ps[hf * HD:hf * HD + HD, X1, 0:BLK], vn[:, b - 1 + kt, (j // 2) * HD:(j // 2) * HD + HD],
                                   pt[:, b % 2, hf, kt * P:(kt + 1) * P], start=(kt == first), stop=(kt == 1))
            op.then_inc(S["o_done"], 1)

        def turn_kv(i):
            pe.wait_ge(S["psum_read"], i * NBC + C_B + 4)
            pe.wait_ge(S["pt_ready"], i * 32 + 1)
            pe.wait_ge(S["o_read"], i * 32 + 1)
            for b in range(NBLK):
                op = pe.transpose(ps[:, X0 + b // 4, (b % 4) * P:(b % 4 + 1) * P], gb[:, b * BLK:(b + 1) * BLK], ident[:])
            pe.transpose(ps[0:NB, 3, 0:P], gb[:, SEQ:NT], ident[:])
            pe.transpose(ps[:, 3, P:2 * P], k1[:, SEQ - BLK:SEQ], ident[:])
            op = pe.transpose(ps[0:NB, 3, 2 * P:3 * P], k1[:, SEQ:NT], ident[:])
            op.then_inc(S["v_turned"], 1)

        def body(i, first):
            parts = [{} for _ in range(NBC)]

            def at(slot, f):
                parts[slot // 8].setdefault(slot % 8, []).append(f)

            at(2 * 8 + 2, lambda: turn_kv(i))
            for j, c in enumerate(ATT_AT):
                bank = SETS[(c + 1) % 2]
                for b in range(NBLK):
                    at(c * 8 + b + 3, lambda j=j, b=b: mix(i, j, b))
            for j, c in enumerate(ATT_AT):
                for b in range(NBLK):
                    at(c * 8 + b + 2, lambda j=j, b=b: turn(i, j, b))
            for j, c in enumerate(ATT_AT):
                bank = SETS[(c + 1) % 2]
                for b in range(NBLK):
                    at(c * 8 + b, lambda j=j, b=b, bank=bank: scores(i, j, b, bank))
            if first:
                at(7, lambda: norm_sum(2, C_B + 2))
            for c in range(NBC):
                if c == 1 and first:
                    pe.wait_ge(S["rstd_ready"], 3)
                if c - 1 in ATT_AT:
                    j = ATT_AT.index(c - 1)
                    pe.wait_ge(S["s_read"], i * 32 + j * NBLK + NBLK + 1)
                if c == 3:
                    pe.wait_ge(S["kv_ready"], i + 1)
                gemm(i * NBC + c + C_B, i * 40 + c * NQ + W_B, c % 2, 16, parts[c])

        body(0, True)
        with pe.Fori(1, B_ITERS) as i:
            body(i, False)

        pe.wait_ge(S["psum_read"], C_O2 + 2)
        pe.wait_ge(S["smp_in"], 16 * 4 * NB)
        for c in range(4):
            for b in range(NB):
                if b % 4 == 0 and c > 0:
                    pe.wait_ge(S["smp_act"], 2 * (c - 1) + b // 4 + 1)
                op = pe.transpose(ps[:, 1 + b // 4, (b % 4) * P:(b % 4 + 1) * P], kc[:, c, b, :], ident[:])
                if b % 4 == 3:
                    op.then_inc(S["smp_pe"], 1)
            for e in range(2):
                for b in range(NB):
                    if e == 0 and b % 4 == 0:
                        pe.wait_ge(S["smp_act"], 2 * c + b // 4 + 1)
                    col = ((2 * c + e) * NB + b) * 4
                    r = slice(e * HD, e * HD + HD)
                    op = pe.matmul(ps[:, 3 + e, col:col + 4], kst[r, b, :], qs[r, 4 * c + 2 * e:4 * c + 2 * e + 2, :, b],
                                   start=True, stop=True)
            op.then_inc(S["smp_pe"], 1)
        pe.wait_ge(S["smp_dve"], 2)
        for n in range(2):
            pe.transpose(ps[:, 5, n * P:(n + 1) * P], sa[:, n, :], ident[:])
            op = pe.matmul(ps[:, 6, n:n + 1], skr[:, n * P:(n + 1) * P], ones[0:1, 0:1], start=True, stop=True)
        op.then_inc(S["smp_pe"], 1)
        pe.wait_ge(S["smp_dve"], 4)
        for n in range(2):
            op = pe.transpose(ps[:, 7, n * P:(n + 1) * P], sbm[:, n, :], ident[:])
        op.then_inc(S["smp_pe"], 1)
        pe.wait_ge(S["smp_dve"], 5)
        for hk in range(NKV):
            for b in range(NB):
                col = (hk * NB + b) * 4
                op = pe.matmul(ps[0:HD, 0, col:col + 4], vc[:, hk // 2, b, (hk % 2) * HD:(hk % 2) * HD + HD],
                               sa[:, col // P, col % P:col % P + 4], start=True, stop=True)
        op.then_inc(S["smp_pe"], 1)
        pe.wait_ge(S["smp_split"], 2)
        out_phase(C_O2, W_O2, 32)
        norm_sum(3, C_O2 + KT + 2)
        pe.wait_ge(S["rstd_ready"], 4)
        with pe.Fori(0, 4) as i:
            for s in range(4):
                b0 = SETS[s % 2]
                pe.wait_ge(S["fin_ready"], i * 4 + s + 1)
                pe.wait_ge(S["fin_sb"], i * 4 + s + 1)
                for b in range(NBLK):
                    pe.transpose(ps[:, b0 + b // 4, (b % 4) * P:(b % 4 + 1) * P], stg[:, s, 0, b * P:(b + 1) * P], ident[:])
                pe.transpose(ps[0:NB, b0 + 2, 0:P], stg[:, s, 0, SEQ:NT], ident[:]).then_inc(S["fin_turned"], 1)


    @block.scalar
    def _(act):
        for s in range(4):
            act.sem_inc(S[f"x1_out{s}"], 16)
        for n in ("o_out0", "o_out1", "y_out0", "y_out1", "yb_out0", "yb_out1", "fin_out0", "fin_out1"):
            act.sem_inc(S[n], 16)
        act.sem_inc(S["kv_out"], 64)
        act.sem_inc(S["pt_ready"], 1)
        act.sem_inc(S["r_read"], 1)
        act.sem_inc(S["fin_sb"], 2)
        act.wait_ge(S["x_turned"], 1)
        for n in range(2):
            act.activation(prm[:, n * 8:n * 8 + 8, :].rearrange("p a b -> p (a b)"), ps[:, X0 + n, 0:8 * NROW], ACT.Copy)\
                .then_inc(S["par_turned"], 1)
        act.wait_ge(S["root_in"], 1)
        act.activation(spt[:, 1, :], spt[:, 0, :], ACT.Exp, scale=-1.0).then_inc(S["root_done"], 1)
        for n in range(9):
            w = P if n < 8 else NB
            if n >= 2:
                act.wait_ge(S["x_lo"], n - 1)
                act.wait_ge(S[f"xt_out{n % 2}"], 16 * (n // 2))
            for j in range(NQ):
                act.wait_ge(S["x_turned"], n * NQ + j + 2)
                act.activation(st[:, n % 2, j * QK:(j + 1) * QK, 0:w],
                               ps[:, 4 * (n % 2) + j, 0:QK * P].rearrange("p (k c) -> p k c", k=QK)[:, :, 0:w], ACT.Copy)\
                    .then_inc(S["x_staged"], 1)
            act.wait_ge(S["x_staged"], (n + 1) * NQ)
            act.dma_start(x_t[:, :, n * P:n * P + w].rearrange("k p c -> p k c"), st[:, n % 2, :, 0:w])\
                .then_inc(S[f"xt_out{n % 2}"], 16)
        act.wait_ge(S["bias_sb"], 1)
        act.dma_start(bias_row[:, :], rstd[0:NH, 0:BW]).then_inc(S["bias_out"], 16)
        act.wait_ge(S["root_in"], 2)
        act.activation(sxs[:, 1, 0:8], sxs[:, 0, 0:8], ACT.Sqrt).then_inc(S["root_done"], 1)
        act.activation(sxs[0:NB, 1, 8:9], sxs[0:NB, 0, 8:9], ACT.Sqrt).then_inc(S["root_done"], 1)

        def conv_hi(i, g):
            act.activation(csp[:, g % 2, 0, :, :], cv[:, :, grp(g)], ACT.Copy).then_inc(S["conv_hi"], 1)

        def gate_tanh(c, n, which):
            for g in range(GROUPS):
                act.wait_ge(S["gs_ready"], n * GROUPS + g + 1)
                act.activation(ps[:, SETS[which] + g, 0:TG], (gs if c is None else gb)[:, grp(g)], ACT.Tanh, scale=0.5)\
                    .then_inc(S["gt_ready"], 1)

        A_STEPS = 6
        with act.Fori(0, A_ITERS) as i:
            own = Chain(act, S["act_step"], 0, A_STEPS, i)
            act.wait_ge(S["cv_ready"], i * 2 + 2)
            for g in range(2):
                conv_hi(i, g)
            gate_tanh(None, i * 2, 0)
            for g in range(GROUPS):
                for m in range(2):
                    u0 = i * 12 + g * 4 + m * 2
                    k = i * 2 + m
                    hold(act, S["ri_done"], u0 + 1)
                    hm = h[:, m, grp(g)]
                    act.activation(hm, ps[:, X0, 0:TG], ACT.Tanh, bias=hbr[:, bass.ds(k, 1)], scale=0.5).then_inc(S["r_read"], 1)
                    hold(act, S["ri_done"], u0 + 2)
                    act.activation(ps[:, X1, 0:TG], ps[:, X1, 0:TG], ACT.Tanh, bias=hbi[:, bass.ds(k, 1)], scale=0.5)\
                        .then_inc(S["i_turned"], 1)
                    hold(act, S["r_read"], i * 6 + g * 2 + m + 2)
                    own.step(act.activation(hm, hm, ACT.Tanh, bias=sp2[:, bass.ds(k, 1)], scale=sp2[:, bass.ds(k, 1)]))
                if g == 0:
                    act.wait_ge(S["ri_done"], i * 12 + 4)
                    conv_hi(i, 2)
            own.end()
            act.wait_ge(S["rc_ready"], i + 1)
            act.activation(h[:, :, :], h[:, :, :], ACT.Sqrt).then_inc(S["root"], 1)
            act.wait_ge(S["y_ready"], i * 2 + 1)
            act.dma_start(y_t[bass.ds(i * 2, 1)].rearrange("o p n -> (o p) n"), gs[:]).then_inc(S["y_out0"], 16)
            gate_tanh(None, i * 2 + 1, 1)
            act.wait_ge(S["y_ready"], i * 2 + 2)
            act.dma_start(y_t[bass.ds(i * 2 + 1, 1)].rearrange("o p n -> (o p) n"), gs[:]).then_inc(S["y_out1"], 16)

        def restage(loaded, q0, cols):
            for kq in range(4):
                act.wait_ge(S["w_used"], q0 + kq + 1 + CREDIT)
                for s in range(4):
                    act.wait_ge(S[f"stage_in{s}"], loaded + 16 * (kq + 1))
                    act.activation(xsp[:, kq * 4 + s, 0, 0:cols], stg[:, s, 0, 0:cols], ACT.Copy).then_inc(S["stage_hi"], 1)

        def out_phase(c_base, before):
            with act.Fori(0, O_ITERS) as i:
                for m in range(2):
                    c = i * 2 + m
                    chunk_done(act, c + c_base)
                    act.wait_ge(S[f"o_out{m}"], i * 16 + 16 * O_ITERS * before + 16)
                    act.wait_ge(S["o_sq"], c + KT * before + 1)
                    for g in range(GROUPS):
                        act.activation(stg[:, m, 0, grp(g)], ps[:, SETS[m] + g, 0:TG], ACT.Copy)
                        op = act.activation(stg[:, m, 1, grp(g)], ps[:, SETS[m] + g, 0:TG], ACT.Square)
                    op.then_inc(S["psum_read"], 1)
                    act.wait_ge(S["psum_read"], c + c_base + 3)
                    act.dma_start(o_t[bass.ds(c, 1)].rearrange("o p n -> (o p) n"), stg[:, m, 0, :]).then_inc(S[f"o_out{m}"], 16)

        def root_of_norm(n):
            act.wait_ge(S["root_in"], n)
            act.activation(rstd[:], rstd[:], ACT.Sqrt).then_inc(S["root_done"], 1)

        restage(0, Q_O1 - NQ, NT)
        out_phase(C_O1, 0)
        act.wait_ge(S["oc_turned"], 1)
        for n in range(4):
            op = act.activation(rows[:, n * 512:(n + 1) * 512], ps[0:NOC, n, :], ACT.Copy)
        op.then_inc(S["oc_sb"], 1)
        act.wait_ge(S["oc_sb"], 1)
        act.dma_start(t["prompt_conv"][0, 0], rows[0:3, :]).then_inc(S["state_out"], 16)
        act.dma_start(t["sample_conv"][0, :, 2, :], rows[3:11, :]).then_inc(S["state_out"], 16)
        act.dma_start(t["prompt_h"][0], rows[11:12, :]).then_inc(S["state_out"], 16)
        act.dma_start(t["sample_h"][0], rows[12:20, :]).then_inc(S["state_out"], 16)
        root_of_norm(3)
        with act.Fori(0, 4) as i:
            for s in range(4):
                k = i * 4 + s
                hold(act, S["x1_ready"], k + 1)
                act.activation(xsp[:, bass.ds(k, 1), 0, :].rearrange("p o n -> p (o n)"), stg[:, s, 1, :], ACT.Copy)\
                    .then_inc(S["stage_hi"], 1)
                act.activation(stg[:, s, 0, :], stg[:, s, 1, :], ACT.Square).then_inc(S["x1_sq"], 1)
                act.dma_start(x1_t[bass.ds(k, 1)].rearrange("o p n -> (o p) n"), stg[:, s, 1, :]).then_inc(S[f"x1_out{s}"], 16)
        root_of_norm(4)

        pk = t["prompt_k"].rearrange("a r h d -> (a r) (h d)")
        pv = t["prompt_v"].rearrange("a r h d -> (a r) (h d)")
        sk = t["sample_k"].rearrange("b o h d -> (b o) (h d)")
        sv = t["sample_v"].rearrange("b o h d -> (b o) (h d)")

        def keys_values(i):
            act.wait_ge(S["psum_read"], i * NBC + C_B + 3)
            act.activation(k2[0:HD, :], k1[HD:P, :], ACT.Copy)
            act.activation(k2[HD:P, :], k1[0:HD, :], ACT.Copy)
            act.wait_ge(S["v_turned"], i + 1)
            act.wait_ge(S["kv_out"], i * 64 + 64)
            for n in range(2):
                act.activation(vn[:, n * 4:n * 4 + 4, :].rearrange("p a b -> p (a b)"), ps[:, X0 + n, :], ACT.Copy)
            act.activation(kvo[0:NB, 0, :], ps[0:NB, 3, 0:P], ACT.Copy)
            act.activation(kvo[:, 1, :], ps[:, 3, P:2 * P], ACT.Copy)
            act.activation(kvo[0:NB, 2, :], ps[0:NB, 3, 2 * P:3 * P], ACT.Copy).then_inc(S["kv_ready"], 1)
            act.wait_ge(S["kv_ready"], i + 1)
            col = bass.ds(i * P, P)
            act.dma_start(pk[:, col], kvo[:, 1, :]).then_inc(S["kv_out"], 16)
            act.dma_start(pv[:, col], vn[:, NBLK - 1, :]).then_inc(S["kv_out"], 16)
            act.dma_start(sk[:, col], kvo[0:NB, 2, :]).then_inc(S["kv_out"], 16)
            act.dma_start(sv[:, col], kvo[0:NB, 0, :]).then_inc(S["kv_out"], 16)

        def exps(i, j, b):
            n = i * 32 + j * NBLK + b
            lo = BLK if b == 0 else 0
            act.wait_ge(S["negm"], n + 1)
            act.activation(mx[:, 3, :], mx[:, 2, :], ACT.Exp)
            for hf in range(2):
                s = pp[:, b % 2, hf, lo:2 * BLK]
                op = act.activation(s, s, ACT.Exp, bias=mx[:, 1, hf:hf + 1], accum_out=mx[:, 4, hf:hf + 1])
            op.then_inc(S["p_exp"], 1)

        def turned(i, j, b):
            n = i * 32 + j * NBLK + b
            act.wait_ge(S["p_turned"], n + 1)
            if b == 0:
                act.activation(pt[:, 0, :, BLK:2 * BLK], ps[:, X0, :].rearrange("p (h c) -> p h c", h=2)[:, :, BLK:2 * BLK], ACT.Copy)\
                    .then_inc(S["pt_ready"], 1)
            else:
                act.activation(pt[:, b % 2, :, :].rearrange("p h c -> p (h c)"), ps[:, X0, :], ACT.Copy).then_inc(S["pt_ready"], 1)

        def store_y(i, j):
            act.wait_ge(S["y_ready"], i * 4 + j + 1 + 2 * A_ITERS)
            act.dma_start(y_t[bass.ds(i * 4 + j, 1), :, 0:SEQ].rearrange("o p n -> (o p) n"), q[:, j % 2, 0:SEQ])\
                .then_inc(S[f"yb_out{j % 2}"], 16)

        with act.Fori(0, B_ITERS) as i:
            todo = [(16, 0, lambda: keys_values(i))]
            for j in range(4):
                at = ATT_AT[j] * 8
                for b in range(NBLK):
                    todo.append((at + b + 2, 1, lambda j=j, b=b: turned(i, j, b)))
                    todo.append((at + b, 2, lambda j=j, b=b: exps(i, j, b)))
                g = G_CHUNK[j]
                todo.append((g * 8 + 8, 0, lambda j=j, g=g: (gate_tanh(g, i * 4 + j + 2 * A_ITERS, g % 2), store_y(i, j))))
            for _, _, f in sorted(todo, key=lambda x: x[:2]):
                f()

        for c in range(4):
            act.wait_ge(S["smp_pe"], 3 * c + 1)
            for n in range(2):
                act.wait_ge(S["smp_pe"], 3 * c + n + 1)
                act.activation(kst[:, n * 4:n * 4 + 4, :].rearrange("p a b -> p (a b)"), ps[:, 1 + n, :], ACT.Copy)\
                    .then_inc(S["smp_act"], 1)
        act.wait_ge(S["smp_dve"], 3)
        act.activation(sx[:, 3, :], sx[:, 2, :], ACT.Exp)
        for n in range(2):
            op = act.activation(sbm[:, n, :], ps[:, 5, n * P:(n + 1) * P], ACT.Exp, bias=sx[:, 1, n:n + 1],
                                accum_out=sx[:, 4, n:n + 1])
        op.then_inc(S["smp_act"], 1)
        restage(192, Q_O2 - NQ, SEQ)
        out_phase(C_O2, 1)
        root_of_norm(5)
        yp = t["y_prompt"][0].rearrange("(b p) (k c) -> k p b c", p=P, c=P)
        with act.Fori(0, 4) as i:
            for s in range(4):
                k, b0 = i * 4 + s, SETS[s % 2]
                yn = raw[:, 2 * (s % 2):2 * (s % 2) + 2].rearrange("p a b c -> p (a b c)")
                act.wait_ge(S["fin_turned"], k + 1 + CREDIT)
                act.wait_ge(S[f"fin_out{s % 2}"], i * 32 + 16 * (s // 2) + 16)
                for n in range(2):
                    act.activation(yn[:, n * 512:(n + 1) * 512], ps[:, b0 + n, :], ACT.Copy)
                act.activation(rows[0:NB, bass.ds(k * P, P)], ps[0:NB, b0 + 2, 0:P], ACT.Copy).then_inc(S["fin_sb"], 1)
                act.wait_ge(S["fin_sb"], k + 3)
                act.dma_start(yp[bass.ds(k, 1)].rearrange("o p b c -> p (o b) c"), yn.rearrange("p (b c) -> p b c", c=P))\
                    .then_inc(S[f"fin_out{s % 2}"], 16)
        act.dma_start(t["y_sample"].rearrange("b o n -> (b o) n"), rows[0:NB, :]).then_inc(S["ys_out"], 16)

    @block.vector
    def _(dve):
        own = Chain(dve, S["dve_step"])
        for n, v in (("psum_read", 2), ("stage_used", CREDIT), ("fin_turned", CREDIT), ("o_sq", 2), ("s_read", 1),
                     ("o_read", 1), ("i_read", 1)):
            dve.sem_inc(S[n], v)
        dve.wait_ge(S["tab_in"], 64)
        own.link(dve.memset(tab[NBUCKET:NBUCKET + 1, :, :], 1.0))
        own.link(dve.tensor_scalar(sxs[0:1, 0, 0:16], skp[0:1, 0:16], 1.0, None, ALU.mult))
        own.link(dve.tensor_scalar(sxs[0:1, 1, 0:16], skp[0:1, 16:32], 1.0, None, ALU.mult))
        by = tab[0:NBUCKET, :, :].rearrange("p v (c e j w) -> p v c e j w", c=4, e=2, j=2)
        for e in range(2):
            for w in range(2):
                for c in range(4):
                    own.step(dve.tensor_copy(by[:, 1, c, e, :, w], by[:, 0, c, e, :, w ^ e]))
        for half in range(2):
            src = sxs[0:1, half, :].rearrange("p (c e j w) -> p c e j w", c=2, e=2, j=2)
            dst = skp[0:1, half * 16:half * 16 + 16].rearrange("p (c e j w) -> p c e j w", c=2, e=2, j=2)
            for e in range(2):
                for w in range(2):
                    for c in range(2):
                        own.step(dve.tensor_copy(dst[:, c, e, :, w], src[:, c, e, :, w ^ e]))
        own.wait()
        dve.tensor_scalar(nsk[:], nsk[:], -1.0, None, ALU.mult).then_inc(S["tab_ready"], 1)
        dve.wait_ge(S["par_turned"], 2)
        lam = prm[:, :, R_LAM]
        own.link(dve.tensor_scalar(spt[:, 2, :], lam, -1.0, None, ALU.mult))
        dve.tensor_tensor(spt[:, 0, :], lam, spt[:, 2, :], ALU.max).then_inc(S["root_in"], 1)
        own.step(dve.tensor_scalar(hbr[:], prm[:, :, R_BR], 0.5, None, ALU.mult))
        own.step(dve.tensor_scalar(hbi[:], prm[:, :, R_BI], 0.5, None, ALU.mult))
        own.link(dve.tensor_scalar(spt[:, 2, :], spt[:, 2, :], 0.0, 2.0, ALU.max, ALU.mult))
        dve.wait_ge(S["root_done"], 1)
        e_, s_, s2_ = spt[:, 1, :], spt[:, 0, :], spt[:, 3, :]
        own.link(dve.tensor_scalar(s_, e_, 2.0, None, ALU.add))
        own.link(dve.reciprocal(s_, s_))
        own.link(dve.tensor_tensor(s_, s_, e_, ALU.mult))
        own.link(dve.tensor_tensor(s2_, s_, s_, ALU.mult))
        own.link(dve.tensor_scalar(sp2[:], s2_, 1.0 / 17.0, 1.0 / 15.0, ALU.mult, ALU.add))
        for n in (13, 11, 9, 7, 5, 3, 1):
            own.link(dve.tensor_tensor(sp2[:], sp2[:], s2_, ALU.mult))
            own.link(dve.tensor_scalar(sp2[:], sp2[:], 1.0 / n, None, ALU.add))
        own.link(dve.scalar_tensor_tensor(out=sp2[:], in0=sp2[:], scalar=4.0, in1=s_, op0=ALU.mult, op1=ALU.mult))
        own.link(dve.tensor_tensor(sp2[:], sp2[:], spt[:, 2, :], ALU.add))
        for n in range(9):
            w = P if n < 8 else NB
            cols = slice(n * P, n * P + w)
            dve.wait_ge(S["x_staged"], (n + 1) * NQ)
            dve.tensor_copy(xsp[:, :, 0, cols], st[:, n % 2, :, 0:w]).then_inc(S["x_hi"], 1)
            dve.wait_ge(S["x_hi"], n + 1)
            dve.tensor_tensor(xsp[:, :, 1, cols], st[:, n % 2, :, 0:w], xsp[:, :, 0, cols].bitcast(F32), ALU.subtract)\
                .then_inc(S["x_lo"], 1)
            xt = xr[0:w, n % 3, :]
            dve.tensor_tensor_reduce(xt, xt, xt, 1.0, 0.0, ALU.mult, ALU.add, sxs[0:w, 0, n:n + 1]).then_inc(S["x_squared"], 1)
        dve.wait_ge(S["x_squared"], 9)
        dve.wait_ge(S["bias_mm"], 1)
        own.step(dve.tensor_copy(bsm[:], ps[:, 5, 0:NH]))
        dve.tensor_copy(rstd[0:NH, 0:BW], ps[0:NH, 4, 0:BW]).then_inc(S["bias_sb"], 1)

        def mean_eps(out, in_):
            return dve.tensor_scalar(out, in_, 1.0 / D, EPS, ALU.mult, ALU.add)

        own.step(mean_eps(sxs[:, 0, 0:8], sxs[:, 0, 0:8]))
        mean_eps(sxs[0:NB, 0, 8:9], sxs[0:NB, 0, 8:9]).then_inc(S["root_in"], 1)
        dve.wait_ge(S["root_done"], 3)
        own.step(dve.reciprocal(sxs[:, 1, 0:8], sxs[:, 1, 0:8]))
        own.link(dve.reciprocal(sxs[0:NB, 1, 8:9], sxs[0:NB, 1, 8:9]))
        for n in range(9):
            w = P if n < 8 else NB
            if n >= 2:
                dve.wait_ge(S["diag_mm"], n - 1)
            dve.tensor_scalar(dg[0:w, n % 2, 0:w], ident[0:w, 0:w], sxs[0:w, 1, n:n + 1], None, ALU.mult).then_inc(S["diag"], 1)
        dve.wait_ge(S["diag_mm"], 9)
        dve.wait_ge(S["bias_out"], 16)
        own.step(dve.tensor_copy(rstd[:, 0:512], ps[:, 0, :]))
        own.step(dve.tensor_copy(rstd[:, 512:SEQ], ps[:, 1, :]))
        dve.tensor_copy(rstd[:, SEQ:NT], ps[:, 6, 0:NB]).then_inc(S["rstd_ready"], 1)
        dve.wait_ge(S["rstd_ready"], 1)
        dve.wait_ge(S["xt_out0"], 16 * 5)
        dve.wait_ge(S["xt_out1"], 16 * 4)
        own.link(dve.memset(u[:, 0:4], 0.0))

        def evac(c, dst, which, scale=None, last=None):
            chunk_done(dve, c)
            for g in range(GROUPS):
                src = ps[:, SETS[which] + g, 0:TG]
                if scale is None:
                    op = dve.tensor_tensor(dst[:, grp(g)], src, rstd[:, grp(g)], ALU.mult)
                else:
                    op = dve.scalar_tensor_tensor(out=dst[:, grp(g)], in0=src, scalar=scale, in1=rstd[:, grp(g)],
                                                  op0=ALU.mult, op1=ALU.mult)
                if last is None:
                    op.then_inc(S["gs_ready"], 1)
            if last is not None:
                op.then_inc(last, 1)

        def silu(n, dst, which):
            for g in range(GROUPS):
                dve.wait_ge(S["gt_ready"], n * GROUPS + g + 1)
                op = dve.scalar_tensor_tensor(out=dst[:, grp(g)], in0=ps[:, SETS[which] + g, 0:TG], scalar=1.0,
                                              in1=dst[:, grp(g)], op0=ALU.add, op1=ALU.mult)
            op.then_inc(S["psum_read"], 1)

        A_STEPS = 25
        base = own.end()
        with dve.Fori(0, A_ITERS) as i:
            own = Chain(dve, S["dve_step"], base, A_STEPS, i)
            for m in range(2):
                k, c = i * 2 + m, i * 4 + m

                def col(r, w=1, k=k):
                    return prm[:, bass.ds(k, 1), r:r + w].rearrange("p o n -> p (o n)")

                evac(c, u[:, 3:3 + NT], m, last=S["psum_read"])
                dve.wait_ge(S["psum_read"], c + 3)
                oc = ocols[:, bass.ds(k, 1), :].rearrange("p o n -> p (o n)")
                own.step(dve.tensor_copy(oc[:, 0:11], u[:, SEQ:SEQ + 11]))
                v = cv[:, m, :]
                own.link(dve.tensor_scalar(v, u[:, 3:3 + NT], col(R_CW + 3), col(R_CB), ALU.mult, ALU.add))
                for tap in (2, 1, 0):
                    own.link(dve.scalar_tensor_tensor(out=v[:, 0:SEQ], in0=u[:, tap:tap + SEQ], scalar=col(R_CW + tap),
                                                      in1=v[:, 0:SEQ], op0=ALU.mult, op1=ALU.add))
                    op = dve.scalar_tensor_tensor(out=v[:, SEQ:NT], in0=col(R_SC, 3 * NB).rearrange("p (b w) -> p b w", w=3)[:, :, tap],
                                                  scalar=col(R_CW + tap), in1=v[:, SEQ:NT], op0=ALU.mult, op1=ALU.add)
                    if tap:
                        own.link(op)
                    else:
                        op.then_inc(S["cv_ready"], 1)
                dve.wait_ge(S["cv_ready"], i * 2 + m + 1)

            def conv_lo(g):
                dve.wait_ge(S["conv_hi"], i * 3 + g + 1)
                dve.tensor_tensor(csp[:, g % 2, 1, :, :], cv[:, :, grp(g)], csp[:, g % 2, 0, :, :].bitcast(F32), ALU.subtract)\
                    .then_inc(S["conv_lo"], 1)

            conv_lo(0)
            conv_lo(1)
            dve.wait_ge(S["y_out1"], i * 16 + 16)
            evac(i * 4 + 2, gs, 0)
            silu(i * 2, gs, 0)
            for g in range(GROUPS):
                for m in range(2):
                    dve.wait_ge(S["i_turned"], i * 6 + g * 2 + m + 1)
                    if g == 1 and m == 0:
                        conv_lo(2)
                    dve.scalar_tensor_tensor(out=cv[:, m, grp(g)], in0=ps[:, X1, 0:TG], scalar=1.0, in1=cv[:, m, grp(g)],
                                             op0=ALU.add, op1=ALU.mult).then_inc(S["i_read"], 1)
            dve.wait_ge(S["act_step"], i * 6 + 6)
            own.link(dve.tensor_scalar(h[:, :, :], h[:, :, :], TINY, None, ALU.max))
            own.link(dve.tensor_scalar(rc[:, :, :], h[:, :, :], 1.0, None, ALU.add))
            dve.reciprocal(rc[:, :, :], rc[:, :, :]).then_inc(S["rc_ready"], 1)
            dve.wait_ge(S["root"], i + 1)
            own.link(dve.tensor_tensor(h[:, :, :], h[:, :, :], rc[:, :, :], ALU.mult))
            own.step(dve.tensor_tensor(cv[:, :, :], cv[:, :, :], h[:, :, :], ALU.mult))
            own.link(dve.tensor_scalar(rc[:, :, :], rc[:, :, :], 2.0, -1.0, ALU.mult, ALU.add))
            for m in range(2):
                k = i * 2 + m
                h0 = prm[:, bass.ds(k, 1), R_SH:R_SH + NB].rearrange("p o n -> p (o n)")
                own.link(dve.tensor_tensor(rc[:, m, SEQ:NT], rc[:, m, SEQ:NT], h0, ALU.mult))
                own.step(dve.tensor_tensor(h[:, m, SEQ:NT], cv[:, m, SEQ:NT], rc[:, m, SEQ:NT], ALU.add))
                own.link(dve.tensor_tensor_scan(h[:, m, 0:SEQ], rc[:, m, 0:SEQ], cv[:, m, 0:SEQ], 0.0, ALU.mult, ALU.add))
                oc = ocols[:, bass.ds(k, 1), :].rearrange("p o n -> p (o n)")
                dve.tensor_copy(oc[:, 11:20], h[:, m, SEQ - 1:NT]).then_inc(S["oc_ready"], 1)
                if m == 1:
                    dve.wait_ge(S["y_out0"], i * 16 + 32)
                    evac(i * 4 + 3, gs, 1)
                    silu(i * 2 + 1, gs, 1)
                dve.wait_ge(S["psum_read"], i * 4 + m + 5)
                dve.scalar_tensor_tensor(out=gs[:], in0=h[:, m, :], scalar=0.5, in1=gs[:], op0=ALU.mult, op1=ALU.mult)\
                    .then_inc(S["y_ready"], 1)
        base = own.end(A_ITERS)

        def restage(before, cols, q0):
            with dve.Fori(0, 4) as i:
                for s in range(4):
                    k = i * 4 + s
                    dve.wait_ge(S["stage_hi"], k + before + 1)
                    x = xsp[:, bass.ds(k, 1), :, 0:cols]
                    dve.tensor_tensor(x[:, :, 1, :].rearrange("p o n -> p (o n)"), stg[:, s, 0, 0:cols],
                                      x[:, :, 0, :].rearrange("p o n -> p (o n)").bitcast(F32), ALU.subtract)\
                        .then_inc(S["stage_used"], 1)

        def out_phase(c_base, before):
            with dve.Fori(0, O_ITERS) as i:
                for m in range(2):
                    c = i * 2 + m
                    dve.wait_ge(S["psum_read"], c + c_base + 3)
                    dve.wait_ge(S["o_sq"], c + KT * before + 2)
                    dve.tensor_tensor(acc[:], acc[:], stg[:, m, 1, :], ALU.add).then_inc(S["o_sq"], 1)
            dve.wait_ge(S["o_sq"], KT * (before + 1) + 2)

        def clear_acc():
            own.link(dve.memset(acc[:], 0.0))

        def norm(n, root):
            dve.wait_ge(S["norm_mm"], n)
            for g in range(GROUPS):
                op = mean_eps(rstd[:, grp(g)], ps[:, 5 + g, 0:TG])
            op.then_inc(S["root_in"], 1)
            dve.wait_ge(S["root_done"], root)
            dve.reciprocal(rstd[:], rstd[:]).then_inc(S["rstd_ready"], 1)
            dve.wait_ge(S["rstd_ready"], n + 1)

        own = Chain(dve, S["dve_step"], base)
        dve.wait_ge(S["y_out0"], 16 * A_ITERS + 16)
        dve.wait_ge(S["y_out1"], 16 * A_ITERS + 16)
        clear_acc()
        restage(0, NT, 0)
        out_phase(C_O1, 0)
        dve.sem_inc(S["acc_ready"], 1)
        norm(1, 4)
        clear_acc()
        with dve.Fori(0, 4) as i:
            for s in range(4):
                k = i * 4 + s
                dve.wait_ge(S[f"stage_in{s}"], i * 32 + 64 + 32)
                a, b = stg[:, s, 0, :], stg[:, s, 1, :]
                dve.tensor_tensor(a, a, rstd[:], ALU.mult).then_inc(S["x1_scaled"], 1)
                dve.wait_ge(S["x1_scaled"], k + 1)
                dve.scalar_tensor_tensor(out=b, in0=a, scalar=prm[:, bass.ds(k, 1), R_GPOST:R_GPOST + 1].rearrange("p o n -> p (o n)"),
                                         in1=b, op0=ALU.mult, op1=ALU.add).then_inc(S["x1_ready"], 1)
                dve.wait_ge(S["x1_sq"], k + 1)
                dve.tensor_tensor(acc[:], acc[:], a, ALU.add).then_inc(S["x1_sum"], 1)
                x = xsp[:, bass.ds(k, 1), :, :]
                dve.tensor_tensor(x[:, :, 1, :].rearrange("p o n -> p (o n)"), b,
                                  x[:, :, 0, :].rearrange("p o n -> p (o n)").bitcast(F32), ALU.subtract)\
                    .then_inc(S["stage_used"], 1)
                dve.wait_ge(S["x1_sum"], k + 1)
        dve.sem_inc(S["acc_ready"], 1)
        norm(2, 5)
        for s in range(4):
            dve.wait_ge(S[f"x1_out{s}"], 80)
        dve.sem_inc(S["b_used"], 2)

        def softmax_in(i, j, b):
            n = i * 32 + j * NBLK + b
            lo = BLK if b == 0 else 0
            bank = SETS[(ATT_AT[j] + 1) % 2]
            if b == 0:
                hold(dve, S[f"b_in{j % 2}"], i * 32 + 16 * (j // 2) + 16)
            hold(dve, S["s_done"], n + 1)
            for hf in range(2):
                op = dve.tensor_tensor_reduce(pp[:, b % 2, hf, lo:2 * BLK], ps[:, bank + hf, lo:2 * BLK],
                                              bb[:, j % 2, hf, lo:2 * BLK], 1.0, NEG, ALU.add, ALU.max, mx[:, 0, hf:hf + 1])
            op.then_inc(S["s_read"], 1)
            dve.wait_ge(S["s_read"], n + 2)
            sk = nsk[:, bass.ds(i * 8 + j * 2, 2)]
            own.link(dve.scalar_tensor_tensor(out=mx[:, 1, :], in0=mx[:, 0, :], scalar=-1.0, in1=sk, op0=ALU.mult, op1=ALU.min))
            dve.tensor_tensor(mx[:, 2, :], mx[:, 1, :], sk, ALU.subtract).then_inc(S["negm"], 1)
            if b == NBLK - 1:
                dve.sem_inc(S["b_used"], 1)

        def softmax_out(i, j, b):
            n = i * 32 + j * NBLK + b
            lo = BLK if b == 0 else 0
            dve.wait_ge(S["p_exp"], n + 1)
            own.link(dve.tensor_tensor(mx[:, 5, :], mx[:, 3, :], mx[:, 4, :], ALU.add))
            own.link(dve.reciprocal(mx[:, 5, :], mx[:, 5, :]))
            for hf in range(2):
                s = pp[:, b % 2, hf, lo:2 * BLK]
                op = dve.tensor_scalar(s, s, mx[:, 5, hf:hf + 1], None, ALU.mult)
            op.then_inc(S["p_ready"], 1)

        def output(i, j, b):
            n = i * 32 + j * NBLK + b
            dve.wait_ge(S["o_done"], n + 1)
            dve.tensor_copy(q[:, j % 2, b * BLK:(b + 1) * BLK], ps[:, X1, 0:BLK]).then_inc(S["o_read"], 1)

        def chunk_out(i, c):
            what, j = B_CHUNKS[c]
            cc = i * NBC + c + C_B
            if what == "k":
                evac(cc, k1, c % 2, last=S["psum_read"])
            elif what == "v":
                evac(cc, gb, c % 2, last=S["psum_read"])
            elif what == "q":
                dve.wait_ge(S[f"yb_out{j % 2}"], i * 32 + 16 * (j // 2) + 16)
                evac(cc, q[:, j % 2, :], c % 2, scale=0.125, last=S["psum_read"])
                dve.wait_ge(S["psum_read"], cc + 3)
                at = bass.ds(i * 4 + j, 1)
                own.step(dve.tensor_copy(qs[:, at, 0, :].rearrange("p o n -> p (o n)"), q[:, j % 2, SEQ:NT]))
                own.step(dve.tensor_copy(qs[0:HD, at, 1, :].rearrange("p o n -> p (o n)"), q[HD:P, j % 2, SEQ:NT]))
                own.step(dve.tensor_copy(qs[HD:P, at, 1, :].rearrange("p o n -> p (o n)"), q[0:HD, j % 2, SEQ:NT]))
            else:
                evac(cc, gb, c % 2)
                silu(i * 4 + j + 2 * A_ITERS, gb, c % 2)
                dve.wait_ge(S["psum_read"], cc + 3)
                own.step(dve.tensor_copy(gsm[:, bass.ds(i * 4 + j, 1), :].rearrange("p o n -> p (o n)"), gb[:, SEQ:NT]))
                dve.wait_ge(S["o_read"], i * 32 + j * NBLK + NBLK + 1)
                dve.scalar_tensor_tensor(out=q[:, j % 2, 0:SEQ], in0=q[:, j % 2, 0:SEQ], scalar=0.5, in1=gb[:, 0:SEQ],
                                         op0=ALU.mult, op1=ALU.mult).then_inc(S["y_ready"], 1)
                dve.wait_ge(S["y_ready"], i * 4 + j + 1 + 2 * A_ITERS)

        base = own.end()
        with dve.Fori(0, B_ITERS) as i:
            own = Chain(dve, S["dve_step"], base, 4 * 3 + 4 + 32 * 3, i)
            todo = [(c * 8 + 8, 0, lambda c=c: chunk_out(i, c)) for c in range(NBC)]
            for j in range(4):
                at = ATT_AT[j] * 8
                for b in range(NBLK):
                    todo.append((at + b + 4, 1, lambda j=j, b=b: output(i, j, b)))
                    todo.append((at + b + 1, 2, lambda j=j, b=b: softmax_out(i, j, b)))
                    todo.append((at + b, 3, lambda j=j, b=b: softmax_in(i, j, b)))
            for _, _, f in sorted(todo, key=lambda x: x[:2]):
                f()
        own = Chain(dve, S["dve_step"], own.end(B_ITERS))

        dve.wait_ge(S["yb_out0"], 32 * B_ITERS + 16)
        dve.wait_ge(S["yb_out1"], 32 * B_ITERS + 16)
        dve.wait_ge(S["smp_pe"], 12)
        sav = sa[:, :, :].rearrange("p n c -> p (n c)").rearrange("p (c e b t) -> p c e b t", c=4, e=2, b=NB)
        bsv = bsm[:].rearrange("p (c e t) -> p c e t", c=4, e=2)
        for e in range(2):
            psv = ps[:, 3 + e, 0:256].rearrange("p (c e b t) -> p c e b t", c=4, e=2, b=NB)
            for b in range(NB):
                op = dve.tensor_tensor(sav[:, :, e, b, :], psv[:, :, e, b, :], bsv[:, :, e, :], ALU.add)
        op.then_inc(S["smp_dve"], 1)
        skv = skr[:].rearrange("p (h b t) -> p h b t", h=NKV, b=NB)
        for b in range(NB):
            op = dve.tensor_copy(skv[:, :, b, :], skp[:].rearrange("p (h t) -> p h t", h=NKV))
        op.then_inc(S["smp_dve"], 1)
        dve.wait_ge(S["smp_pe"], 13)
        own.step(dve.tensor_reduce(sx[:, 0, :], ps[:, 5, 0:256].rearrange("p (n c) -> p n c", n=2), AXX, ALU.max))
        own.link(dve.tensor_copy(sx[:, 5, :], ps[:, 6, 0:2]))
        own.link(dve.tensor_tensor(sx[:, 0, :], sx[:, 0, :], sx[:, 5, :], ALU.max))
        own.link(dve.tensor_scalar(sx[:, 1, :], sx[:, 0, :], -1.0, None, ALU.mult))
        dve.tensor_tensor(sx[:, 2, :], sx[:, 5, :], sx[:, 1, :], ALU.add).then_inc(S["smp_dve"], 1)
        dve.wait_ge(S["smp_act"], 9)
        own.link(dve.tensor_tensor(sx[:, 5, :], sx[:, 3, :], sx[:, 4, :], ALU.add))
        own.link(dve.reciprocal(sx[:, 5, :], sx[:, 5, :]))
        for n in range(2):
            op = dve.tensor_scalar(sbm[:, n, :], sbm[:, n, :], sx[:, 5, n:n + 1], None, ALU.mult)
        op.then_inc(S["smp_dve"], 1)
        dve.wait_ge(S["smp_pe"], 14)
        dve.tensor_copy(sa[:, :, :].rearrange("p n c -> p (n c)"), ps[:, 7, 0:256]).then_inc(S["smp_dve"], 1)
        dve.wait_ge(S["smp_pe"], 15)
        ov = ps[0:HD, 0, 0:256].rearrange("p (c e b j w) -> p c e b j w", c=4, e=2, b=NB, j=2)
        qv = qs[:].rearrange("p (c e j) v b -> p c e j v b", c=4, e=2)
        for e in range(2):
            for w in range(2):
                hf = e ^ w
                for j in range(2):
                    own.step(dve.tensor_copy(qv[hf * HD:hf * HD + HD, :, e, j, 0, :], ov[:, :, e, :, j, w]))
        own.wait()
        own.link(dve.scalar_tensor_tensor(out=qs[:, :, 0, :], in0=qs[:, :, 0, :], scalar=0.5, in1=gsm[:], op0=ALU.mult, op1=ALU.mult))
        chunk_done(dve, C_O2 - 1)
        dve.tensor_copy(xsp[:, :, 0, SEQ:NT], qs[:, :, 0, :]).then_inc(S["smp_split"], 1)
        dve.wait_ge(S["smp_split"], 1)
        dve.tensor_tensor(xsp[:, :, 1, SEQ:NT], qs[:, :, 0, :], xsp[:, :, 0, SEQ:NT].bitcast(F32), ALU.subtract)\
            .then_inc(S["smp_split"], 1)
        clear_acc()
        restage(32, SEQ, 0)
        out_phase(C_O2, 1)
        dve.sem_inc(S["acc_ready"], 1)
        norm(3, 6)
        with dve.Fori(0, 4) as i:
            for s in range(4):
                k = i * 4 + s
                dve.wait_ge(S[f"stage_in{s}"], i * 32 + 256 + 32)
                a, b = stg[:, s, 0, :], stg[:, s, 1, :]
                dve.tensor_tensor(a, a, rstd[:], ALU.mult).then_inc(S["x1_scaled"], 1)
                dve.wait_ge(S["x1_scaled"], k + KT + 1)
                dve.scalar_tensor_tensor(out=a, in0=a, scalar=prm[:, bass.ds(k, 1), R_BPOST:R_BPOST + 1].rearrange("p o n -> p (o n)"),
                                         in1=b, op0=ALU.mult, op1=ALU.add).then_inc(S["fin_ready"], 1)


_OUTS = [("y_prompt", (1, SEQ, D)), ("y_sample", (NB, 1, D)), ("prompt_conv", (1, 1, 3, D)), ("prompt_h", (1, 1, D)),
         ("prompt_k", (1, BLK, NKV, HD)), ("prompt_v", (1, BLK, NKV, HD)), ("sample_conv", (1, NB, 3, D)),
         ("sample_h", (1, NB, D)), ("sample_k", (NB, 1, NKV, HD)), ("sample_v", (NB, 1, NKV, HD))]


def kernel(**inputs):
    import concourse.bacc as bacc
    from concourse.bass_utils import run_bass_kernel_spmd

    nc = bacc.Bacc("TRN2", target_bir_lowering=False, num_devices=1)
    arrays, t = {}, {}
    for name, a in {**inputs, "ident": np.eye(P, dtype=np.float32), "onehot": bucket_one_hot()}.items():
        a = np.ascontiguousarray(a)
        arrays[f"in_{name}"] = a
        t[name] = nc.dram_tensor(f"in_{name}", a.shape, mybir.dt.from_np(a.dtype), kind="ExternalInput").ap()
    for name, shape in _OUTS:
        t[name] = nc.dram_tensor(f"out_{name}", shape, F32, kind="ExternalOutput").ap()
    build(nc, t)
    r = run_bass_kernel_spmd(nc, [arrays], core_ids=[0])
    return tuple(r.results[0][f"out_{name}"] for name, _ in _OUTS)
```

```python
from contextlib import ExitStack

import concourse.bass as bass
import concourse.mybir as mybir
import numpy as np

F32 = mybir.dt.float32
F32R = mybir.dt.float32r
ALU = mybir.AluOpType
ACT = mybir.ActivationFunctionType
AXX = mybir.AxisListType.X

P = 128
D = 2048
SEQ = 1024
NB = 8
NT = SEQ + NB
GROUPS = 3
TG = NT // GROUPS
KT = D // P
QK = 4
NQ = KT // QK
BLK = 128
NBLK = SEQ // BLK
HD = 64
NH = D // HD
NKV = 8
KVW = NKV * HD
CONV = 4
NBUCKET = 32
MAXDIST = 128
EPS = 1e-6
NEG = -1e30
BW = 3 * BLK
LRU_C = 8.0
TINY = 2.0 ** -113

R_GPRE, R_GPOST, R_CW, R_CB, R_BR, R_BI, R_LAM, R_GKV, R_BPRE, R_BPOST, R_SC, R_SH = 0, 1, 2, 6, 7, 8, 9, 10, 11, 12, 13, 37
NROW = R_SH + NB
NOC = 20

A_ITERS, B_ITERS = 8, 4
A_SPLITS = 4 * NQ + 2
O_ITERS = KT // 2


def bucket_one_hot():
    n = np.arange(MAXDIST)
    exact = NBUCKET // 2
    nf = np.maximum(n, 1).astype(np.float32)
    large = exact + (np.log(nf / np.float32(exact)) / np.float32(np.log(MAXDIST / exact)) * np.float32(NBUCKET - exact)).astype(np.int32)
    b = np.where(n < exact, n, np.minimum(large, NBUCKET - 1))
    row = np.zeros((NBUCKET + 1, BW + P), np.float32)
    row[NBUCKET, :BW] = NEG
    for j in range(BLK, 2 * BLK):
        row[b[2 * BLK - 1 - j], j] = 1.0
        row[NBUCKET, j] = 0.0
    for r in range(P):
        row[b[0 if r == 0 else P - r], BW + r] = 1.0
    return row


def build(nc, t):
    ctx = ExitStack()
    with ctx:
        program(nc, t, ctx)


def program(nc, t, ctx):
    def sb(name, shape, dt=F32, where=ctx):
        return where.enter_context(nc.sbuf_tensor(name, shape, dt))

    def dram(name, shape):
        return nc.dram_tensor(name, shape, F32, kind="Internal").ap()

    def sem(name):
        return ctx.enter_context(nc.semaphore(name))

    x_t = dram("x_t", (KT, P, NT))
    y_t = dram("y_t", (KT, P, NT))
    o_t = dram("o_t", (KT, P, NT))
    x1_t = dram("x1_t", (KT, P, NT))
    bias_row = dram("bias_row", (NH, BW))
    bias_blk = dram("bias_blk", (NH, BLK, 2 * BLK))

    z = ExitStack()
    kc = sb("kc", [P, 4, NB, P], where=z)
    vc = sb("vc", [P, 4, NB, P], where=z)
    z.close()
    xsp = sb("xsp", [P, KT, 2, NT], F32R)
    land = xsp[:, :, :, :].bitcast(F32)
    wsp = sb("wsp", [P, NQ, 2, QK, P], F32R)
    raw = sb("raw", [P, NQ, QK, P])
    rstd = sb("rstd", [P, NT])
    prm = sb("prm", [P, KT, NROW])
    hbr = sb("hbr", [P, KT])
    hbi = sb("hbi", [P, KT])
    sp2 = sb("sp2", [P, KT])
    nsp4 = sb("nsp4", [P, KT])
    ident = sb("ident", [P, P])
    ones = sb("ones", [P, P])
    z = ExitStack()
    ocols = sb("ocols", [P, KT, NOC], where=z)
    z.close()
    qs = sb("qs", [P, KT, 2, NB])
    gsm = sb("gsm", [P, KT, NB])
    bsm = sb("bsm", [P, NH])
    skp = sb("skp", [1, NH])
    nsk = sb("nsk", [P, NH])

    z = ExitStack()
    xr = sb("xr", [P, 3, D], where=z)
    st = sb("st", [P, 2, KT, P], where=z)
    dg = sb("dg", [P, 2, P], where=z)
    ohx = sb("ohx", [NBUCKET + 1, BW + P], where=z)
    tab = sb("tab", [NBUCKET + 1, 2, NH], where=z)
    sxs = sb("sxs", [P, 2, 16], where=z)
    spt = sb("spt", [P, 4, KT], where=z)
    z.close()
    z = ExitStack()
    u = sb("u", [P, 4 + NT], where=z)
    cv = sb("cv", [P, 2, NT], where=z)
    gs = sb("gs", [P, NT], where=z)
    h = sb("h", [P, 2, NT], where=z)
    rc = sb("rc", [P, 2, NT], where=z)
    g1 = u[:, 3:3 + NT]
    csp = sb("csp", [P, 2, 2, 2, TG], F32R, where=z)
    z.close()
    z = ExitStack()
    acc = sb("acc", [P, NT], where=z)
    stg = sb("stg", [P, 4, 2, NT], where=z)
    rows = sb("rows", [NOC, D], where=z)
    z.close()
    z = ExitStack()
    k1 = sb("k1", [P, NT], where=z)
    k2 = sb("k2", [P, NT], where=z)
    vn = sb("vn", [P, NBLK, P], where=z)
    q = sb("q", [P, 2, NT], where=z)
    gb = sb("gb", [P, NT], where=z)
    bb = sb("bb", [P, 2, 2, 2 * BLK], where=z)
    pp = sb("pp", [P, 2, 2, 2 * BLK], where=z)
    pt = sb("pt", [P, 2, 2, 2 * BLK], where=z)
    kvo = sb("kvo", [P, 3, P], where=z)
    mx = sb("mx", [P, 6, 2], where=z)
    z.close()
    z = ExitStack()
    kst = sb("kst", [P, NB, P], where=z)
    sa = sb("sa", [P, 2, P], where=z)
    sbm = sb("sbm", [P, 2, P], where=z)
    skr = sb("skr", [1, 256], where=z)
    sx = sb("sx", [P, 6, 2], where=z)
    z.close()

    ps = ctx.enter_context(nc.psum_tensor("ps", [P, 8, 512], F32))
    SETS = (0, 3)
    X0, X1 = 6, 7

    S = {n: sem(n) for n in (
        "held const_in par_in tab_in x_in0 x_in1 x_in2 x_turned par_turned x_staged x_squared x_hi x_lo xt_out0 xt_out1 "
        "dve_step act_step bias_mm bias_sb bias_out blk_out root_in root_done diag diag_mm rstd_ready tab_ready "
        "raw0 raw1 raw2 raw3 w_gained w_hi w_split w_used psum_read ri_done r_read i_read i_turned cv_ready conv_hi conv_lo gs_ready gt_ready "
        "sig_done w_ready root chain_done y_ready y_out0 y_out1 o_staged o_sq o_out0 o_out1 acc_ready norm_mm "
        "land_in0 land_in1 land_in2 land_in3 stage_hi stage_used x1_ready x1_scaled x1_sum x1_sq x1_out0 x1_out1 x1_out2 x1_out3 "
        "oc_ready oc_turned oc_sb state_out q_ready s_done s_read negm p_exp p_ready p_turned pt_ready o_done o_read "
        "b_in0 b_in1 vt_ready v_turned kv_ready kv_out yb_out0 yb_out1 fin_ready fin_turned fin_sb fin_out0 fin_out1 ys_out "
        "smp_in smp_pe smp_act smp_dve smp_split ones_ready b_used stage_free").split()}
    LAND = [S[f"land_in{i}"] for i in range(NQ)]
    RAW = [S[f"raw{i}"] for i in range(NQ)]

    O2_ORDER = (1, 2, 3, 0)
    G1_SLOTS = (2, 3, 2, 3)
    CREDIT = NQ
    Q_O1 = 16 * A_ITERS
    Q_B = Q_O1 + 64
    Q_O2 = Q_B + 160
    Q_END = Q_O2 + 64
    C_O1, C_B, C_O2 = Q_O1 // NQ, Q_B // NQ, Q_O2 // NQ
    W_O1 = A_SPLITS * A_ITERS
    W_B = W_O1 + 64
    W_O2 = W_B + 160

    def grp(g):
        return slice(g * TG, (g + 1) * TG)

    def hold(eng, s, v):
        eng.wait_ge(s, v)
        eng.sem_inc(S["held"], 1)

    def chunk_done(eng, c):
        eng.wait_ge(S["w_used"], c * NQ + NQ + CREDIT)

    class Chain:

        def __init__(self, eng, s, base=0, per=0, i=0):
            self.eng, self.s, self.base, self.per, self.i, self.n = eng, s, base, per, i, 0

        def step(self, op):
            op.then_inc(self.s, 1)
            self.n += 1

        def wait(self):
            self.eng.wait_ge(self.s, self.i * self.per + (self.base + self.n))

        def link(self, op):
            self.step(op)
            self.wait()

        def end(self, iters=1):
            assert not self.per or self.n == self.per, self.n
            return self.base + (self.per * iters if self.per else self.n)

    w_in = t["a_w_in"][0].rearrange("(k p) n -> p k n", p=P)
    w_r = t["a_w_r"][0].rearrange("n (k p) c -> n p k c", p=P)
    w_i = t["a_w_i"][0].rearrange("n (k p) c -> n p k c", p=P)
    w_oa = t["a_w_out"][0].rearrange("(k p) n -> p k n", p=P)
    w_kv = t["w_kv"].rearrange("(k p) n -> p k n", p=P)
    w_qg = t["b_w_qg"][0].rearrange("(k p) n -> p k n", p=P)
    w_ob = t["b_w_out"][0].rearrange("(k p) n -> p k n", p=P)

    B_CHUNKS = [("k", 0), ("v", 0), ("q", 0), ("q", 1), ("g", 0), ("q", 2), ("g", 1), ("q", 3), ("g", 2), ("g", 3)]
    ATT_AT = [3, 4, 6, 8]
    Q_CHUNK, G_CHUNK = [2, 3, 5, 7], [4, 6, 8, 9]
    NBC = len(B_CHUNKS)

    block = ctx.enter_context(nc.Block())

    @block.sync
    def _(sp):
        sp.dma_start(ident[:], t["ident"]).then_inc(S["const_in"], 16)
        par = [(R_GPRE, t["a_norm_pre"]), (R_GPOST, t["a_norm_post"]), (R_CW, t["a_conv_w"][0]),
               (R_CB, t["a_conv_b"]), (R_BR, t["a_b_r"]), (R_BI, t["a_b_i"]), (R_LAM, t["a_lambda"]),
               (R_GKV, t["kv_norm"].rearrange("(a n) -> a n", a=1)), (R_BPRE, t["b_norm_pre"]),
               (R_BPOST, t["b_norm_post"]), (R_SC, t["state_conv"][0].rearrange("b w n -> (b w) n")),
               (R_SH, t["state_h"][0])]
        for r, src in par:
            sp.dma_start(xr[r:r + src.shape[0], 2, :], src).then_inc(S["par_in"], 16)
        sp.dma_start(ohx[:], t["onehot"]).then_inc(S["tab_in"], 16)
        sp.dma_start(tab[0:NBUCKET, 0, :], t["rel_bias_table"]).then_inc(S["tab_in"], 16)
        sp.dma_start(nsk[:], bass.AP(t["b_sinks"].tensor, 0, [[0, P], [1, NH]])).then_inc(S["tab_in"], 16)
        sp.dma_start(skp[:], t["b_sinks"]).then_inc(S["tab_in"], 16)
        xs = t["x_sample"].rearrange("b o n -> (b o) n")
        for n in range(9):
            slot = n % 3
            if n == 2:
                sp.wait_ge(S["par_turned"], 2)
            elif n > 2:
                sp.wait_ge(S["x_squared"], n - 2)
            if n < 8:
                sp.dma_start(xr[:, slot, :], t["x_prompt"][0, n * P:(n + 1) * P, :]).then_inc(S[f"x_in{slot}"], 16)
            else:
                sp.dma_start(xr[0:NB, slot, :], xs).then_inc(S[f"x_in{slot}"], 16)
        sp.dma_start(t["sample_conv"][0, :, 0:2, :], t["state_conv"][0, :, 1:3, :]).then_inc(S["state_out"], 16)

        def quarter(slot, src, split_before):
            sp.wait_ge(S["w_split"], split_before + 1 + CREDIT)
            sp.dma_start(raw[:, slot, :, :], src).then_inc(RAW[slot], 16)

        def chunk(w, col, base, order=range(NQ)):
            for j, kq in enumerate(order):
                quarter(j, w[:, kq * QK:(kq + 1) * QK, bass.ds(col, P)], base + j - NQ)

        def lands(kq, used, stored, srcs):
            sp.wait_ge(S["w_used"], used + kq + 1 + CREDIT)
            for sm, v in stored:
                sp.wait_ge(S[sm], v)
            for half, src, cols in srcs:
                sp.dma_start(land[:, kq * QK:(kq + 1) * QK, half, 0:cols],
                             src[kq * QK:(kq + 1) * QK, :, 0:cols].rearrange("k p n -> p k n")).then_inc(LAND[kq], 16)

        sp.wait_ge(S["bias_out"], 16)
        sp.dma_start(bias_blk[:, :, :], bass.AP(bias_row.tensor, BLK - 1, [[BW, NH], [-1, BLK], [1, 2 * BLK]]))\
            .then_inc(S["blk_out"], 16)

        with sp.Fori(0, A_ITERS) as i:
            b = i * A_SPLITS
            for n, off in enumerate((0, P, D)):
                for j in range(NQ):
                    quarter(j, w_in[:, j * QK:(j + 1) * QK, bass.ds(i * 256 + off, P)], b + n * NQ + j - NQ)
            for slot, w in ((0, w_r), (1, w_i)):
                sp.wait_ge(S["w_split"], b + 2 * NQ + slot + 1 + CREDIT)
                sp.dma_start(raw[:, slot, :, :].rearrange("p a b -> p (a b)").rearrange("p (k c) -> p k c", k=2),
                             w[bass.ds(i, 1)].rearrange("o p k c -> p (o k) c")).then_inc(RAW[slot], 16)
            for j, last in enumerate((10, 11, 14, 15)):
                quarter(G1_SLOTS[j], w_in[:, j * QK:(j + 1) * QK, bass.ds(i * 256 + D + P, P)], b + last)
        chunk(w_oa, 0, W_O1)
        for kq in range(NQ):
            lands(kq, Q_O1 - NQ, [(f"y_out{m}", 32 * (kq + 1) + 16) for m in range(2)], [(1, y_t, NT)])
        chunk(w_oa, P, W_O1 + NQ)
        with sp.Fori(1, O_ITERS) as i:
            for m in range(2):
                chunk(w_oa, i * 256 + m * P, i * 8 + m * NQ + W_O1)
        chunk(w_kv, 0, W_B)
        for kq in range(NQ):
            lands(kq, Q_B - NQ, [(f"o_out{m}", 32 * (kq + 1) + 16) for m in range(2)] + [("xt_out0", 16 * 5), ("xt_out1", 16 * 4)],
                  [(0, o_t, NT), (1, x_t, NT)])

        def group(i, first):
            b = i * 40 + W_B
            for c, (what, j) in enumerate(B_CHUNKS):
                if what == "q":
                    sp.wait_ge(S["b_used"], i * 4 + j + 1)
                    sp.dma_start(bb[:, j % 2, :, :], bias_blk[bass.ds(i * 8 + j * 2, 2)].rearrange("h q k -> q h k"))\
                        .then_inc(S[f"b_in{j % 2}"], 16)
                if first and c == 0:
                    continue
                w, off = {"k": (w_kv, i * P), "v": (w_kv, i * P + KVW), "q": (w_qg, i * 512 + j * P),
                          "g": (w_qg, i * 512 + j * P + D)}[what]
                chunk(w, off, b + c * NQ)

        sp.wait_ge(S["blk_out"], 16)
        group(0, True)
        with sp.Fori(1, B_ITERS) as i:
            group(i, False)
        chunk(w_ob, 0, W_O2, O2_ORDER)
        sp.wait_ge(S["kv_out"], 64 * B_ITERS + 64)
        sp.wait_ge(S["w_used"], Q_O2 - NQ + 1 + CREDIT)
        for cache, new, dst in ((t["cache_k"], t["sample_k"], kc), (t["cache_v"], t["sample_v"], vc)):
            cr = cache.rearrange("b r h d -> b r (h d)").rearrange("b r (c n) -> b c r n", c=4)
            nr = new.rearrange("b o h d -> b (o h d)").rearrange("b (c n) -> b c n", c=4)
            for b in range(NB):
                sp.dma_start(dst[1:P, :, b, :], cr[b, :, 1:P, :].rearrange("c r n -> r c n")).then_inc(S["smp_in"], 16)
                sp.dma_start(dst[0:1, :, b, :], nr[b:b + 1]).then_inc(S["smp_in"], 16)
            if dst is kc:
                for kq in (1, 2):
                    lands(kq, Q_O2 - NQ, [(f"yb_out{m}", 32 * (kq + 1) + 16) for m in range(2)], [(1, y_t, SEQ)])
        lands(3, Q_O2 - NQ, [(f"yb_out{m}", 32 * B_ITERS + 16) for m in range(2)], [(1, y_t, SEQ)])
        sp.wait_ge(S["smp_pe"], 15)
        lands(0, Q_O2 - NQ, [(f"yb_out{m}", 32 + 16) for m in range(2)], [(1, y_t, SEQ)])
        chunk(w_ob, P, W_O2 + NQ)
        with sp.Fori(1, O_ITERS) as i:
            for m in range(2):
                chunk(w_ob, i * 256 + m * P, i * 8 + m * NQ + W_O2)
        for kq in range(NQ):
            x1_stored = [(f"x1_out{n}", 80) for n in range(4)]
            lands(kq, Q_END - NQ, [(f"o_out{m}", 32 * (kq + 1) + 16 * O_ITERS + 16) for m in range(2)] + x1_stored,
                  [(0, o_t, NT), (1, x1_t, NT)])
        sp.wait_ge(S["state_out"], 16 * 5)
        sp.wait_ge(S["kv_out"], 64 * B_ITERS + 64)
        sp.wait_ge(S["fin_out0"], 16 * 9)
        sp.wait_ge(S["fin_out1"], 16 * 9)
        sp.wait_ge(S["ys_out"], 16)
        for s in range(4):
            sp.wait_ge(S[f"x1_out{s}"], 80)

    @block.gpsimd
    def _(pool):
        pool.sem_inc(S["w_split"], CREDIT)
        pool.memset(ones[:], 1.0).then_inc(S["ones_ready"], 1)

        def split(slot, loads, free, count, gain, k0, also=None, gained=None):
            hold(pool, RAW[slot], loads * 16)
            hold(pool, S["w_used"], free + 1 + CREDIT)
            if also is not None:
                hold(pool, S["ri_done"], also + 1)
            hi, lo, w = wsp[:, slot, 0], wsp[:, slot, 1], raw[:, slot]
            if gain is None:
                pool.tensor_copy(hi, w).then_inc(S["w_hi"], 1)
                hold(pool, S["w_hi"], count)
                pool.tensor_tensor(lo, w, hi.bitcast(F32), ALU.subtract).then_inc(S["w_split"], 1)
                return
            for k in range(QK):
                op = pool.tensor_scalar(w[:, k], w[:, k], prm[:, k0 + k, gain:gain + 1], 1.0, ALU.mult, ALU.mult)
            op.then_inc(S["w_gained"], 1)
            hold(pool, S["w_gained"], gained)
            for k in range(QK):
                op = pool.tensor_scalar(hi[:, k], w[:, k], 1.0, 1.0, ALU.mult, ALU.mult)
            op.then_inc(S["w_hi"], 1)
            hold(pool, S["w_hi"], count)
            pool.tensor_tensor(lo, w, hi.bitcast(F32), ALU.subtract).then_inc(S["w_split"], 1)

        pool.wait_ge(S["par_turned"], 2)
        with pool.Fori(0, A_ITERS) as i:
            n = i * A_SPLITS
            for c in range(3):
                for j in range(NQ):
                    split(j, i * (4 if j < 2 else 5) + c + 1, i * 16 + c * NQ + j - NQ, n + c * NQ + j + 1, R_GPRE, j * QK,
                          also=(i * 12) if c == 0 and j < 2 else None, gained=i * 16 + c * NQ + j + 1)
            for slot in range(2):
                split(slot, i * 4 + 4, i * 16 + 8 + slot, n + 12 + slot + 1, None, 0)
            for j in range(NQ):
                split(G1_SLOTS[j], i * 5 + 4 + j // 2, i * 16 + 10 + j, n + 14 + j + 1, R_GPRE, j * QK, gained=i * 16 + 12 + j + 1)

        def out_phase(loads, qb, wb):
            with pool.Fori(0, O_ITERS) as i:
                for m in range(2):
                    for j in range(NQ):
                        split(j, i * 2 + m + 1 + loads[j], i * 8 + m * NQ + j - NQ + qb, i * 8 + m * NQ + j + 1 + wb, None, 0)

        pool.wait_ge(S["ri_done"], 12 * A_ITERS + 1)
        loads = [4 * A_ITERS, 4 * A_ITERS, 5 * A_ITERS, 5 * A_ITERS]
        out_phase(loads, Q_O1, W_O1)
        loads = [n + KT for n in loads]

        def scale_tiles(base, rstd_count, lands_before):
            pool.wait_ge(S["rstd_ready"], rstd_count)
            for kq in range(NQ):
                pool.wait_ge(LAND[kq], lands_before + 32)
                with pool.Fori(kq * QK, kq * QK + QK) as k:
                    a = land[:, bass.ds(k, 1), 0, :].rearrange("p o n -> p (o n)")
                    pool.tensor_tensor(a, a, rstd[:], ALU.mult).then_inc(S["x1_scaled"], 1)

        def group(i, chunks):
            for c in chunks:
                for j in range(NQ):
                    split(j, i * NBC + c + 1 + loads[j], i * 40 + c * NQ + j - NQ + Q_B, i * 40 + c * NQ + j + 1 + W_B,
                          R_GKV if c < 2 else R_BPRE, j * QK, gained=16 * A_ITERS + i * 40 + c * NQ + j + 1)

        group(0, [0])
        scale_tiles(0, 2, 16)
        group(0, range(1, NBC))
        with pool.Fori(1, B_ITERS) as i:
            group(i, range(NBC))
        loads = [n + NBC * B_ITERS for n in loads]
        out_phase(loads, Q_O2, W_O2)
        scale_tiles(KT, 4, 64)

    @block.tensor
    def _(pe):
        pe.sem_inc(S["w_used"], CREDIT)
        pe.sem_inc(S["ri_done"], 1)
        pe.wait_ge(S["const_in"], 16)
        pe.wait_ge(S["par_in"], 16 * 12)
        for k in range(KT):
            op = pe.transpose(ps[:, X0 + k // 8, (k % 8) * NROW:(k % 8 + 1) * NROW], xr[0:NROW, 2, k * P:(k + 1) * P],
                              ident[0:NROW, 0:NROW])
        op.then_inc(S["x_turned"], 1)
        for n in range(9):
            w = P if n < 8 else NB
            pe.wait_ge(S[f"x_in{n % 3}"], 16 * (n // 3 + 1))
            for j in range(NQ):
                if n >= 2:
                    pe.wait_ge(S["x_staged"], (n - 2) * NQ + j + 1)
                elif n == 1:
                    pe.wait_ge(S["par_turned"], 2)
                for k in range(QK):
                    op = pe.transpose(ps[:, 4 * (n % 2) + j, k * P:k * P + w],
                                      xr[0:w, n % 3, (j * QK + k) * P:(j * QK + k + 1) * P], ident[0:w, 0:w])
                op.then_inc(S["x_turned"], 1)
        pe.wait_ge(S["tab_ready"], 1)
        pe.wait_ge(S["tab_in"], 64)
        pe.wait_ge(S["x_staged"], 9 * NQ)
        pe.matmul(ps[0:NH, 4, 0:BW], tab[:, 0, :], ohx[:, 0:BW], start=True, stop=True)
        pe.matmul(ps[:, 5, 0:NH], ohx[:, BW:BW + P], tab[:, 1, :], start=True, stop=True).then_inc(S["bias_mm"], 1)
        pe.wait_ge(S["ones_ready"], 1)
        for n in range(9):
            w = P if n < 8 else NB
            pe.wait_ge(S["diag"], n + 1)
            pe.matmul(ps[:, (0, 1, 6)[n // 4], (n % 4) * P:(n % 4) * P + w], ones[0:w, :], dg[0:w, n % 2, 0:w],
                      start=True, stop=True).then_inc(S["diag_mm"], 1)

        def gemm(c, w0, which, ready, parts=None, slots=range(NQ), order=range(NQ),
                 before=None):
            b0 = SETS[which]
            pe.wait_ge(S["psum_read"], c + 1)
            for j in range(NQ):
                if before is not None:
                    before(j)
                if ready is not None:
                    pe.wait_ge(S["stage_used"], ready + (j + 1) * QK)
                pe.wait_ge(S["w_split"], w0 + j + 1 + CREDIT)
                for k in range(QK):
                    kk = order[j] * QK + k
                    for n, (wh, xh) in enumerate(((0, 0), (0, 1), (1, 0))):
                        for g in range(GROUPS):
                            op = pe.matmul(ps[:, b0 + g, 0:TG], wsp[:, slots[j], wh, k, :], xsp[:, kk, xh, grp(g)],
                                           start=(j == 0 and k == 0 and n == 0),
                                           stop=(j == NQ - 1 and k == QK - 1 and n == 2))
                    if k == QK - 1:
                        op.then_inc(S["w_used"], 1)
                    if k % 2 == 1 and parts:
                        for f in parts.get(j * 2 + k // 2, ()):
                            f()

        def gates(i, g, m):
            if g == 0 and m == 0:
                pe.wait_ge(S["w_split"], i * A_SPLITS + 14 + CREDIT)
            if m == 0:
                pe.wait_ge(S["conv_lo"], i * 3 + g + 1)
            for gate in range(2):
                pe.wait_ge(S["r_read" if gate == 0 else "i_read"], i * 6 + g * 2 + m + 1)
                for k in range(2):
                    for n, (wh, xh) in enumerate(((0, 0), (0, 1), (1, 0))):
                        col = k * 256 + m * P
                        w = wsp[:, gate, wh].rearrange("p a b -> p (a b)")[:, col:col + P]
                        op = pe.matmul(ps[:, X0 + gate, 0:TG], w, csp[:, g % 2, xh, k, :],
                                       start=(k == 0 and n == 0), stop=(k == 1 and n == 2))
                op.then_inc(S["ri_done"], 1)

        pe.wait_ge(S["x_lo"], 9)
        pe.wait_ge(S["rstd_ready"], 1)
        with pe.Fori(0, A_ITERS) as i:
            w0, c0 = i * A_SPLITS, i * 4
            gemm(c0, w0, 0, None)
            gemm(c0 + 1, w0 + 4, 1, None)
            gemm(c0 + 2, w0 + 8, 0, None)
            gemm(c0 + 3, w0 + 14, 1, None, {n: [lambda n=n: gates(i, n // 2, n % 2)] for n in range(6)}, G1_SLOTS)

        def out_phase(c_base, w_base, ready, order):
            for m in range(2):
                gemm(m + c_base, m * NQ + w_base, m, ready, order=range(NQ) if m else order)
            with pe.Fori(1, O_ITERS) as i:
                for m in range(2):
                    gemm(i * 2 + m + c_base, i * 8 + m * NQ + w_base, m, None)

        def norm_sum(count, reads):
            pe.wait_ge(S["psum_read"], reads)
            pe.wait_ge(S["acc_ready"], count)
            for g in range(GROUPS):
                op = pe.matmul(ps[:, 5 + g, 0:TG], ones[:], acc[:, grp(g)], start=True, stop=True)
            op.then_inc(S["norm_mm"], 1)

        out_phase(C_O1, W_O1, 0, range(NQ))
        pe.wait_ge(S["psum_read"], C_B + 2)
        pe.wait_ge(S["oc_ready"], 1)
        for k in range(KT):
            op = pe.transpose(ps[0:NOC, k // 4, (k % 4) * P:(k % 4 + 1) * P], ocols[:, k, :], ident[:])
        op.then_inc(S["oc_turned"], 1)
        norm_sum(1, C_B + 2)
        pe.wait_ge(S["oc_sb"], 1)
        pe.wait_ge(S["rstd_ready"], 2)

        def scores(i, j, b, bank):
            n = i * 32 + j * NBLK + b
            pe.wait_ge(S["s_read"], n + 1)
            if b == 0:
                pe.wait_ge(S["psum_read"], i * NBC + Q_CHUNK[j] + C_B + 3)
            e, lo = j // 2, max(b - 1, 0) * BLK
            for hf in range(2):
                keys, r = (k1 if hf == e else k2), slice(hf * HD, hf * HD + HD)
                op = pe.matmul(ps[:, bank + hf, (BLK if b == 0 else 0):2 * BLK], q[r, j % 2, b * BLK:(b + 1) * BLK],
                               keys[r, lo:(b + 1) * BLK], start=True, stop=True)
            op.then_inc(S["s_done"], 1)

        def turn(i, j, b):
            n = i * 32 + j * NBLK + b
            pe.wait_ge(S["p_ready"], n + 1)
            pe.wait_ge(S["pt_ready"], n + 1)
            if b == 0 and j == 0:
                pe.wait_ge(S["kv_ready"], i + 1)
            for hf in range(2):
                for kt in range(1 if b == 0 else 0, 2):
                    op = pe.transpose(ps[:, X0, (hf * 2 + kt) * P:(hf * 2 + kt + 1) * P],
                                      pp[:, b % 2, hf, kt * P:(kt + 1) * P], ident[:])
            op.then_inc(S["p_turned"], 1)

        def mix(i, j, b):
            n = i * 32 + j * NBLK + b
            pe.wait_ge(S["pt_ready"], n + 2)
            pe.wait_ge(S["o_read"], n + 1)
            first = 1 if b == 0 else 0
            for hf in range(2):
                for kt in range(first, 2):
                    op = pe.matmul(ps[hf * HD:hf * HD + HD, X1, 0:BLK], vn[:, b - 1 + kt, (j // 2) * HD:(j // 2) * HD + HD],
                                   pt[:, b % 2, hf, kt * P:(kt + 1) * P], start=(kt == first), stop=(kt == 1))
            op.then_inc(S["o_done"], 1)

        def turn_kv(i):
            pe.wait_ge(S["psum_read"], i * NBC + C_B + 4)
            pe.wait_ge(S["pt_ready"], i * 32 + 1)
            pe.wait_ge(S["o_read"], i * 32 + 1)
            for b in range(NBLK):
                op = pe.transpose(ps[:, X0 + b // 4, (b % 4) * P:(b % 4 + 1) * P], gb[:, b * BLK:(b + 1) * BLK], ident[:])
            pe.transpose(ps[0:NB, 3, 0:P], gb[:, SEQ:NT], ident[:])
            pe.transpose(ps[:, 3, P:2 * P], k1[:, SEQ - BLK:SEQ], ident[:])
            op = pe.transpose(ps[0:NB, 3, 2 * P:3 * P], k1[:, SEQ:NT], ident[:])
            op.then_inc(S["v_turned"], 1)

        def squares(kq):
            for k in range(kq * QK, kq * QK + QK):
                pe.wait_ge(S["x1_sq"], k + 1)
                for g in range(GROUPS):
                    op = pe.matmul(ps[:, 5 + g, 0:TG], ones[:], stg[:, k % 4, 1, grp(g)], start=(k == 0), stop=(k == KT - 1))
                op.then_inc(S["x1_sum"], 1)

        def body(i, first):
            parts = [{} for _ in range(NBC)]

            def at(slot, f):
                parts[slot // 8].setdefault(slot % 8, []).append(f)

            at(2 * 8 + 2, lambda: turn_kv(i))
            for j, c in enumerate(ATT_AT):
                bank = SETS[(c + 1) % 2]
                for b in range(NBLK):
                    at(c * 8 + b + 3, lambda j=j, b=b: mix(i, j, b))
            for j, c in enumerate(ATT_AT):
                for b in range(NBLK):
                    at(c * 8 + b + 2, lambda j=j, b=b: turn(i, j, b))
            for j, c in enumerate(ATT_AT):
                bank = SETS[(c + 1) % 2]
                for b in range(NBLK):
                    at(c * 8 + b, lambda j=j, b=b, bank=bank: scores(i, j, b, bank))
            for c in range(NBC):
                if c == 1 and first:
                    pe.wait_ge(S["rstd_ready"], 3)
                if c - 1 in ATT_AT:
                    j = ATT_AT.index(c - 1)
                    pe.wait_ge(S["s_read"], i * 32 + j * NBLK + NBLK + 1)
                if c == 3:
                    pe.wait_ge(S["kv_ready"], i + 1)
                gemm(i * NBC + c + C_B, i * 40 + c * NQ + W_B, c % 2, 16 if first and c == 0 else None, parts[c],
                     before=squares if first and c == 0 else None)

        body(0, True)
        with pe.Fori(1, B_ITERS) as i:
            body(i, False)

        pe.wait_ge(S["psum_read"], C_O2 + 2)
        pe.wait_ge(S["smp_in"], 16 * 4 * NB)
        for c in range(4):
            for b in range(NB):
                if b % 4 == 0 and c > 0:
                    pe.wait_ge(S["smp_act"], 2 * (c - 1) + b // 4 + 1)
                op = pe.transpose(ps[:, 1 + b // 4, (b % 4) * P:(b % 4 + 1) * P], kc[:, c, b, :], ident[:])
                if b % 4 == 3:
                    op.then_inc(S["smp_pe"], 1)
            for e in range(2):
                for b in range(NB):
                    if e == 0 and b % 4 == 0:
                        pe.wait_ge(S["smp_act"], 2 * c + b // 4 + 1)
                    col = ((2 * c + e) * NB + b) * 4
                    r = slice(e * HD, e * HD + HD)
                    op = pe.matmul(ps[:, 3 + e, col:col + 4], kst[r, b, :], qs[r, 4 * c + 2 * e:4 * c + 2 * e + 2, :, b],
                                   start=True, stop=True)
            op.then_inc(S["smp_pe"], 1)
        pe.wait_ge(S["smp_dve"], 2)
        for n in range(2):
            pe.transpose(ps[:, 5, n * P:(n + 1) * P], sa[:, n, :], ident[:])
            op = pe.matmul(ps[:, 6, n:n + 1], skr[:, n * P:(n + 1) * P], ones[0:1, 0:1], start=True, stop=True)
        op.then_inc(S["smp_pe"], 1)
        pe.wait_ge(S["smp_dve"], 4)
        for n in range(2):
            op = pe.transpose(ps[:, 7, n * P:(n + 1) * P], sbm[:, n, :], ident[:])
        op.then_inc(S["smp_pe"], 1)
        pe.wait_ge(S["smp_dve"], 5)
        for hk in range(NKV):
            for b in range(NB):
                col = (hk * NB + b) * 4
                op = pe.matmul(ps[0:HD, 0, col:col + 4], vc[:, hk // 2, b, (hk % 2) * HD:(hk % 2) * HD + HD],
                               sa[:, col // P, col % P:col % P + 4], start=True, stop=True)
        op.then_inc(S["smp_pe"], 1)
        pe.wait_ge(S["smp_split"], 2)
        out_phase(C_O2, W_O2, 32, O2_ORDER)
        norm_sum(2, C_O2 + KT + 2)
        pe.wait_ge(S["rstd_ready"], 4)
        with pe.Fori(0, 4) as i:
            for s in range(4):
                b0 = SETS[s % 2]
                pe.wait_ge(S["fin_ready"], i * 4 + s + 1)
                pe.wait_ge(S["fin_sb"], i * 4 + s + 1)
                y = stg[:, s, 0, :]
                for b in range(NBLK):
                    pe.transpose(ps[:, b0 + b // 4, (b % 4) * P:(b % 4 + 1) * P], y[:, b * BLK:(b + 1) * BLK], ident[:])
                pe.transpose(ps[0:NB, b0 + 2, 0:P], y[:, SEQ:NT], ident[:]).then_inc(S["fin_turned"], 1)


    @block.scalar
    def _(act):
        for s in range(4):
            act.sem_inc(S[f"x1_out{s}"], 16)
        for n in ("o_out0", "o_out1", "y_out0", "y_out1", "yb_out0", "yb_out1", "fin_out0", "fin_out1"):
            act.sem_inc(S[n], 16)
        act.sem_inc(S["kv_out"], 64)
        act.sem_inc(S["pt_ready"], 1)
        act.sem_inc(S["r_read"], 1)
        act.sem_inc(S["fin_sb"], 2)
        act.sem_inc(S["x1_sum"], 4)
        act.wait_ge(S["x_turned"], 1)
        for n in range(2):
            act.activation(prm[:, n * 8:n * 8 + 8, :].rearrange("p a b -> p (a b)"), ps[:, X0 + n, 0:8 * NROW], ACT.Copy)\
                .then_inc(S["par_turned"], 1)
        act.wait_ge(S["root_in"], 1)
        act.activation(spt[:, 1, :], spt[:, 0, :], ACT.Exp, scale=-1.0).then_inc(S["root_done"], 1)
        for n in range(9):
            w = P if n < 8 else NB
            if n >= 2:
                act.wait_ge(S["x_lo"], n - 1)
                act.wait_ge(S[f"xt_out{n % 2}"], 16 * (n // 2))
            for j in range(NQ):
                act.wait_ge(S["x_turned"], n * NQ + j + 2)
                act.activation(st[:, n % 2, j * QK:(j + 1) * QK, 0:w],
                               ps[:, 4 * (n % 2) + j, 0:QK * P].rearrange("p (k c) -> p k c", k=QK)[:, :, 0:w], ACT.Copy)\
                    .then_inc(S["x_staged"], 1)
            act.wait_ge(S["x_staged"], (n + 1) * NQ)
            act.dma_start(x_t[:, :, n * P:n * P + w].rearrange("k p c -> p k c"), st[:, n % 2, :, 0:w])\
                .then_inc(S[f"xt_out{n % 2}"], 16)
        act.wait_ge(S["bias_sb"], 1)
        act.dma_start(bias_row[:, :], rstd[0:NH, 0:BW]).then_inc(S["bias_out"], 16)
        act.wait_ge(S["root_in"], 2)
        act.activation(sxs[:, 1, 0:8], sxs[:, 0, 0:8], ACT.Sqrt).then_inc(S["root_done"], 1)
        act.activation(sxs[0:NB, 1, 8:9], sxs[0:NB, 0, 8:9], ACT.Sqrt).then_inc(S["root_done"], 1)

        def conv_hi(i, g):
            act.activation(csp[:, g % 2, 0, :, :], cv[:, :, grp(g)], ACT.Copy).then_inc(S["conv_hi"], 1)

        def gate_tanh(src, n, which):
            for g in range(GROUPS):
                act.wait_ge(S["gs_ready"], n * GROUPS + g + 1)
                act.activation(ps[:, SETS[which] + g, 0:TG], src[:, grp(g)], ACT.Tanh, scale=0.5)\
                    .then_inc(S["gt_ready"], 1)

        A_STEPS = 12
        with act.Fori(0, A_ITERS) as i:
            own = Chain(act, S["act_step"], 0, A_STEPS, i)
            act.wait_ge(S["cv_ready"], i * 2 + 2)
            for g in range(2):
                conv_hi(i, g)
            gate_tanh(gs, i * 2, 0)
            for g in range(GROUPS):
                for m in range(2):
                    u0 = i * 12 + g * 4 + m * 2
                    k = i * 2 + m
                    hold(act, S["ri_done"], u0 + 2)
                    hm = h[:, m, grp(g)]
                    act.activation(hm, ps[:, X0, 0:TG], ACT.Tanh, bias=hbr[:, bass.ds(k, 1)], scale=0.5).then_inc(S["r_read"], 1)
                    hold(act, S["ri_done"], u0 + 3)
                    act.activation(ps[:, X1, 0:TG], ps[:, X1, 0:TG], ACT.Tanh, bias=hbi[:, bass.ds(k, 1)], scale=0.5)\
                        .then_inc(S["i_turned"], 1)
                    hold(act, S["r_read"], i * 6 + g * 2 + m + 2)
                    own.step(act.activation(rc[:, m, grp(g)], hm, ACT.Exp, bias=nsp4[:, bass.ds(k, 1)], scale=nsp4[:, bass.ds(k, 1)]))
                    hold(act, S["act_step"], i * A_STEPS + own.n)
                    own.step(act.activation(hm, hm, ACT.Tanh, bias=sp2[:, bass.ds(k, 1)], scale=sp2[:, bass.ds(k, 1)]))
                if g == 0:
                    act.wait_ge(S["ri_done"], i * 12 + 5)
                    conv_hi(i, 2)
            own.end()
            act.wait_ge(S["w_ready"], i + 1)
            act.activation(h[:, :, :], h[:, :, :], ACT.Sqrt).then_inc(S["root"], 1)
            gate_tanh(g1, i * 2 + 1, 1)
            act.wait_ge(S["y_ready"], i * 2 + 1)
            act.dma_start(y_t[bass.ds(i * 2, 1)].rearrange("o p n -> (o p) n"), gs[:]).then_inc(S["y_out0"], 16)
            act.wait_ge(S["y_ready"], i * 2 + 2)
            act.dma_start(y_t[bass.ds(i * 2 + 1, 1)].rearrange("o p n -> (o p) n"), g1).then_inc(S["y_out1"], 16)

        def restage(loaded, cols, quarters):
            for kq in quarters:
                act.wait_ge(LAND[kq], loaded)
                for k in range(kq * QK, kq * QK + QK):
                    act.activation(xsp[:, k, 0, 0:cols], xsp[:, k, 1, 0:cols].bitcast(F32), ACT.Copy).then_inc(S["stage_hi"], 1)

        def out_phase(c_base, before):
            with act.Fori(0, O_ITERS) as i:
                for m in range(2):
                    c = i * 2 + m
                    chunk_done(act, c + c_base)
                    act.wait_ge(S[f"o_out{m}"], i * 16 + 16 * O_ITERS * before + 16)
                    act.wait_ge(S["o_sq"], c + KT * before + 1)
                    for g in range(GROUPS):
                        act.activation(stg[:, m, 0, grp(g)], ps[:, SETS[m] + g, 0:TG], ACT.Copy)
                        op = act.activation(stg[:, m, 1, grp(g)], ps[:, SETS[m] + g, 0:TG], ACT.Square)
                    op.then_inc(S["psum_read"], 1)
                    act.wait_ge(S["psum_read"], c + c_base + 3)
                    act.dma_start(o_t[bass.ds(c, 1)].rearrange("o p n -> (o p) n"), stg[:, m, 0, :]).then_inc(S[f"o_out{m}"], 16)

        def root_of_norm(n):
            act.wait_ge(S["root_in"], n)
            act.activation(rstd[:], rstd[:], ACT.Sqrt).then_inc(S["root_done"], 1)

        restage(16, NT, range(NQ))
        out_phase(C_O1, 0)
        act.wait_ge(S["oc_turned"], 1)
        for n in range(4):
            op = act.activation(rows[:, n * 512:(n + 1) * 512], ps[0:NOC, n, :], ACT.Copy)
        op.then_inc(S["oc_sb"], 1)
        act.wait_ge(S["oc_sb"], 1)
        act.dma_start(t["prompt_conv"][0, 0], rows[0:3, :]).then_inc(S["state_out"], 16)
        act.dma_start(t["sample_conv"][0, :, 2, :], rows[3:11, :]).then_inc(S["state_out"], 16)
        act.dma_start(t["prompt_h"][0], rows[11:12, :]).then_inc(S["state_out"], 16)
        act.dma_start(t["sample_h"][0], rows[12:20, :]).then_inc(S["state_out"], 16)
        root_of_norm(3)
        with act.Fori(0, 4) as i:
            for s in range(4):
                k = i * 4 + s
                x1 = stg[:, s, 0, :]
                hold(act, S["x1_ready"], k + 1)
                act.activation(xsp[:, bass.ds(k, 1), 0, :].rearrange("p o n -> p (o n)"), x1, ACT.Copy).then_inc(S["stage_hi"], 1)
                act.wait_ge(S["x1_sum"], k + 1)
                act.activation(stg[:, s, 1, :], x1, ACT.Square).then_inc(S["x1_sq"], 1)
                act.dma_start(x1_t[bass.ds(k, 1)].rearrange("o p n -> (o p) n"), x1).then_inc(S[f"x1_out{s}"], 16)
        root_of_norm(4)

        pk = t["prompt_k"].rearrange("a r h d -> (a r) (h d)")
        pv = t["prompt_v"].rearrange("a r h d -> (a r) (h d)")
        sk = t["sample_k"].rearrange("b o h d -> (b o) (h d)")
        sv = t["sample_v"].rearrange("b o h d -> (b o) (h d)")

        def keys_values(i):
            act.wait_ge(S["psum_read"], i * NBC + C_B + 3)
            act.activation(k2[0:HD, :], k1[HD:P, :], ACT.Copy)
            act.activation(k2[HD:P, :], k1[0:HD, :], ACT.Copy)
            act.wait_ge(S["v_turned"], i + 1)
            act.wait_ge(S["kv_out"], i * 64 + 64)
            for n in range(2):
                act.activation(vn[:, n * 4:n * 4 + 4, :].rearrange("p a b -> p (a b)"), ps[:, X0 + n, :], ACT.Copy)
            act.activation(kvo[0:NB, 0, :], ps[0:NB, 3, 0:P], ACT.Copy)
            act.activation(kvo[:, 1, :], ps[:, 3, P:2 * P], ACT.Copy)
            act.activation(kvo[0:NB, 2, :], ps[0:NB, 3, 2 * P:3 * P], ACT.Copy).then_inc(S["kv_ready"], 1)
            act.wait_ge(S["kv_ready"], i + 1)
            col = bass.ds(i * P, P)
            act.dma_start(pk[:, col], kvo[:, 1, :]).then_inc(S["kv_out"], 16)
            act.dma_start(pv[:, col], vn[:, NBLK - 1, :]).then_inc(S["kv_out"], 16)
            act.dma_start(sk[:, col], kvo[0:NB, 2, :]).then_inc(S["kv_out"], 16)
            act.dma_start(sv[:, col], kvo[0:NB, 0, :]).then_inc(S["kv_out"], 16)

        def exps(i, j, b):
            n = i * 32 + j * NBLK + b
            lo = BLK if b == 0 else 0
            act.wait_ge(S["negm"], n + 1)
            act.activation(mx[:, 3, :], mx[:, 2, :], ACT.Exp)
            for hf in range(2):
                s = pp[:, b % 2, hf, lo:2 * BLK]
                op = act.activation(s, s, ACT.Exp, bias=mx[:, 1, hf:hf + 1], accum_out=mx[:, 4, hf:hf + 1])
            op.then_inc(S["p_exp"], 1)

        def turned(i, j, b):
            n = i * 32 + j * NBLK + b
            act.wait_ge(S["p_turned"], n + 1)
            if b == 0:
                act.activation(pt[:, 0, :, BLK:2 * BLK], ps[:, X0, :].rearrange("p (h c) -> p h c", h=2)[:, :, BLK:2 * BLK], ACT.Copy)\
                    .then_inc(S["pt_ready"], 1)
            else:
                act.activation(pt[:, b % 2, :, :].rearrange("p h c -> p (h c)"), ps[:, X0, :], ACT.Copy).then_inc(S["pt_ready"], 1)

        def store_y(i, j):
            act.wait_ge(S["y_ready"], i * 4 + j + 1 + 2 * A_ITERS)
            act.dma_start(y_t[bass.ds(i * 4 + j, 1), :, 0:SEQ].rearrange("o p n -> (o p) n"), q[:, j % 2, 0:SEQ])\
                .then_inc(S[f"yb_out{j % 2}"], 16)

        with act.Fori(0, B_ITERS) as i:
            todo = [(16, 0, lambda: keys_values(i))]
            for j in range(4):
                at = ATT_AT[j] * 8
                for b in range(NBLK):
                    todo.append((at + b + 2, 1, lambda j=j, b=b: turned(i, j, b)))
                    todo.append((at + b, 2, lambda j=j, b=b: exps(i, j, b)))
                g = G_CHUNK[j]
                todo.append((g * 8 + 8, 0, lambda j=j, g=g: (gate_tanh(gb, i * 4 + j + 2 * A_ITERS, g % 2), store_y(i, j))))
            for _, _, f in sorted(todo, key=lambda x: x[:2]):
                f()

        restage(64, SEQ, (1, 2))
        for c in range(4):
            act.wait_ge(S["smp_pe"], 3 * c + 1)
            for n in range(2):
                act.wait_ge(S["smp_pe"], 3 * c + n + 1)
                act.activation(kst[:, n * 4:n * 4 + 4, :].rearrange("p a b -> p (a b)"), ps[:, 1 + n, :], ACT.Copy)\
                    .then_inc(S["smp_act"], 1)
        act.wait_ge(S["smp_dve"], 3)
        act.activation(sx[:, 3, :], sx[:, 2, :], ACT.Exp)
        for n in range(2):
            op = act.activation(sbm[:, n, :], ps[:, 5, n * P:(n + 1) * P], ACT.Exp, bias=sx[:, 1, n:n + 1],
                                accum_out=sx[:, 4, n:n + 1])
        op.then_inc(S["smp_act"], 1)
        restage(64, SEQ, (3, 0))
        out_phase(C_O2, 1)
        root_of_norm(5)
        yp = t["y_prompt"][0].rearrange("(b p) (k c) -> k p b c", p=P, c=P)
        with act.Fori(0, 4) as i:
            for s in range(4):
                k, b0 = i * 4 + s, SETS[s % 2]
                yn = raw[:, 2 * (s % 2):2 * (s % 2) + 2].rearrange("p a b c -> p (a b c)")
                act.wait_ge(S["fin_turned"], k + 1 + CREDIT)
                act.wait_ge(S[f"fin_out{s % 2}"], i * 32 + 16 * (s // 2) + 16)
                for n in range(2):
                    act.activation(yn[:, n * 512:(n + 1) * 512], ps[:, b0 + n, :], ACT.Copy)
                act.activation(rows[0:NB, bass.ds(k * P, P)], ps[0:NB, b0 + 2, 0:P], ACT.Copy).then_inc(S["fin_sb"], 1)
                act.wait_ge(S["fin_sb"], k + 3)
                act.dma_start(yp[bass.ds(k, 1)].rearrange("o p b c -> p (o b) c"), yn.rearrange("p (b c) -> p b c", c=P))\
                    .then_inc(S[f"fin_out{s % 2}"], 16)
        act.dma_start(t["y_sample"].rearrange("b o n -> (b o) n"), rows[0:NB, :]).then_inc(S["ys_out"], 16)

    @block.vector
    def _(dve):
        own = Chain(dve, S["dve_step"])
        for n, v in (("psum_read", 2), ("fin_turned", CREDIT), ("o_sq", 2), ("s_read", 1),
                     ("o_read", 1), ("i_read", 1)):
            dve.sem_inc(S[n], v)
        dve.wait_ge(S["tab_in"], 64)
        own.link(dve.memset(tab[NBUCKET:NBUCKET + 1, :, :], 1.0))
        own.link(dve.tensor_scalar(sxs[0:1, 0, 0:16], skp[0:1, 0:16], 1.0, None, ALU.mult))
        own.link(dve.tensor_scalar(sxs[0:1, 1, 0:16], skp[0:1, 16:32], 1.0, None, ALU.mult))
        by = tab[0:NBUCKET, :, :].rearrange("p v (c e j w) -> p v c e j w", c=4, e=2, j=2)
        for e in range(2):
            for w in range(2):
                for c in range(4):
                    own.step(dve.tensor_copy(by[:, 1, c, e, :, w], by[:, 0, c, e, :, w ^ e]))
        for half in range(2):
            src = sxs[0:1, half, :].rearrange("p (c e j w) -> p c e j w", c=2, e=2, j=2)
            dst = skp[0:1, half * 16:half * 16 + 16].rearrange("p (c e j w) -> p c e j w", c=2, e=2, j=2)
            for e in range(2):
                for w in range(2):
                    for c in range(2):
                        own.step(dve.tensor_copy(dst[:, c, e, :, w], src[:, c, e, :, w ^ e]))
        own.wait()
        dve.tensor_scalar(nsk[:], nsk[:], -1.0, None, ALU.mult).then_inc(S["tab_ready"], 1)
        dve.wait_ge(S["par_turned"], 2)
        lam = prm[:, :, R_LAM]
        own.link(dve.tensor_scalar(spt[:, 2, :], lam, -1.0, None, ALU.mult))
        dve.tensor_tensor(spt[:, 0, :], lam, spt[:, 2, :], ALU.max).then_inc(S["root_in"], 1)
        own.step(dve.tensor_scalar(hbr[:], prm[:, :, R_BR], 0.5, None, ALU.mult))
        own.step(dve.tensor_scalar(hbi[:], prm[:, :, R_BI], 0.5, None, ALU.mult))
        own.link(dve.tensor_scalar(spt[:, 2, :], spt[:, 2, :], 0.0, 2.0, ALU.max, ALU.mult))
        dve.wait_ge(S["root_done"], 1)
        e_, s_, s2_ = spt[:, 1, :], spt[:, 0, :], spt[:, 3, :]
        own.link(dve.tensor_scalar(s_, e_, 2.0, None, ALU.add))
        own.link(dve.reciprocal(s_, s_))
        own.link(dve.tensor_tensor(s_, s_, e_, ALU.mult))
        own.link(dve.tensor_tensor(s2_, s_, s_, ALU.mult))
        own.link(dve.tensor_scalar(sp2[:], s2_, 1.0 / 17.0, 1.0 / 15.0, ALU.mult, ALU.add))
        for n in (13, 11, 9, 7, 5, 3, 1):
            own.link(dve.tensor_tensor(sp2[:], sp2[:], s2_, ALU.mult))
            own.link(dve.tensor_scalar(sp2[:], sp2[:], 1.0 / n, None, ALU.add))
        own.link(dve.scalar_tensor_tensor(out=sp2[:], in0=sp2[:], scalar=4.0, in1=s_, op0=ALU.mult, op1=ALU.mult))
        own.link(dve.tensor_tensor(sp2[:], sp2[:], spt[:, 2, :], ALU.add))
        own.step(dve.tensor_scalar(nsp4[:], sp2[:], -2.0, None, ALU.mult))
        for n in range(9):
            w = P if n < 8 else NB
            cols = slice(n * P, n * P + w)
            dve.wait_ge(S["x_staged"], (n + 1) * NQ)
            dve.tensor_copy(xsp[:, :, 0, cols], st[:, n % 2, :, 0:w]).then_inc(S["x_hi"], 1)
            dve.wait_ge(S["x_hi"], n + 1)
            dve.tensor_tensor(xsp[:, :, 1, cols], st[:, n % 2, :, 0:w], xsp[:, :, 0, cols].bitcast(F32), ALU.subtract)\
                .then_inc(S["x_lo"], 1)
            xt = xr[0:w, n % 3, :]
            dve.tensor_tensor_reduce(xt, xt, xt, 1.0, 0.0, ALU.mult, ALU.add, sxs[0:w, 0, n:n + 1]).then_inc(S["x_squared"], 1)
        dve.wait_ge(S["x_squared"], 9)
        dve.wait_ge(S["bias_mm"], 1)
        own.step(dve.tensor_copy(bsm[:], ps[:, 5, 0:NH]))
        dve.tensor_copy(rstd[0:NH, 0:BW], ps[0:NH, 4, 0:BW]).then_inc(S["bias_sb"], 1)

        def mean_eps(out, in_):
            return dve.tensor_scalar(out, in_, 1.0 / D, EPS, ALU.mult, ALU.add)

        own.step(mean_eps(sxs[:, 0, 0:8], sxs[:, 0, 0:8]))
        mean_eps(sxs[0:NB, 0, 8:9], sxs[0:NB, 0, 8:9]).then_inc(S["root_in"], 1)
        dve.wait_ge(S["root_done"], 3)
        own.step(dve.reciprocal(sxs[:, 1, 0:8], sxs[:, 1, 0:8]))
        own.link(dve.reciprocal(sxs[0:NB, 1, 8:9], sxs[0:NB, 1, 8:9]))
        for n in range(9):
            w = P if n < 8 else NB
            if n >= 2:
                dve.wait_ge(S["diag_mm"], n - 1)
            dve.tensor_scalar(dg[0:w, n % 2, 0:w], ident[0:w, 0:w], sxs[0:w, 1, n:n + 1], None, ALU.mult).then_inc(S["diag"], 1)
        dve.wait_ge(S["diag_mm"], 9)
        dve.wait_ge(S["bias_out"], 16)
        own.step(dve.tensor_copy(rstd[:, 0:512], ps[:, 0, :]))
        own.step(dve.tensor_copy(rstd[:, 512:SEQ], ps[:, 1, :]))
        dve.tensor_copy(rstd[:, SEQ:NT], ps[:, 6, 0:NB]).then_inc(S["rstd_ready"], 1)
        dve.wait_ge(S["rstd_ready"], 1)
        dve.wait_ge(S["xt_out0"], 16 * 5)
        dve.wait_ge(S["xt_out1"], 16 * 4)
        own.link(dve.memset(u[:, 0:4], 0.0))

        def evac(c, dst, which, scale=None, last=None):
            chunk_done(dve, c)
            for g in range(GROUPS):
                src = ps[:, SETS[which] + g, 0:TG]
                if scale is None:
                    op = dve.tensor_tensor(dst[:, grp(g)], src, rstd[:, grp(g)], ALU.mult)
                else:
                    op = dve.scalar_tensor_tensor(out=dst[:, grp(g)], in0=src, scalar=scale, in1=rstd[:, grp(g)],
                                                  op0=ALU.mult, op1=ALU.mult)
                if last is None:
                    op.then_inc(S["gs_ready"], 1)
            if last is not None:
                op.then_inc(last, 1)

        def silu(n, dst, which):
            for g in range(GROUPS):
                dve.wait_ge(S["gt_ready"], n * GROUPS + g + 1)
                op = dve.scalar_tensor_tensor(out=dst[:, grp(g)], in0=ps[:, SETS[which] + g, 0:TG], scalar=1.0,
                                              in1=dst[:, grp(g)], op0=ALU.add, op1=ALU.mult)
            op.then_inc(S["psum_read"], 1)

        A_STEPS = 22
        base = own.end()
        with dve.Fori(0, A_ITERS) as i:
            own = Chain(dve, S["dve_step"], base, A_STEPS, i)
            for m in range(2):
                k, c = i * 2 + m, i * 4 + m

                def col(r, w=1, k=k):
                    return prm[:, bass.ds(k, 1), r:r + w].rearrange("p o n -> p (o n)")

                if m == 0:
                    dve.wait_ge(S["y_out1"], i * 16 + 16)
                evac(c, u[:, 3:3 + NT], m, last=S["psum_read"])
                dve.wait_ge(S["psum_read"], c + 3)
                oc = ocols[:, bass.ds(k, 1), :].rearrange("p o n -> p (o n)")
                own.step(dve.tensor_copy(oc[:, 0:11], u[:, SEQ:SEQ + 11]))
                v = cv[:, m, :]
                own.link(dve.tensor_scalar(v, u[:, 3:3 + NT], col(R_CW + 3), col(R_CB), ALU.mult, ALU.add))
                for tap in (2, 1, 0):
                    own.link(dve.scalar_tensor_tensor(out=v[:, 0:SEQ], in0=u[:, tap:tap + SEQ], scalar=col(R_CW + tap),
                                                      in1=v[:, 0:SEQ], op0=ALU.mult, op1=ALU.add))
                    op = dve.scalar_tensor_tensor(out=v[:, SEQ:NT], in0=col(R_SC, 3 * NB).rearrange("p (b w) -> p b w", w=3)[:, :, tap],
                                                  scalar=col(R_CW + tap), in1=v[:, SEQ:NT], op0=ALU.mult, op1=ALU.add)
                    if tap:
                        own.link(op)
                    else:
                        op.then_inc(S["cv_ready"], 1)
                dve.wait_ge(S["cv_ready"], i * 2 + m + 1)

            def conv_lo(g):
                dve.wait_ge(S["conv_hi"], i * 3 + g + 1)
                dve.tensor_tensor(csp[:, g % 2, 1, :, :], cv[:, :, grp(g)], csp[:, g % 2, 0, :, :].bitcast(F32), ALU.subtract)\
                    .then_inc(S["conv_lo"], 1)

            conv_lo(0)
            conv_lo(1)
            dve.wait_ge(S["y_out0"], i * 16 + 16)
            evac(i * 4 + 2, gs, 0)
            silu(i * 2, gs, 0)
            for g in range(GROUPS):
                for m in range(2):
                    dve.wait_ge(S["i_turned"], i * 6 + g * 2 + m + 1)
                    if g == 1 and m == 0:
                        conv_lo(2)
                    dve.scalar_tensor_tensor(out=cv[:, m, grp(g)], in0=ps[:, X1, 0:TG], scalar=1.0, in1=cv[:, m, grp(g)],
                                             op0=ALU.add, op1=ALU.mult).then_inc(S["i_read"], 1)
            dve.wait_ge(S["act_step"], i * 12 + 12)
            dve.tensor_scalar(h[:, :, :], h[:, :, :], TINY, None, ALU.max).then_inc(S["w_ready"], 1)
            evac(i * 4 + 3, g1, 1)
            dve.wait_ge(S["root"], i + 1)
            own.link(dve.scalar_tensor_tensor(out=h[:, :, :], in0=rc[:, :, :], scalar=1.0, in1=h[:, :, :], op0=ALU.add, op1=ALU.mult))
            own.step(dve.scalar_tensor_tensor(out=cv[:, :, :], in0=cv[:, :, :], scalar=0.5, in1=h[:, :, :], op0=ALU.mult, op1=ALU.mult))
            silu(i * 2 + 1, g1, 1)
            own.wait()
            for m in range(2):
                k = i * 2 + m
                h0 = prm[:, bass.ds(k, 1), R_SH:R_SH + NB].rearrange("p o n -> p (o n)")
                own.link(dve.tensor_tensor(rc[:, m, SEQ:NT], rc[:, m, SEQ:NT], h0, ALU.mult))
                own.step(dve.tensor_tensor(h[:, m, SEQ:NT], cv[:, m, SEQ:NT], rc[:, m, SEQ:NT], ALU.add))
                own.link(dve.tensor_tensor_scan(h[:, m, 0:SEQ], rc[:, m, 0:SEQ], cv[:, m, 0:SEQ], 0.0, ALU.mult, ALU.add))
                oc = ocols[:, bass.ds(k, 1), :].rearrange("p o n -> p (o n)")
                dve.tensor_copy(oc[:, 11:20], h[:, m, SEQ - 1:NT]).then_inc(S["oc_ready"], 1)
                gate = (gs[:], g1)[m]
                dve.wait_ge(S["psum_read"], i * 4 + 6)
                dve.scalar_tensor_tensor(out=gate, in0=h[:, m, :], scalar=0.5, in1=gate, op0=ALU.mult, op1=ALU.mult)\
                    .then_inc(S["y_ready"], 1)
        base = own.end(A_ITERS)

        def restage(before, cols, quarters):
            for n, kq in enumerate(quarters):
                for k in range(kq * QK, kq * QK + QK):
                    dve.wait_ge(S["stage_hi"], before + n * QK + k % QK + 1)
                    dve.tensor_tensor(xsp[:, k, 1, 0:cols], xsp[:, k, 1, 0:cols].bitcast(F32), xsp[:, k, 0, 0:cols].bitcast(F32), ALU.subtract)\
                        .then_inc(S["stage_used"], 1)

        def out_phase(c_base, before):
            with dve.Fori(0, O_ITERS) as i:
                for m in range(2):
                    c = i * 2 + m
                    dve.wait_ge(S["psum_read"], c + c_base + 3)
                    dve.wait_ge(S["o_sq"], c + KT * before + 2)
                    dve.tensor_tensor(acc[:], acc[:], stg[:, m, 1, :], ALU.add).then_inc(S["o_sq"], 1)
            dve.wait_ge(S["o_sq"], KT * (before + 1) + 2)

        def clear_acc():
            own.link(dve.memset(acc[:], 0.0))

        def norm(n, root, summed):
            dve.wait_ge(*summed)
            for g in range(GROUPS):
                op = mean_eps(rstd[:, grp(g)], ps[:, 5 + g, 0:TG])
            op.then_inc(S["root_in"], 1)
            dve.wait_ge(S["root_done"], root)
            dve.reciprocal(rstd[:], rstd[:]).then_inc(S["rstd_ready"], 1)
            dve.wait_ge(S["rstd_ready"], n + 1)

        own = Chain(dve, S["dve_step"], base)
        dve.wait_ge(S["y_out0"], 16 * A_ITERS + 16)
        dve.wait_ge(S["y_out1"], 16 * A_ITERS + 16)
        clear_acc()
        restage(0, NT, range(NQ))
        out_phase(C_O1, 0)
        dve.sem_inc(S["acc_ready"], 1)
        norm(1, 4, (S["norm_mm"], 1))
        dve.wait_ge(S["o_out0"], 16 * O_ITERS + 16)
        dve.wait_ge(S["o_out1"], 16 * O_ITERS + 16)
        with dve.Fori(0, 4) as i:
            for s in range(4):
                k = i * 4 + s
                tile = land[:, bass.ds(k, 1), :, :]
                hold(dve, S["x1_scaled"], k + 1)
                hold(dve, S[f"x1_out{s}"], i * 16 + 16)
                dve.scalar_tensor_tensor(out=stg[:, s, 0, :], in0=tile[:, :, 0, :].rearrange("p o n -> p (o n)"),
                                         scalar=prm[:, bass.ds(k, 1), R_GPOST:R_GPOST + 1].rearrange("p o n -> p (o n)"),
                                         in1=tile[:, :, 1, :].rearrange("p o n -> p (o n)"), op0=ALU.mult, op1=ALU.add)\
                    .then_inc(S["x1_ready"], 1)
            for s in range(4):
                k = i * 4 + s
                x = xsp[:, bass.ds(k, 1), :, :]
                dve.wait_ge(S["stage_hi"], k + KT + 1)
                dve.tensor_tensor(x[:, :, 1, :].rearrange("p o n -> p (o n)"), stg[:, s, 0, :],
                                  x[:, :, 0, :].rearrange("p o n -> p (o n)").bitcast(F32), ALU.subtract)\
                    .then_inc(S["stage_used"], 1)
            dve.wait_ge(S["x1_sq"], i * 4 + 4)
            dve.wait_ge(S["stage_used"], i * 4 + KT + 4)
        norm(2, 5, (S["x1_sum"], KT + 4))
        for s in range(4):
            dve.wait_ge(S[f"x1_out{s}"], 80)
        dve.sem_inc(S["b_used"], 2)

        def softmax_in(i, j, b):
            n = i * 32 + j * NBLK + b
            lo = BLK if b == 0 else 0
            bank = SETS[(ATT_AT[j] + 1) % 2]
            if b == 0:
                hold(dve, S[f"b_in{j % 2}"], i * 32 + 16 * (j // 2) + 16)
            hold(dve, S["s_done"], n + 1)
            for hf in range(2):
                op = dve.tensor_tensor_reduce(pp[:, b % 2, hf, lo:2 * BLK], ps[:, bank + hf, lo:2 * BLK],
                                              bb[:, j % 2, hf, lo:2 * BLK], 1.0, NEG, ALU.add, ALU.max, mx[:, 0, hf:hf + 1])
            op.then_inc(S["s_read"], 1)
            dve.wait_ge(S["s_read"], n + 2)
            sk = nsk[:, bass.ds(i * 8 + j * 2, 2)]
            own.link(dve.scalar_tensor_tensor(out=mx[:, 1, :], in0=mx[:, 0, :], scalar=-1.0, in1=sk, op0=ALU.mult, op1=ALU.min))
            dve.tensor_tensor(mx[:, 2, :], mx[:, 1, :], sk, ALU.subtract).then_inc(S["negm"], 1)
            if b == NBLK - 1:
                dve.sem_inc(S["b_used"], 1)

        def softmax_out(i, j, b):
            n = i * 32 + j * NBLK + b
            lo = BLK if b == 0 else 0
            dve.wait_ge(S["p_exp"], n + 1)
            own.link(dve.tensor_tensor(mx[:, 5, :], mx[:, 3, :], mx[:, 4, :], ALU.add))
            own.link(dve.reciprocal(mx[:, 5, :], mx[:, 5, :]))
            for hf in range(2):
                s = pp[:, b % 2, hf, lo:2 * BLK]
                op = dve.tensor_scalar(s, s, mx[:, 5, hf:hf + 1], None, ALU.mult)
            op.then_inc(S["p_ready"], 1)

        def output(i, j, b):
            n = i * 32 + j * NBLK + b
            dve.wait_ge(S["o_done"], n + 1)
            dve.tensor_copy(q[:, j % 2, b * BLK:(b + 1) * BLK], ps[:, X1, 0:BLK]).then_inc(S["o_read"], 1)

        def chunk_out(i, c):
            what, j = B_CHUNKS[c]
            cc = i * NBC + c + C_B
            if what == "k":
                evac(cc, k1, c % 2, last=S["psum_read"])
            elif what == "v":
                evac(cc, gb, c % 2, last=S["psum_read"])
            elif what == "q":
                dve.wait_ge(S[f"yb_out{j % 2}"], i * 32 + 16 * (j // 2) + 16)
                evac(cc, q[:, j % 2, :], c % 2, scale=0.125, last=S["psum_read"])
                dve.wait_ge(S["psum_read"], cc + 3)
                at = bass.ds(i * 4 + j, 1)
                own.step(dve.tensor_copy(qs[:, at, 0, :].rearrange("p o n -> p (o n)"), q[:, j % 2, SEQ:NT]))
                own.step(dve.tensor_copy(qs[0:HD, at, 1, :].rearrange("p o n -> p (o n)"), q[HD:P, j % 2, SEQ:NT]))
                own.step(dve.tensor_copy(qs[HD:P, at, 1, :].rearrange("p o n -> p (o n)"), q[0:HD, j % 2, SEQ:NT]))
            else:
                evac(cc, gb, c % 2)
                silu(i * 4 + j + 2 * A_ITERS, gb, c % 2)
                dve.wait_ge(S["psum_read"], cc + 3)
                own.step(dve.tensor_copy(gsm[:, bass.ds(i * 4 + j, 1), :].rearrange("p o n -> p (o n)"), gb[:, SEQ:NT]))
                dve.wait_ge(S["o_read"], i * 32 + j * NBLK + NBLK + 1)
                dve.scalar_tensor_tensor(out=q[:, j % 2, 0:SEQ], in0=q[:, j % 2, 0:SEQ], scalar=0.5, in1=gb[:, 0:SEQ],
                                         op0=ALU.mult, op1=ALU.mult).then_inc(S["y_ready"], 1)
                dve.wait_ge(S["y_ready"], i * 4 + j + 1 + 2 * A_ITERS)

        base = own.end()
        with dve.Fori(0, B_ITERS) as i:
            own = Chain(dve, S["dve_step"], base, 4 * 3 + 4 + 32 * 3, i)
            todo = [(c * 8 + 8, 0, lambda c=c: chunk_out(i, c)) for c in range(NBC)]
            for j in range(4):
                at = ATT_AT[j] * 8
                for b in range(NBLK):
                    todo.append((at + b + 4, 1, lambda j=j, b=b: output(i, j, b)))
                    todo.append((at + b + 1, 2, lambda j=j, b=b: softmax_out(i, j, b)))
                    todo.append((at + b, 3, lambda j=j, b=b: softmax_in(i, j, b)))
            for _, _, f in sorted(todo, key=lambda x: x[:2]):
                f()
        own = Chain(dve, S["dve_step"], own.end(B_ITERS))

        restage(32, SEQ, (1, 2))
        dve.wait_ge(S["yb_out0"], 32 * B_ITERS + 16)
        dve.wait_ge(S["yb_out1"], 32 * B_ITERS + 16)
        dve.wait_ge(S["smp_pe"], 12)
        sav = sa[:, :, :].rearrange("p n c -> p (n c)").rearrange("p (c e b t) -> p c e b t", c=4, e=2, b=NB)
        bsv = bsm[:].rearrange("p (c e t) -> p c e t", c=4, e=2)
        for e in range(2):
            psv = ps[:, 3 + e, 0:256].rearrange("p (c e b t) -> p c e b t", c=4, e=2, b=NB)
            for b in range(NB):
                op = dve.tensor_tensor(sav[:, :, e, b, :], psv[:, :, e, b, :], bsv[:, :, e, :], ALU.add)
        op.then_inc(S["smp_dve"], 1)
        skv = skr[:].rearrange("p (h b t) -> p h b t", h=NKV, b=NB)
        for b in range(NB):
            op = dve.tensor_copy(skv[:, :, b, :], skp[:].rearrange("p (h t) -> p h t", h=NKV))
        op.then_inc(S["smp_dve"], 1)
        dve.wait_ge(S["smp_pe"], 13)
        own.step(dve.tensor_reduce(sx[:, 0, :], ps[:, 5, 0:256].rearrange("p (n c) -> p n c", n=2), AXX, ALU.max))
        own.link(dve.tensor_copy(sx[:, 5, :], ps[:, 6, 0:2]))
        own.link(dve.tensor_tensor(sx[:, 0, :], sx[:, 0, :], sx[:, 5, :], ALU.max))
        own.link(dve.tensor_scalar(sx[:, 1, :], sx[:, 0, :], -1.0, None, ALU.mult))
        dve.tensor_tensor(sx[:, 2, :], sx[:, 5, :], sx[:, 1, :], ALU.add).then_inc(S["smp_dve"], 1)
        dve.wait_ge(S["smp_act"], 9)
        own.link(dve.tensor_tensor(sx[:, 5, :], sx[:, 3, :], sx[:, 4, :], ALU.add))
        own.link(dve.reciprocal(sx[:, 5, :], sx[:, 5, :]))
        for n in range(2):
            op = dve.tensor_scalar(sbm[:, n, :], sbm[:, n, :], sx[:, 5, n:n + 1], None, ALU.mult)
        op.then_inc(S["smp_dve"], 1)
        dve.wait_ge(S["smp_pe"], 14)
        dve.tensor_copy(sa[:, :, :].rearrange("p n c -> p (n c)"), ps[:, 7, 0:256]).then_inc(S["smp_dve"], 1)
        dve.wait_ge(S["smp_pe"], 15)
        ov = ps[0:HD, 0, 0:256].rearrange("p (c e b j w) -> p c e b j w", c=4, e=2, b=NB, j=2)
        qv = qs[:].rearrange("p (c e j) v b -> p c e j v b", c=4, e=2)
        for e in range(2):
            for w in range(2):
                hf = e ^ w
                for j in range(2):
                    own.step(dve.tensor_copy(qv[hf * HD:hf * HD + HD, :, e, j, 0, :], ov[:, :, e, :, j, w]))
        own.wait()
        own.link(dve.scalar_tensor_tensor(out=qs[:, :, 0, :], in0=qs[:, :, 0, :], scalar=0.5, in1=gsm[:], op0=ALU.mult, op1=ALU.mult))
        chunk_done(dve, C_O2 - 1)
        dve.tensor_copy(xsp[:, :, 0, SEQ:NT], qs[:, :, 0, :]).then_inc(S["smp_split"], 1)
        dve.wait_ge(S["smp_split"], 1)
        dve.tensor_tensor(xsp[:, :, 1, SEQ:NT], qs[:, :, 0, :], xsp[:, :, 0, SEQ:NT].bitcast(F32), ALU.subtract)\
            .then_inc(S["smp_split"], 1)
        clear_acc()
        restage(40, SEQ, (3, 0))
        out_phase(C_O2, 1)
        dve.sem_inc(S["acc_ready"], 1)
        norm(3, 6, (S["norm_mm"], 2))
        dve.wait_ge(S["o_out0"], 32 * O_ITERS + 16)
        dve.wait_ge(S["o_out1"], 32 * O_ITERS + 16)
        with dve.Fori(0, 4) as i:
            for s in range(4):
                k = i * 4 + s
                tile = land[:, bass.ds(k, 1), :, :]
                hold(dve, S["x1_scaled"], k + KT + 1)
                hold(dve, S["fin_turned"], k + 1)
                dve.scalar_tensor_tensor(out=stg[:, s, 0, :], in0=tile[:, :, 0, :].rearrange("p o n -> p (o n)"),
                                         scalar=prm[:, bass.ds(k, 1), R_BPOST:R_BPOST + 1].rearrange("p o n -> p (o n)"),
                                         in1=tile[:, :, 1, :].rearrange("p o n -> p (o n)"), op0=ALU.mult, op1=ALU.add)\
                    .then_inc(S["fin_ready"], 1)


_OUTS = [("y_prompt", (1, SEQ, D)), ("y_sample", (NB, 1, D)), ("prompt_conv", (1, 1, 3, D)), ("prompt_h", (1, 1, D)),
         ("prompt_k", (1, BLK, NKV, HD)), ("prompt_v", (1, BLK, NKV, HD)), ("sample_conv", (1, NB, 3, D)),
         ("sample_h", (1, NB, D)), ("sample_k", (NB, 1, NKV, HD)), ("sample_v", (NB, 1, NKV, HD))]


def kernel(**inputs):
    import concourse.bacc as bacc
    from concourse.bass_utils import run_bass_kernel_spmd

    nc = bacc.Bacc("TRN2", target_bir_lowering=False, num_devices=1)
    arrays, t = {}, {}
    for name, a in {**inputs, "ident": np.eye(P, dtype=np.float32), "onehot": bucket_one_hot()}.items():
        a = np.ascontiguousarray(a)
        arrays[f"in_{name}"] = a
        t[name] = nc.dram_tensor(f"in_{name}", a.shape, mybir.dt.from_np(a.dtype), kind="ExternalInput").ap()
    for name, shape in _OUTS:
        t[name] = nc.dram_tensor(f"out_{name}", shape, F32, kind="ExternalOutput").ap()
    build(nc, t)
    r = run_bass_kernel_spmd(nc, [arrays], core_ids=[0])
    return tuple(r.results[0][f"out_{name}"] for name, _ in _OUTS)
```

```python
from contextlib import ExitStack

import concourse.bass as bass
import concourse.mybir as mybir
import numpy as np

F32 = mybir.dt.float32
F32R = mybir.dt.float32r
ALU = mybir.AluOpType
ACT = mybir.ActivationFunctionType
AXX = mybir.AxisListType.X

P = 128
D = 2048
SEQ = 1024
NB = 8
NT = SEQ + NB
GROUPS = 3
TG = NT // GROUPS
KT = D // P
QK = 4
NQ = KT // QK
BLK = 128
NBLK = SEQ // BLK
HD = 64
NH = D // HD
NKV = 8
KVW = NKV * HD
CONV = 4
NBUCKET = 32
MAXDIST = 128
EPS = 1e-6
NEG = -1e30
BW = 3 * BLK
LRU_C = 8.0
TINY = 2.0 ** -113

R_GPRE, R_GPOST, R_CW, R_CB, R_BR, R_BI, R_LAM, R_GKV, R_BPRE, R_BPOST, R_SC, R_SH = 0, 1, 2, 6, 7, 8, 9, 10, 11, 12, 13, 37
NROW = R_SH + NB
NOC = 20

A_ITERS, B_ITERS = 8, 4
A_SPLITS = 4 * NQ + 2
O_ITERS = KT // 2


def bucket_one_hot():
    n = np.arange(MAXDIST)
    exact = NBUCKET // 2
    nf = np.maximum(n, 1).astype(np.float32)
    large = exact + (np.log(nf / np.float32(exact)) / np.float32(np.log(MAXDIST / exact)) * np.float32(NBUCKET - exact)).astype(np.int32)
    b = np.where(n < exact, n, np.minimum(large, NBUCKET - 1))
    row = np.zeros((NBUCKET + 1, BW + P), np.float32)
    row[NBUCKET, :BW] = NEG
    for j in range(BLK, 2 * BLK):
        row[b[2 * BLK - 1 - j], j] = 1.0
        row[NBUCKET, j] = 0.0
    for r in range(P):
        row[b[0 if r == 0 else P - r], BW + r] = 1.0
    return row


def build(nc, t):
    ctx = ExitStack()
    with ctx:
        program(nc, t, ctx)


def program(nc, t, ctx):
    def sb(name, shape, dt=F32, where=ctx):
        return where.enter_context(nc.sbuf_tensor(name, shape, dt))

    def dram(name, shape):
        return nc.dram_tensor(name, shape, F32, kind="Internal").ap()

    def sem(name):
        return ctx.enter_context(nc.semaphore(name))

    x_t = dram("x_t", (KT, P, NT))
    y_t = dram("y_t", (KT, P, NT))
    o_t = dram("o_t", (KT, P, NT))
    x1_t = dram("x1_t", (KT, P, NT))
    bias_row = dram("bias_row", (NH, BW))
    bias_blk = dram("bias_blk", (NH, BLK, 2 * BLK))

    z = ExitStack()
    kc = sb("kc", [P, 4, NB, P], where=z)
    vc = sb("vc", [P, 4, NB, P], where=z)
    z.close()
    xsp = sb("xsp", [P, KT, 2, NT], F32R)
    land = xsp[:, :, :, :].bitcast(F32)
    wsp = sb("wsp", [P, NQ, 2, QK, P], F32R)
    raw = sb("raw", [P, NQ, QK, P])
    rstd = sb("rstd", [P, NT])
    prm = sb("prm", [P, KT, NROW])
    hbr = sb("hbr", [P, KT])
    hbi = sb("hbi", [P, KT])
    sp2 = sb("sp2", [P, KT])
    nsp4 = sb("nsp4", [P, KT])
    ident = sb("ident", [P, P])
    ones = sb("ones", [P, P])
    warm = sb("warm", [P, 3])
    z = ExitStack()
    ocols = sb("ocols", [P, KT, NOC], where=z)
    z.close()
    qs = sb("qs", [P, KT, 2, NB])
    gsm = sb("gsm", [P, KT, NB])
    bsm = sb("bsm", [P, NH])
    skp = sb("skp", [1, NH])
    nsk = sb("nsk", [P, NH])

    z = ExitStack()
    xr = sb("xr", [P, 3, D], where=z)
    st = sb("st", [P, 2, KT, P], where=z)
    dg = sb("dg", [P, 2, P], where=z)
    ohx = sb("ohx", [NBUCKET + 1, BW + P], where=z)
    tab = sb("tab", [NBUCKET + 1, 2, NH], where=z)
    sxs = sb("sxs", [P, 2, 16], where=z)
    spt = sb("spt", [P, 4, KT], where=z)
    z.close()
    z = ExitStack()
    u = sb("u", [P, 4 + NT], where=z)
    cv = sb("cv", [P, 2, NT], where=z)
    gs = sb("gs", [P, NT], where=z)
    h = sb("h", [P, 2, NT], where=z)
    rc = sb("rc", [P, 2, NT], where=z)
    g1 = u[:, 3:3 + NT]
    csp = sb("csp", [P, 2, 2, 2, TG], F32R, where=z)
    z.close()
    z = ExitStack()
    acc = sb("acc", [P, NT], where=z)
    stg = sb("stg", [P, 4, 2, NT], where=z)
    rows = sb("rows", [NOC, D], where=z)
    z.close()
    z = ExitStack()
    k1 = sb("k1", [P, NT], where=z)
    k2 = sb("k2", [P, NT], where=z)
    vn = sb("vn", [P, NBLK, 2, 2, HD], F32R, where=z)
    q = sb("q", [P, 2, NT], where=z)
    gb = sb("gb", [P, NT], where=z)
    bb = sb("bb", [P, 2, 2, 2 * BLK], where=z)
    pp = sb("pp", [P, 2, 2, 2 * BLK], where=z)
    pt = sb("pt", [P, 2, 2, 2 * BLK], F32R, where=z)
    ptl = sb("ptl", [P, 2, 2 * BLK], F32R, where=z)
    kvo = sb("kvo", [P, 2, P], where=z)
    ol = sb("ol", [P, 2 * BLK], where=z)
    mx = sb("mx", [P, 6, 2], where=z)
    z.close()
    z = ExitStack()
    kst = sb("kst", [P, NB, P], where=z)
    sa = sb("sa", [P, 2, P], where=z)
    sbm = sb("sbm", [P, 2, P], where=z)
    skr = sb("skr", [1, 256], where=z)
    qbd = sb("qbd", [P, 4, NB, 2, 2, 2], where=z)
    sx = sb("sx", [P, 6, 2], where=z)
    z.close()

    ps = ctx.enter_context(nc.psum_tensor("ps", [P, 8, 512], F32))
    SETS = (0, 3)
    X0, X1 = 6, 7

    S = {n: sem(n) for n in (
        "held const_in par_in tab_in x_in0 x_in1 x_in2 x_turned par_turned x_staged x_squared x_hi x_lo xt_out0 xt_out1 "
        "dve_step act_step bias_mm bias_sb bias_out blk_out root_in root_done diag diag_mm rstd_ready tab_ready raw0 "
        "raw1 raw2 raw3 w_gained w_hi w_split w_used psum_read ri_done r_read i_read i_turned cv_ready conv_hi conv_lo "
        "gs_ready gt_ready w_ready root y_ready y_out0 y_out1 o_sq o_out0 o_out1 acc_ready norm_mm land_in0 land_in1 "
        "land_in2 land_in3 stage_hi stage_used x1_ready x1_scaled x1_back x1_sum x1_sq x1_out0 x1_out1 x1_out2 x1_out3 "
        "oc_ready oc_turned oc_sb state_out s_done s_read negm p_exp p_ready p_turned pt_ready o_done o_read b_in0 "
        "b_in1 v_turned v_hi v_lo kv_ready pt_lo o_low kv_out yb_out0 yb_out1 fin_ready fin_turned fin_sb fin_out0 "
        "fin_out1 ys_out smp_k_in smp_v_in smp_q smp_pe smp_act smp_dve smp_split ones_ready b_used").split()}
    LAND = [S[f"land_in{i}"] for i in range(NQ)]
    RAW = [S[f"raw{i}"] for i in range(NQ)]

    O2_ORDER = (1, 2, 3, 0)
    FIN_LANDED = [96, 96, 96, 80]
    X1_SLOTS = (2, 3, 0, 1)
    G1_SLOTS = (2, 3, 2, 3)
    CREDIT = NQ
    Q_O1 = 16 * A_ITERS
    Q_B = Q_O1 + 64
    Q_O2 = Q_B + 160
    Q_END = Q_O2 + 64
    C_O1, C_B, C_O2 = Q_O1 // NQ, Q_B // NQ, Q_O2 // NQ
    W_O1 = A_SPLITS * A_ITERS
    W_B = W_O1 + 64
    W_O2 = W_B + 160

    def grp(g):
        return slice(g * TG, (g + 1) * TG)

    def hold(eng, s, v):
        eng.wait_ge(s, v)
        eng.sem_inc(S["held"], 1)

    def chunk_done(eng, c):
        eng.wait_ge(S["w_used"], c * NQ + NQ + CREDIT)

    class Chain:

        def __init__(self, eng, s, base=0, per=0, i=0):
            self.eng, self.s, self.base, self.per, self.i, self.n = eng, s, base, per, i, 0

        def step(self, op):
            op.then_inc(self.s, 1)
            self.n += 1

        def wait(self):
            self.eng.wait_ge(self.s, self.i * self.per + (self.base + self.n))

        def link(self, op):
            self.step(op)
            self.wait()

        def end(self, iters=1):
            assert not self.per or self.n == self.per, self.n
            return self.base + (self.per * iters if self.per else self.n)

    w_in = t["a_w_in"][0].rearrange("(k p) n -> p k n", p=P)
    w_r = t["a_w_r"][0].rearrange("n (k p) c -> n p k c", p=P)
    w_i = t["a_w_i"][0].rearrange("n (k p) c -> n p k c", p=P)
    w_oa = t["a_w_out"][0].rearrange("(k p) n -> p k n", p=P)
    w_kv = t["w_kv"].rearrange("(k p) n -> p k n", p=P)
    w_qg = t["b_w_qg"][0].rearrange("(k p) n -> p k n", p=P)
    w_ob = t["b_w_out"][0].rearrange("(k p) n -> p k n", p=P)

    B_CHUNKS = [("k", 0), ("v", 0), ("q", 0), ("q", 1), ("g", 0), ("q", 2), ("g", 1), ("q", 3), ("g", 2), ("g", 3)]
    ATT_AT = [3, 4, 6, 8]
    Q_CHUNK, G_CHUNK = [2, 3, 5, 7], [4, 6, 8, 9]
    NBC = len(B_CHUNKS)

    block = ctx.enter_context(nc.Block())

    @block.sync
    def _(sp):
        sp.dma_start(ident[:], t["ident"]).then_inc(S["const_in"], 16)
        par = [(R_GPRE, t["a_norm_pre"]), (R_GPOST, t["a_norm_post"]), (R_CW, t["a_conv_w"][0]),
               (R_CB, t["a_conv_b"]), (R_BR, t["a_b_r"]), (R_BI, t["a_b_i"]), (R_LAM, t["a_lambda"]),
               (R_GKV, t["kv_norm"].rearrange("(a n) -> a n", a=1)), (R_BPRE, t["b_norm_pre"]),
               (R_BPOST, t["b_norm_post"]), (R_SC, t["state_conv"][0].rearrange("b w n -> (b w) n")),
               (R_SH, t["state_h"][0])]
        for r, src in par:
            sp.dma_start(xr[r:r + src.shape[0], 2, :], src).then_inc(S["par_in"], 16)
        sp.dma_start(ohx[:], t["onehot"]).then_inc(S["tab_in"], 16)
        sp.dma_start(tab[0:NBUCKET, 0, :], t["rel_bias_table"]).then_inc(S["tab_in"], 16)
        sp.dma_start(nsk[:], bass.AP(t["b_sinks"].tensor, 0, [[0, P], [1, NH]])).then_inc(S["tab_in"], 16)
        sp.dma_start(skp[:], t["b_sinks"]).then_inc(S["tab_in"], 16)
        xs = t["x_sample"].rearrange("b o n -> (b o) n")
        for n in range(9):
            slot = n % 3
            if n == 2:
                sp.wait_ge(S["par_turned"], 2)
            elif n > 2:
                sp.wait_ge(S["x_squared"], n - 2)
            if n < 8:
                sp.dma_start(xr[:, slot, :], t["x_prompt"][0, n * P:(n + 1) * P, :]).then_inc(S[f"x_in{slot}"], 16)
            else:
                sp.dma_start(xr[0:NB, slot, :], xs).then_inc(S[f"x_in{slot}"], 16)
        sp.dma_start(t["sample_conv"][0, :, 0:2, :], t["state_conv"][0, :, 1:3, :]).then_inc(S["state_out"], 16)

        def quarter(slot, src, split_before):
            sp.wait_ge(S["w_split"], split_before + 1 + CREDIT)
            sp.dma_start(raw[:, slot, :, :], src).then_inc(RAW[slot], 16)

        def chunk(w, col, base, order=range(NQ)):
            for j, kq in enumerate(order):
                quarter(j, w[:, kq * QK:(kq + 1) * QK, bass.ds(col, P)], base + j - NQ)

        def lands(kq, used, stored, srcs, n=QK):
            sp.wait_ge(S["w_used"], used + kq + 1 + CREDIT)
            for sm, v in stored:
                sp.wait_ge(S[sm], v)
            for half, src, cols in srcs:
                sp.dma_start(land[:, kq * QK:kq * QK + n, half, 0:cols],
                             src[kq * QK:kq * QK + n, :, 0:cols].rearrange("k p n -> p k n")).then_inc(LAND[kq], 16)

        with sp.Fori(0, A_ITERS) as i:
            b = i * A_SPLITS
            for n, off in enumerate((0, P, D)):
                for j in range(NQ):
                    quarter(j, w_in[:, j * QK:(j + 1) * QK, bass.ds(i * 256 + off, P)], b + n * NQ + j - NQ)
            for slot, w in ((0, w_r), (1, w_i)):
                sp.wait_ge(S["w_split"], b + 2 * NQ + slot + 1 + CREDIT)
                sp.dma_start(raw[:, slot, :, :].rearrange("p a b -> p (a b)").rearrange("p (k c) -> p k c", k=2),
                             w[bass.ds(i, 1)].rearrange("o p k c -> p (o k) c")).then_inc(RAW[slot], 16)
            for j, last in enumerate((10, 11, 14, 15)):
                quarter(G1_SLOTS[j], w_in[:, j * QK:(j + 1) * QK, bass.ds(i * 256 + D + P, P)], b + last)
        chunk(w_oa, 0, W_O1)
        for kq in range(NQ):
            n = QK if kq < NQ - 1 else QK - 2
            lands(kq, Q_O1 - NQ, [(f"y_out{m}", 32 * kq + 8 * n + 16) for m in range(2)], [(1, y_t, NT)], n)
        chunk(w_oa, P, W_O1 + NQ)
        with sp.Fori(1, O_ITERS) as i:
            for m in range(2):
                chunk(w_oa, i * 256 + m * P, i * 8 + m * NQ + W_O1)
        chunk(w_kv, 0, W_B)
        for kq in range(NQ):
            lands(kq, Q_B - NQ, [(f"o_out{m}", 32 * (kq + 1) + 16) for m in range(2)] + [("xt_out0", 16 * 5), ("xt_out1", 16 * 4)],
                  [(0, o_t, NT), (1, x_t, NT)])

        def group(i, first):
            b = i * 40 + W_B
            for c, (what, j) in enumerate(B_CHUNKS):
                if what == "q":
                    sp.wait_ge(S["b_used"], i * 4 + j + 1)
                    sp.dma_start(bb[:, j % 2, :, :], bias_blk[bass.ds(i * 8 + j * 2, 2)].rearrange("h q k -> q h k"))\
                        .then_inc(S[f"b_in{j % 2}"], 16)
                if first and c == 0:
                    continue
                w, off = {"k": (w_kv, i * P), "v": (w_kv, i * P + KVW), "q": (w_qg, i * 512 + j * P),
                          "g": (w_qg, i * 512 + j * P + D)}[what]
                chunk(w, off, b + c * NQ)

        sp.wait_ge(S["blk_out"], 16)
        group(0, True)
        with sp.Fori(1, B_ITERS) as i:
            group(i, False)
        chunk(w_ob, 0, W_O2, O2_ORDER)
        for n in range(4):
            sp.wait_ge(S[f"x1_out{n}"], 80)
        sp.wait_ge(S["kv_out"], 64 * B_ITERS + 64)
        sp.wait_ge(S["w_used"], Q_O2 - NQ + 1 + CREDIT)
        for cache, new, dst in ((t["cache_k"], t["sample_k"], kc), (t["cache_v"], t["sample_v"], vc)):
            cr = cache.rearrange("b r h d -> b r (h d)").rearrange("b r (c n) -> b c r n", c=4)
            nr = new.rearrange("b o h d -> b (o h d)").rearrange("b (c n) -> b c n", c=4)
            for b in range(NB):
                there = S["smp_k_in" if dst is kc else "smp_v_in"]
                sp.dma_start(dst[1:P, :, b, :], cr[b, :, 1:P, :].rearrange("c r n -> r c n")).then_inc(there, 16)
                sp.dma_start(dst[0:1, :, b, :], nr[b:b + 1]).then_inc(there, 16)
            if dst is kc:
                for kq in (1, 2):
                    lands(kq, Q_O2 - NQ, [(f"yb_out{m}", 32 * (kq + 1) + 16) for m in range(2)], [(1, y_t, SEQ)])
        lands(3, Q_O2 - NQ, [(f"yb_out{m}", 32 * B_ITERS + 16) for m in range(2)], [(1, y_t, SEQ)])
        sp.wait_ge(S["smp_pe"], 15)
        lands(0, Q_O2 - NQ, [(f"yb_out{m}", 32 + 16) for m in range(2)], [(1, y_t, SEQ)])
        chunk(w_ob, P, W_O2 + NQ)
        sp.dma_start(stg[:, 2:4, :, :].rearrange("p a b n -> p (a b) n"), x1_t[KT - QK:KT, :, :].rearrange("k p n -> p k n"))\
            .then_inc(S["x1_back"], 16)
        with sp.Fori(1, O_ITERS) as i:
            for m in range(2):
                chunk(w_ob, i * 256 + m * P, i * 8 + m * NQ + W_O2)
        for kq in range(NQ):
            lands(kq, Q_END - NQ, [(f"o_out{m}", 32 * (kq + 1) + 16 * O_ITERS + 16) for m in range(2)],
                  [(0, o_t, NT), (1, x1_t, NT)][:1 if kq == NQ - 1 else 2])
        sp.wait_ge(S["state_out"], 16 * 5)
        sp.wait_ge(S["kv_out"], 64 * B_ITERS + 64)
        sp.wait_ge(S["fin_out0"], 16 * 9)
        sp.wait_ge(S["fin_out1"], 16 * 9)
        sp.wait_ge(S["ys_out"], 16)
        for s in range(4):
            sp.wait_ge(S[f"x1_out{s}"], 80)

    @block.gpsimd
    def _(pool):
        pool.sem_inc(S["w_split"], CREDIT)
        pool.memset(ones[:], 1.0).then_inc(S["ones_ready"], 1)

        def split(slot, loads, free, count, gain, k0, also=None, gained=None):
            hold(pool, RAW[slot], loads * 16)
            hold(pool, S["w_used"], free + 1 + CREDIT)
            if also is not None:
                hold(pool, S["ri_done"], also + 1)
            hi, lo, w = wsp[:, slot, 0], wsp[:, slot, 1], raw[:, slot]
            if gain is None:
                pool.tensor_copy(hi, w).then_inc(S["w_hi"], 1)
                hold(pool, S["w_hi"], count)
                pool.tensor_tensor(lo, w, hi.bitcast(F32), ALU.subtract).then_inc(S["w_split"], 1)
                return
            for k in range(QK):
                op = pool.tensor_scalar(w[:, k], w[:, k], prm[:, k0 + k, gain:gain + 1], 1.0, ALU.mult, ALU.mult)
            op.then_inc(S["w_gained"], 1)
            hold(pool, S["w_gained"], gained)
            for k in range(QK):
                op = pool.tensor_scalar(hi[:, k], w[:, k], 1.0, 1.0, ALU.mult, ALU.mult)
            op.then_inc(S["w_hi"], 1)
            hold(pool, S["w_hi"], count)
            pool.tensor_tensor(lo, w, hi.bitcast(F32), ALU.subtract).then_inc(S["w_split"], 1)

        pool.wait_ge(S["par_turned"], 2)
        with pool.Fori(0, A_ITERS) as i:
            n = i * A_SPLITS
            for c in range(3):
                for j in range(NQ):
                    split(j, i * (4 if j < 2 else 5) + c + 1, i * 16 + c * NQ + j - NQ, n + c * NQ + j + 1, R_GPRE, j * QK,
                          also=(i * 12) if c == 0 and j < 2 else None, gained=i * 16 + c * NQ + j + 1)
            for slot in range(2):
                split(slot, i * 4 + 4, i * 16 + 8 + slot, n + 12 + slot + 1, None, 0)
            for j in range(NQ):
                split(G1_SLOTS[j], i * 5 + 4 + j // 2, i * 16 + 10 + j, n + 14 + j + 1, R_GPRE, j * QK, gained=i * 16 + 12 + j + 1)

        def out_phase(loads, qb, wb):
            with pool.Fori(0, O_ITERS) as i:
                for m in range(2):
                    for j in range(NQ):
                        split(j, i * 2 + m + 1 + loads[j], i * 8 + m * NQ + j - NQ + qb, i * 8 + m * NQ + j + 1 + wb, None, 0)

        pool.wait_ge(S["ri_done"], 12 * A_ITERS + 1)
        loads = [4 * A_ITERS, 4 * A_ITERS, 5 * A_ITERS, 5 * A_ITERS]
        out_phase(loads, Q_O1, W_O1)
        loads = [n + KT for n in loads]

        def scale_tiles(rstd_count, landed, step):
            pool.wait_ge(S["rstd_ready"], rstd_count)
            for kq in range(NQ):
                pool.wait_ge(LAND[kq], landed[kq])
                with pool.Fori(0, QK // step) as n:
                    a = land[:, bass.ds(n * step + (kq * QK + step - 1), 1), 0, :].rearrange("p o n -> p (o n)")
                    pool.tensor_tensor(a, a, rstd[:], ALU.mult).then_inc(S["x1_scaled"], 1)

        def group(i, chunks):
            for c in chunks:
                for j in range(NQ):
                    split(j, i * NBC + c + 1 + loads[j], i * 40 + c * NQ + j - NQ + Q_B, i * 40 + c * NQ + j + 1 + W_B,
                          R_GKV if c < 2 else R_BPRE, j * QK, gained=16 * A_ITERS + i * 40 + c * NQ + j + 1)

        group(0, [0])
        scale_tiles(2, [48] * NQ, 1)
        group(0, range(1, NBC))
        with pool.Fori(1, B_ITERS) as i:
            group(i, range(NBC))
        loads = [n + NBC * B_ITERS for n in loads]
        out_phase(loads, Q_O2, W_O2)
        scale_tiles(4, FIN_LANDED, 2)

    @block.tensor
    def _(pe):
        pe.sem_inc(S["w_used"], CREDIT)
        pe.sem_inc(S["ri_done"], 1)
        pe.wait_ge(S["const_in"], 16)
        pe.wait_ge(S["par_in"], 16 * 12)
        for k in range(KT):
            op = pe.transpose(ps[:, X0 + k // 8, (k % 8) * NROW:(k % 8 + 1) * NROW], xr[0:NROW, 2, k * P:(k + 1) * P],
                              ident[0:NROW, 0:NROW])
        op.then_inc(S["x_turned"], 1)
        for n in range(9):
            w = P if n < 8 else NB
            pe.wait_ge(S[f"x_in{n % 3}"], 16 * (n // 3 + 1))
            for j in range(NQ):
                if n >= 2:
                    pe.wait_ge(S["x_staged"], (n - 2) * NQ + j + 1)
                elif n == 1:
                    pe.wait_ge(S["par_turned"], 2)
                for k in range(QK):
                    op = pe.transpose(ps[:, 4 * (n % 2) + j, k * P:k * P + w],
                                      xr[0:w, n % 3, (j * QK + k) * P:(j * QK + k + 1) * P], ident[0:w, 0:w])
                op.then_inc(S["x_turned"], 1)
        def gemm(c, w0, which, ready, parts=None, slots=range(NQ), order=range(NQ),
                 before=None):
            b0 = SETS[which]
            pe.wait_ge(S["psum_read"], c + 1)
            for j in range(NQ):
                if before is not None:
                    before(j)
                if ready is not None:
                    pe.wait_ge(S["stage_used"], ready + (j + 1) * QK)
                pe.wait_ge(S["w_split"], w0 + j + 1 + CREDIT)
                for k in range(QK):
                    kk = order[j] * QK + k
                    for n, (wh, xh) in enumerate(((0, 0), (0, 1), (1, 0))):
                        for g in range(GROUPS):
                            op = pe.matmul(ps[:, b0 + g, 0:TG], wsp[:, slots[j], wh, k, :], xsp[:, kk, xh, grp(g)],
                                           start=(j == 0 and k == 0 and n == 0),
                                           stop=(j == NQ - 1 and k == QK - 1 and n == 2))
                    if k == QK - 1:
                        op.then_inc(S["w_used"], 1)
                    if k % 2 == 1 and parts:
                        for f in parts.get(j * 2 + k // 2, ()):
                            f()

        def tables_and_rms():
            pe.wait_ge(S["tab_ready"], 1)
            pe.wait_ge(S["tab_in"], 64)
            pe.wait_ge(S["x_staged"], 9 * NQ)
            pe.matmul(ps[0:NH, 3, 0:BW], tab[:, 0, :], ohx[:, 0:BW], start=True, stop=True)
            pe.matmul(ps[:, 4, 0:NH], ohx[:, BW:BW + P], tab[:, 1, :], start=True, stop=True).then_inc(S["bias_mm"], 1)
            pe.wait_ge(S["ones_ready"], 1)
            for n in range(9):
                w = P if n < 8 else NB
                pe.wait_ge(S["diag"], n + 1)
                pe.matmul(ps[:, (6, 7, 5)[n // 4], (n % 4) * P:(n % 4) * P + w], ones[0:w, :], dg[0:w, n % 2, 0:w],
                          start=True, stop=True).then_inc(S["diag_mm"], 1)

        def gates(i, g, m):
            if g == 0 and m == 0:
                pe.wait_ge(S["w_split"], i * A_SPLITS + 14 + CREDIT)
            if m == 0:
                pe.wait_ge(S["conv_lo"], i * 3 + g + 1)
            for gate in range(2):
                pe.wait_ge(S["r_read" if gate == 0 else "i_read"], i * 6 + g * 2 + m + 1)
                for k in range(2):
                    for n, (wh, xh) in enumerate(((0, 0), (0, 1), (1, 0))):
                        col = k * 256 + m * P
                        w = wsp[:, gate, wh].rearrange("p a b -> p (a b)")[:, col:col + P]
                        op = pe.matmul(ps[:, X0 + gate, 0:TG], w, csp[:, g % 2, xh, k, :],
                                       start=(k == 0 and n == 0), stop=(k == 1 and n == 2))
                op.then_inc(S["ri_done"], 1)

        def a_block(i, c0_parts=None):
            w0, c0 = i * A_SPLITS, i * 4
            gemm(c0, w0, 0, None, c0_parts)
            if c0_parts is not None:
                pe.wait_ge(S["rstd_ready"], 1)
            gemm(c0 + 1, w0 + 4, 1, None)
            gemm(c0 + 2, w0 + 8, 0, None)
            gemm(c0 + 3, w0 + 14, 1, None, {n: [lambda n=n: gates(i, n // 2, n % 2)] for n in range(6)}, G1_SLOTS)

        pe.wait_ge(S["x_lo"], 9)
        a_block(0, {1: [tables_and_rms]})
        with pe.Fori(1, A_ITERS) as i:
            a_block(i)

        def out_phase(c_base, w_base, ready, order):
            for m in range(2):
                gemm(m + c_base, m * NQ + w_base, m, ready, order=range(NQ) if m else order)
            with pe.Fori(1, O_ITERS) as i:
                for m in range(2):
                    gemm(i * 2 + m + c_base, i * 8 + m * NQ + w_base, m, None)

        def norm_sum(count, reads):
            pe.wait_ge(S["psum_read"], reads)
            pe.wait_ge(S["acc_ready"], count)
            for g in range(GROUPS):
                op = pe.matmul(ps[:, 5 + g, 0:TG], ones[:], acc[:, grp(g)], start=True, stop=True)
            op.then_inc(S["norm_mm"], 1)

        out_phase(C_O1, W_O1, 0, range(NQ))
        pe.wait_ge(S["psum_read"], C_B + 2)
        pe.wait_ge(S["oc_ready"], 1)
        for k in range(KT):
            op = pe.transpose(ps[0:NOC, k // 4, (k % 4) * P:(k % 4 + 1) * P], ocols[:, k, :], ident[:])
        op.then_inc(S["oc_turned"], 1)
        norm_sum(1, C_B + 2)
        pe.wait_ge(S["oc_sb"], 1)
        pe.wait_ge(S["rstd_ready"], 2)

        def scores(i, j, b, bank):
            n = i * 32 + j * NBLK + b
            pe.wait_ge(S["s_read"], n + 1)
            if b == 0:
                pe.wait_ge(S["psum_read"], i * NBC + Q_CHUNK[j] + C_B + 3)
            e, lo = j // 2, max(b - 1, 0) * BLK
            for hf in range(2):
                keys, r = (k1 if hf == e else k2), slice(hf * HD, hf * HD + HD)
                op = pe.matmul(ps[:, bank + hf, (BLK if b == 0 else 0):2 * BLK], q[r, j % 2, b * BLK:(b + 1) * BLK],
                               keys[r, lo:(b + 1) * BLK], start=True, stop=True)
            op.then_inc(S["s_done"], 1)

        def turn(i, j, b):
            n = i * 32 + j * NBLK + b
            pe.wait_ge(S["p_ready"], n + 1)
            pe.wait_ge(S["pt_lo"], n + 1)
            if b == 0 and j == 0:
                pe.wait_ge(S["kv_ready"], i + 1)
                pe.wait_ge(S["v_lo"], i + 1)
            for hf in range(2):
                for kt in range(1 if b == 0 else 0, 2):
                    op = pe.transpose(ps[:, X0, (hf * 2 + kt) * P:(hf * 2 + kt + 1) * P],
                                      pp[:, b % 2, hf, kt * P:(kt + 1) * P], ident[:])
            op.then_inc(S["p_turned"], 1)

        def mix(i, j, b):
            n = i * 32 + j * NBLK + b
            pe.wait_ge(S["pt_lo"], n + 2)
            pe.wait_ge(S["o_read"], n + 1)
            first = 1 if b == 0 else 0
            for kt in range(first, 2):
                v = vn[:, b - 1 + kt, j // 2].rearrange("p v d -> p (v d)")
                for part, p in enumerate((pt[:, b % 2], ptl[:, :, :])):
                    op = pe.matmul(ps[:, X1, 0:2 * BLK], v, p[:, :, kt * P:(kt + 1) * P],
                                   start=(kt == first and part == 0), stop=(kt == 1 and part == 1))
            op.then_inc(S["o_done"], 1)

        def turn_kv(i):
            pe.wait_ge(S["psum_read"], i * NBC + C_B + 4)
            pe.wait_ge(S["pt_lo"], i * 32 + 1)
            pe.wait_ge(S["o_read"], i * 32 + 1)
            for b in range(NBLK):
                op = pe.transpose(ps[:, X0 + b // 4, (b % 4) * P:(b % 4 + 1) * P], gb[:, b * BLK:(b + 1) * BLK], ident[:])
            pe.transpose(ps[0:NB, 3, 0:P], gb[:, SEQ:NT], ident[:])
            pe.transpose(ps[:, 3, P:2 * P], k1[:, SEQ - BLK:SEQ], ident[:])
            op = pe.transpose(ps[0:NB, 3, 2 * P:3 * P], k1[:, SEQ:NT], ident[:])
            op.then_inc(S["v_turned"], 1)

        def squares(kq):
            for k in range(kq * QK, kq * QK + QK):
                pe.wait_ge(S["x1_sq"], k + 1)
                for g in range(GROUPS):
                    op = pe.matmul(ps[:, 5 + g, 0:TG], ones[:], stg[:, X1_SLOTS[k % 4], 1, grp(g)], start=(k == 0), stop=(k == KT - 1))
                op.then_inc(S["x1_sum"], 1)

        def body(i, first):
            parts = [{} for _ in range(NBC)]

            def at(slot, f):
                parts[slot // 8].setdefault(slot % 8, []).append(f)

            at(2 * 8 + 2, lambda: turn_kv(i))
            for j, c in enumerate(ATT_AT):
                for b in range(NBLK):
                    at(c * 8 + b + 3, lambda j=j, b=b: mix(i, j, b))
            for j, c in enumerate(ATT_AT):
                for b in range(NBLK):
                    at(c * 8 + b + 2, lambda j=j, b=b: turn(i, j, b))
            for j, c in enumerate(ATT_AT):
                bank = SETS[(c + 1) % 2]
                for b in range(NBLK):
                    at(c * 8 + b, lambda j=j, b=b, bank=bank: scores(i, j, b, bank))
            for c in range(NBC):
                if c == 1 and first:
                    pe.wait_ge(S["rstd_ready"], 3)
                if c - 1 in ATT_AT:
                    j = ATT_AT.index(c - 1)
                    pe.wait_ge(S["s_read"], i * 32 + j * NBLK + NBLK + 1)
                if c == 3:
                    pe.wait_ge(S["kv_ready"], i + 1)
                gemm(i * NBC + c + C_B, i * 40 + c * NQ + W_B, c % 2, 16 if first and c == 0 else None, parts[c],
                     before=squares if first and c == 0 else None)

        body(0, True)
        with pe.Fori(1, B_ITERS) as i:
            body(i, False)

        pe.wait_ge(S["psum_read"], C_O2 + 2)
        pe.wait_ge(S["smp_k_in"], 16 * 2 * NB)
        for c in range(4):
            for b in range(NB):
                if b % 4 == 0 and c > 0:
                    pe.wait_ge(S["smp_act"], 2 * (c - 1) + b // 4 + 1)
                op = pe.transpose(ps[:, 1 + b // 4, (b % 4) * P:(b % 4 + 1) * P], kc[:, c, b, :], ident[:])
                if b % 4 == 3:
                    op.then_inc(S["smp_pe"], 1)
            for b in range(NB):
                if b % 4 == 0:
                    pe.wait_ge(S["smp_act"], 2 * c + b // 4 + 1)
                if b == 0 and c == 0:
                    pe.wait_ge(S["smp_q"], 1)
                col = (c * NB + b) * 8
                op = pe.matmul(ps[:, 3, col:col + 8], kst[:, b, :], qbd[:, c, b].rearrange("p e j v -> p (e j v)"),
                               start=True, stop=True)
            op.then_inc(S["smp_pe"], 1)
        pe.wait_ge(S["smp_dve"], 2)
        for n in range(2):
            pe.transpose(ps[:, 5, n * P:(n + 1) * P], sa[:, n, :], ident[:])
            op = pe.matmul(ps[:, 6, n:n + 1], skr[:, n * P:(n + 1) * P], ones[0:1, 0:1], start=True, stop=True)
        op.then_inc(S["smp_pe"], 1)
        pe.wait_ge(S["smp_dve"], 4)
        for n in range(2):
            op = pe.transpose(ps[:, 7, n * P:(n + 1) * P], sbm[:, n, :], ident[:])
        op.then_inc(S["smp_pe"], 1)
        pe.wait_ge(S["smp_dve"], 5)
        pe.wait_ge(S["smp_v_in"], 16 * 2 * NB)
        pairs = sa[:, :, :].rearrange("p n c -> p (n c)").rearrange("p (c e b t) -> p c b e t", c=4, e=2, b=NB)
        for c in range(4):
            for b in range(NB):
                col = (c * NB + b) * 8
                op = pe.matmul(ps[:, 0, col:col + 8], vc[:, c, b, :], pairs[:, c, b], start=True, stop=True)
        op.then_inc(S["smp_pe"], 1)
        pe.wait_ge(S["smp_split"], 2)
        out_phase(C_O2, W_O2, 32, O2_ORDER)
        norm_sum(2, C_O2 + KT + 2)
        pe.wait_ge(S["rstd_ready"], 4)
        for k in range(KT):
            b0, y = SETS[k % 2], land[:, k, 0, :]
            pe.wait_ge(S["fin_ready"], k + 1)
            pe.wait_ge(S["fin_sb"], k + 1)
            for b in range(NBLK):
                pe.transpose(ps[:, b0 + b // 4, (b % 4) * P:(b % 4 + 1) * P], y[:, b * BLK:(b + 1) * BLK], ident[:])
            pe.transpose(ps[0:NB, b0 + 2, 0:P], y[:, SEQ:NT], ident[:]).then_inc(S["fin_turned"], 1)


    @block.scalar
    def _(act):
        for s in range(4):
            act.sem_inc(S[f"x1_out{s}"], 16)
        for n in ("o_out0", "o_out1", "y_out0", "y_out1", "yb_out0", "yb_out1", "fin_out0", "fin_out1"):
            act.sem_inc(S[n], 16)
        act.sem_inc(S["kv_out"], 64)
        act.sem_inc(S["pt_ready"], 1)
        act.sem_inc(S["pt_lo"], 1)
        act.sem_inc(S["r_read"], 1)
        act.sem_inc(S["fin_sb"], 2)
        act.sem_inc(S["x1_sum"], 4)
        act.wait_ge(S["x_turned"], 1)
        for n in range(2):
            act.activation(prm[:, n * 8:n * 8 + 8, :].rearrange("p a b -> p (a b)"), ps[:, X0 + n, 0:8 * NROW], ACT.Copy)\
                .then_inc(S["par_turned"], 1)
        act.wait_ge(S["root_in"], 1)
        act.activation(spt[:, 1, :], spt[:, 0, :], ACT.Exp, scale=-1.0).then_inc(S["root_done"], 1)
        for n in range(9):
            w = P if n < 8 else NB
            if n >= 2:
                act.wait_ge(S["x_lo"], n - 1)
                act.wait_ge(S[f"xt_out{n % 2}"], 16 * (n // 2))
            for j in range(NQ):
                act.wait_ge(S["x_turned"], n * NQ + j + 2)
                act.activation(st[:, n % 2, j * QK:(j + 1) * QK, 0:w],
                               ps[:, 4 * (n % 2) + j, 0:QK * P].rearrange("p (k c) -> p k c", k=QK)[:, :, 0:w], ACT.Copy)\
                    .then_inc(S["x_staged"], 1)
            xt = xr[0:w, n % 3, :]
            act.activation(xt, xt, ACT.Square, accum_out=sxs[0:w, 0, n:n + 1]).then_inc(S["x_squared"], 1)
            act.wait_ge(S["x_staged"], (n + 1) * NQ)
            act.dma_start(x_t[:, :, n * P:n * P + w].rearrange("k p c -> p k c"), st[:, n % 2, :, 0:w])\
                .then_inc(S[f"xt_out{n % 2}"], 16)
        act.wait_ge(S["bias_sb"], 1)
        act.dma_start(bias_row[:, :], rstd[0:NH, 0:BW]).then_inc(S["bias_out"], 16)
        act.wait_ge(S["bias_out"], 16)
        act.dma_start(bias_blk[:, :, :], bass.AP(bias_row.tensor, BLK - 1, [[BW, NH], [-1, BLK], [1, 2 * BLK]]))\
            .then_inc(S["blk_out"], 16)
        act.wait_ge(S["root_in"], 2)
        act.activation(sxs[:, 1, 0:8], sxs[:, 0, 0:8], ACT.Sqrt).then_inc(S["root_done"], 1)
        act.activation(sxs[0:NB, 1, 8:9], sxs[0:NB, 0, 8:9], ACT.Sqrt).then_inc(S["root_done"], 1)

        def conv_hi(i, g):
            act.activation(csp[:, g % 2, 0, :, :], cv[:, :, grp(g)], ACT.Copy).then_inc(S["conv_hi"], 1)

        def gate_tanh(src, n, which):
            for g in range(GROUPS):
                act.wait_ge(S["gs_ready"], n * GROUPS + g + 1)
                act.activation(ps[:, SETS[which] + g, 0:TG], src[:, grp(g)], ACT.Tanh, scale=0.5)\
                    .then_inc(S["gt_ready"], 1)

        def restage(loaded, cols, quarters, tiles=QK):
            for kq in quarters:
                act.wait_ge(LAND[kq], loaded)
                for k in range(kq * QK, kq * QK + tiles):
                    act.activation(xsp[:, k, 0, 0:cols], land[:, k, 1, 0:cols], ACT.Copy).then_inc(S["stage_hi"], 1)

        A_STEPS = 12

        def recurrent(i, last):
            own = Chain(act, S["act_step"], 0, A_STEPS, i)
            act.wait_ge(S["cv_ready"], i * 2 + 2)
            for g in range(2):
                conv_hi(i, g)
            gate_tanh(gs, i * 2, 0)
            for g in range(GROUPS):
                for m in range(2):
                    u0 = i * 12 + g * 4 + m * 2
                    k = i * 2 + m
                    hold(act, S["ri_done"], u0 + 2)
                    hm = h[:, m, grp(g)]
                    act.activation(hm, ps[:, X0, 0:TG], ACT.Tanh, bias=hbr[:, bass.ds(k, 1)], scale=0.5).then_inc(S["r_read"], 1)
                    hold(act, S["ri_done"], u0 + 3)
                    act.activation(ps[:, X1, 0:TG], ps[:, X1, 0:TG], ACT.Tanh, bias=hbi[:, bass.ds(k, 1)], scale=0.5)\
                        .then_inc(S["i_turned"], 1)
                    hold(act, S["r_read"], i * 6 + g * 2 + m + 2)
                    own.step(act.activation(rc[:, m, grp(g)], hm, ACT.Exp, bias=nsp4[:, bass.ds(k, 1)], scale=nsp4[:, bass.ds(k, 1)]))
                    hold(act, S["act_step"], i * A_STEPS + own.n)
                    own.step(act.activation(hm, hm, ACT.Tanh, bias=sp2[:, bass.ds(k, 1)], scale=sp2[:, bass.ds(k, 1)]))
                if g == 0:
                    act.wait_ge(S["ri_done"], i * 12 + 5)
                    conv_hi(i, 2)
            own.end()
            if last:
                restage(16, NT, (0,))
            act.wait_ge(S["w_ready"], i + 1)
            act.activation(h[:, :, :], h[:, :, :], ACT.Sqrt).then_inc(S["root"], 1)
            if last:
                restage(16, NT, (1,))
            gate_tanh(g1, i * 2 + 1, 1)
            if last:
                restage(16, NT, (2,))
                restage(16, NT, (3,), 2)
                act.wait_ge(S["w_used"], Q_O1 + CREDIT)
                for m in range(2):
                    act.wait_ge(S["y_ready"], i * 2 + m + 1)
                    act.activation(xsp[:, KT - 2 + m, 0, :], (gs[:], g1)[m], ACT.Copy).then_inc(S["stage_hi"], 1)
                return
            for m in range(2):
                act.wait_ge(S["y_ready"], i * 2 + m + 1)
                act.dma_start(y_t[bass.ds(i * 2 + m, 1)].rearrange("o p n -> (o p) n"), (gs[:], g1)[m]).then_inc(S[f"y_out{m}"], 16)

        with act.Fori(0, A_ITERS - 1) as i:
            recurrent(i, False)
        recurrent(A_ITERS - 1, True)

        def out_phase(c_base, before):
            with act.Fori(0, O_ITERS) as i:
                for m in range(2):
                    c = i * 2 + m
                    chunk_done(act, c + c_base)
                    act.wait_ge(S[f"o_out{m}"], i * 16 + 16 * O_ITERS * before + 16)
                    act.wait_ge(S["o_sq"], c + KT * before + 1)
                    for g in range(GROUPS):
                        act.activation(stg[:, m, 0, grp(g)], ps[:, SETS[m] + g, 0:TG], ACT.Copy)
                        op = act.activation(stg[:, m, 1, grp(g)], ps[:, SETS[m] + g, 0:TG], ACT.Square)
                    op.then_inc(S["psum_read"], 1)
                    act.wait_ge(S["psum_read"], c + c_base + 3)
                    act.dma_start(o_t[bass.ds(c, 1)].rearrange("o p n -> (o p) n"), stg[:, m, 0, :]).then_inc(S[f"o_out{m}"], 16)

        def root_of_norm(n):
            act.activation(warm[:, n - 1:n], ident[:, 0:1], ACT.Sqrt)
            for g in range(GROUPS):
                act.wait_ge(S["root_in"], 2 + (n - 1) * GROUPS + g + 1)
                act.activation(rstd[:, grp(g)], rstd[:, grp(g)], ACT.Sqrt).then_inc(S["root_done"], 1)

        out_phase(C_O1, 0)
        act.wait_ge(S["oc_turned"], 1)
        for n in range(4):
            op = act.activation(rows[:, n * 512:(n + 1) * 512], ps[0:NOC, n, :], ACT.Copy)
        op.then_inc(S["oc_sb"], 1)
        act.wait_ge(S["oc_sb"], 1)
        act.dma_start(t["prompt_conv"][0, 0], rows[0:3, :]).then_inc(S["state_out"], 16)
        act.dma_start(t["sample_conv"][0, :, 2, :], rows[3:11, :]).then_inc(S["state_out"], 16)
        act.dma_start(t["prompt_h"][0], rows[11:12, :]).then_inc(S["state_out"], 16)
        act.dma_start(t["sample_h"][0], rows[12:20, :]).then_inc(S["state_out"], 16)
        root_of_norm(1)
        with act.Fori(0, 4) as i:
            for s in range(4):
                k = i * 4 + s
                x1, sq = stg[:, X1_SLOTS[s], 0, :], stg[:, X1_SLOTS[s], 1, :]
                hold(act, S["x1_ready"], k + 1)
                act.activation(xsp[:, bass.ds(k, 1), 0, :].rearrange("p o n -> p (o n)"), x1, ACT.Copy).then_inc(S["stage_hi"], 1)
                act.wait_ge(S["x1_sum"], k + 1)
                act.activation(sq, x1, ACT.Square).then_inc(S["x1_sq"], 1)
                act.dma_start(x1_t[bass.ds(k, 1)].rearrange("o p n -> (o p) n"), x1).then_inc(S[f"x1_out{s}"], 16)
        root_of_norm(2)

        pk = t["prompt_k"].rearrange("a r h d -> (a r) (h d)")
        pv = t["prompt_v"].rearrange("a r h d -> (a r) (h d)")
        sk = t["sample_k"].rearrange("b o h d -> (b o) (h d)")
        sv = t["sample_v"].rearrange("b o h d -> (b o) (h d)")

        def keys_values(i):
            act.wait_ge(S["psum_read"], i * NBC + C_B + 3)
            act.activation(k2[0:HD, :], k1[HD:P, :], ACT.Copy)
            act.activation(k2[HD:P, :], k1[0:HD, :], ACT.Copy)
            act.wait_ge(S["v_turned"], i + 1)
            act.wait_ge(S["kv_out"], i * 64 + 64)
            for n in range(2):
                act.activation(vn[:, n * 4:n * 4 + 4, :, 0, :], ps[:, X0 + n, :].rearrange("p (b e d) -> p b e d", e=2, d=HD), ACT.Copy)
            act.activation(kvo[:, 0, :], ps[:, X1, 3 * P:4 * P], ACT.Copy).then_inc(S["v_hi"], 1)
            act.activation(ol[HD:HD + NB, 0:P], ps[0:NB, 3, 0:P], ACT.Copy)
            act.activation(kvo[:, 1, :], ps[:, 3, P:2 * P], ACT.Copy)
            act.activation(ol[HD:HD + NB, P:2 * P], ps[0:NB, 3, 2 * P:3 * P], ACT.Copy).then_inc(S["kv_ready"], 1)
            act.wait_ge(S["kv_ready"], i + 1)
            col = bass.ds(i * P, P)
            act.dma_start(pk[:, col], kvo[:, 1, :]).then_inc(S["kv_out"], 16)
            act.dma_start(pv[:, col], kvo[:, 0, :]).then_inc(S["kv_out"], 16)
            act.dma_start(sk[:, col], ol[HD:HD + NB, P:2 * P]).then_inc(S["kv_out"], 16)
            act.dma_start(sv[:, col], ol[HD:HD + NB, 0:P]).then_inc(S["kv_out"], 16)

        def exps(i, j, b):
            n = i * 32 + j * NBLK + b
            lo = BLK if b == 0 else 0
            act.wait_ge(S["negm"], n + 1)
            act.activation(mx[:, 3, :], mx[:, 2, :], ACT.Exp)
            for hf in range(2):
                s = pp[:, b % 2, hf, lo:2 * BLK]
                op = act.activation(s, s, ACT.Exp, bias=mx[:, 1, hf:hf + 1], accum_out=mx[:, 4, hf:hf + 1])
            op.then_inc(S["p_exp"], 1)

        def turned(i, j, b):
            n = i * 32 + j * NBLK + b
            act.wait_ge(S["p_turned"], n + 1)
            if b == 0:
                act.activation(pt[:, 0, :, BLK:2 * BLK], ps[:, X0, :].rearrange("p (h c) -> p h c", h=2)[:, :, BLK:2 * BLK], ACT.Copy)\
                    .then_inc(S["pt_ready"], 1)
            else:
                act.activation(pt[:, b % 2, :, :].rearrange("p h c -> p (h c)"), ps[:, X0, :], ACT.Copy).then_inc(S["pt_ready"], 1)

        def output_low(i, j, b):
            act.wait_ge(S["o_done"], i * 32 + j * NBLK + b + 1)
            act.activation(ol[0:HD, :], ps[HD:P, X1, 0:2 * BLK], ACT.Copy).then_inc(S["o_low"], 1)

        def store_y(i, j):
            act.wait_ge(S["y_ready"], i * 4 + j + 1 + 2 * A_ITERS)
            act.dma_start(y_t[bass.ds(i * 4 + j, 1), :, 0:SEQ].rearrange("o p n -> (o p) n"), q[:, j % 2, 0:SEQ])\
                .then_inc(S[f"yb_out{j % 2}"], 16)

        with act.Fori(0, B_ITERS) as i:
            todo = [(16, 0, lambda: keys_values(i))]
            for j in range(4):
                at = ATT_AT[j] * 8
                for b in range(NBLK):
                    todo.append((at + b + 3, 0.5, lambda j=j, b=b: output_low(i, j, b)))
                    todo.append((at + b + 2, 1, lambda j=j, b=b: turned(i, j, b)))
                    todo.append((at + b, 2, lambda j=j, b=b: exps(i, j, b)))
                g = G_CHUNK[j]
                todo.append((g * 8 + 8, 3, lambda j=j, g=g: gate_tanh(gb, i * 4 + j + 2 * A_ITERS, g % 2)))
                todo.append((g * 8 + 10, 0, lambda j=j: store_y(i, j)))
            for _, _, f in sorted(todo, key=lambda x: x[:2]):
                f()

        restage(64, SEQ, (1, 2))
        for c in range(4):
            act.wait_ge(S["smp_pe"], 3 * c + 1)
            for n in range(2):
                act.wait_ge(S["smp_pe"], 3 * c + n + 1)
                act.activation(kst[:, n * 4:n * 4 + 4, :].rearrange("p a b -> p (a b)"), ps[:, 1 + n, :], ACT.Copy)\
                    .then_inc(S["smp_act"], 1)
        act.wait_ge(S["smp_dve"], 3)
        act.activation(sx[:, 3, :], sx[:, 2, :], ACT.Exp)
        for n in range(2):
            op = act.activation(sbm[:, n, :], ps[:, 5, n * P:(n + 1) * P], ACT.Exp, bias=sx[:, 1, n:n + 1],
                                accum_out=sx[:, 4, n:n + 1])
        op.then_inc(S["smp_act"], 1)
        restage(64, SEQ, (3, 0))
        out_phase(C_O2, 1)
        root_of_norm(3)
        yp = t["y_prompt"][0].rearrange("(b p) (k c) -> k p b c", p=P, c=P)
        with act.Fori(0, 4) as i:
            for s in range(4):
                k, b0 = i * 4 + s, SETS[s % 2]
                yn = raw[:, 2 * (s % 2):2 * (s % 2) + 2].rearrange("p a b c -> p (a b c)")
                act.wait_ge(S["fin_turned"], k + 1)
                act.wait_ge(S[f"fin_out{s % 2}"], i * 32 + 16 * (s // 2) + 16)
                for n in range(2):
                    act.activation(yn[:, n * 512:(n + 1) * 512], ps[:, b0 + n, :], ACT.Copy)
                act.activation(rows[0:NB, bass.ds(k * P, P)], ps[0:NB, b0 + 2, 0:P], ACT.Copy).then_inc(S["fin_sb"], 1)
                act.wait_ge(S["fin_sb"], k + 3)
                act.dma_start(yp[bass.ds(k, 1)].rearrange("o p b c -> p (o b) c"), yn.rearrange("p (b c) -> p b c", c=P))\
                    .then_inc(S[f"fin_out{s % 2}"], 16)
        act.dma_start(t["y_sample"].rearrange("b o n -> (b o) n"), rows[0:NB, :]).then_inc(S["ys_out"], 16)

    @block.vector
    def _(dve):
        own = Chain(dve, S["dve_step"])
        for n, v in (("psum_read", 2), ("o_sq", 2), ("s_read", 1),
                     ("o_read", 1), ("i_read", 1)):
            dve.sem_inc(S[n], v)
        dve.wait_ge(S["tab_in"], 64)
        own.link(dve.memset(tab[NBUCKET:NBUCKET + 1, :, :], 1.0))
        own.link(dve.tensor_scalar(sxs[0:1, 0, 0:16], skp[0:1, 0:16], 1.0, None, ALU.mult))
        own.link(dve.tensor_scalar(sxs[0:1, 1, 0:16], skp[0:1, 16:32], 1.0, None, ALU.mult))
        by = tab[0:NBUCKET, :, :].rearrange("p v (c e j w) -> p v c e j w", c=4, e=2, j=2)
        for e in range(2):
            for w in range(2):
                for c in range(4):
                    own.step(dve.tensor_copy(by[:, 1, c, e, :, w], by[:, 0, c, e, :, w ^ e]))
        for half in range(2):
            src = sxs[0:1, half, :].rearrange("p (c e j w) -> p c e j w", c=2, e=2, j=2)
            dst = skp[0:1, half * 16:half * 16 + 16].rearrange("p (c e j w) -> p c e j w", c=2, e=2, j=2)
            for e in range(2):
                for w in range(2):
                    for c in range(2):
                        own.step(dve.tensor_copy(dst[:, c, e, :, w], src[:, c, e, :, w ^ e]))
        own.wait()
        dve.tensor_scalar(nsk[:], nsk[:], -1.0, None, ALU.mult).then_inc(S["tab_ready"], 1)
        dve.wait_ge(S["par_turned"], 2)
        lam = prm[:, :, R_LAM]
        own.link(dve.tensor_scalar(spt[:, 2, :], lam, -1.0, None, ALU.mult))
        dve.tensor_tensor(spt[:, 0, :], lam, spt[:, 2, :], ALU.max).then_inc(S["root_in"], 1)
        own.step(dve.tensor_scalar(hbr[:], prm[:, :, R_BR], 0.5, None, ALU.mult))
        own.step(dve.tensor_scalar(hbi[:], prm[:, :, R_BI], 0.5, None, ALU.mult))
        own.link(dve.tensor_scalar(spt[:, 2, :], spt[:, 2, :], 0.0, 2.0, ALU.max, ALU.mult))
        dve.wait_ge(S["root_done"], 1)
        e_, s_, s2_ = spt[:, 1, :], spt[:, 0, :], spt[:, 3, :]
        own.link(dve.tensor_scalar(s_, e_, 2.0, None, ALU.add))
        own.link(dve.reciprocal(s_, s_))
        own.link(dve.tensor_tensor(s_, s_, e_, ALU.mult))
        own.link(dve.tensor_tensor(s2_, s_, s_, ALU.mult))
        own.link(dve.tensor_scalar(sp2[:], s2_, 1.0 / 17.0, 1.0 / 15.0, ALU.mult, ALU.add))
        for n in (13, 11, 9, 7, 5, 3, 1):
            own.link(dve.tensor_tensor(sp2[:], sp2[:], s2_, ALU.mult))
            own.link(dve.tensor_scalar(sp2[:], sp2[:], 1.0 / n, None, ALU.add))
        own.link(dve.scalar_tensor_tensor(out=sp2[:], in0=sp2[:], scalar=4.0, in1=s_, op0=ALU.mult, op1=ALU.mult))
        own.link(dve.tensor_tensor(sp2[:], sp2[:], spt[:, 2, :], ALU.add))
        own.step(dve.tensor_scalar(nsp4[:], sp2[:], -2.0, None, ALU.mult))
        for n in range(9):
            w = P if n < 8 else NB
            cols = slice(n * P, n * P + w)
            dve.wait_ge(S["x_staged"], (n + 1) * NQ)
            dve.tensor_copy(xsp[:, :, 0, cols], st[:, n % 2, :, 0:w]).then_inc(S["x_hi"], 1)
            dve.wait_ge(S["x_hi"], n + 1)
            dve.tensor_tensor(xsp[:, :, 1, cols], st[:, n % 2, :, 0:w], xsp[:, :, 0, cols].bitcast(F32), ALU.subtract)\
                .then_inc(S["x_lo"], 1)
        dve.wait_ge(S["x_squared"], 9)
        dve.wait_ge(S["bias_mm"], 1)
        own.step(dve.tensor_copy(bsm[:], ps[:, 4, 0:NH]))
        dve.tensor_copy(rstd[0:NH, 0:BW], ps[0:NH, 3, 0:BW]).then_inc(S["bias_sb"], 1)

        def mean_eps(out, in_):
            return dve.tensor_scalar(out, in_, 1.0 / D, EPS, ALU.mult, ALU.add)

        own.step(mean_eps(sxs[:, 0, 0:8], sxs[:, 0, 0:8]))
        mean_eps(sxs[0:NB, 0, 8:9], sxs[0:NB, 0, 8:9]).then_inc(S["root_in"], 1)
        dve.wait_ge(S["root_done"], 3)
        own.step(dve.reciprocal(sxs[:, 1, 0:8], sxs[:, 1, 0:8]))
        own.link(dve.reciprocal(sxs[0:NB, 1, 8:9], sxs[0:NB, 1, 8:9]))
        for n in range(9):
            w = P if n < 8 else NB
            if n >= 2:
                dve.wait_ge(S["diag_mm"], n - 1)
            dve.tensor_scalar(dg[0:w, n % 2, 0:w], ident[0:w, 0:w], sxs[0:w, 1, n:n + 1], None, ALU.mult).then_inc(S["diag"], 1)
        dve.wait_ge(S["diag_mm"], 9)
        dve.wait_ge(S["bias_out"], 16)
        own.step(dve.tensor_copy(rstd[:, 0:512], ps[:, 6, :]))
        own.step(dve.tensor_copy(rstd[:, 512:SEQ], ps[:, 7, :]))
        dve.tensor_copy(rstd[:, SEQ:NT], ps[:, 5, 0:NB]).then_inc(S["rstd_ready"], 1)
        dve.wait_ge(S["rstd_ready"], 1)
        dve.wait_ge(S["xt_out0"], 16 * 5)
        dve.wait_ge(S["xt_out1"], 16 * 4)
        own.link(dve.memset(u[:, 0:4], 0.0))

        def evac(c, dst, which, scale=None, last=None):
            chunk_done(dve, c)
            for g in range(GROUPS):
                src = ps[:, SETS[which] + g, 0:TG]
                if scale is None:
                    op = dve.tensor_tensor(dst[:, grp(g)], src, rstd[:, grp(g)], ALU.mult)
                else:
                    op = dve.scalar_tensor_tensor(out=dst[:, grp(g)], in0=src, scalar=scale, in1=rstd[:, grp(g)],
                                                  op0=ALU.mult, op1=ALU.mult)
                if last is None:
                    op.then_inc(S["gs_ready"], 1)
            if last is not None:
                op.then_inc(last, 1)

        def silu(n, dst, which):
            for g in range(GROUPS):
                dve.wait_ge(S["gt_ready"], n * GROUPS + g + 1)
                op = dve.scalar_tensor_tensor(out=dst[:, grp(g)], in0=ps[:, SETS[which] + g, 0:TG], scalar=1.0,
                                              in1=dst[:, grp(g)], op0=ALU.add, op1=ALU.mult)
            op.then_inc(S["psum_read"], 1)

        A_STEPS = 22
        base = own.end()

        def restage(before, cols, quarters, tiles=QK):
            for n, kq in enumerate(quarters):
                for k in range(kq * QK, kq * QK + tiles):
                    dve.wait_ge(S["stage_hi"], before + n * QK + k % QK + 1)
                    dve.tensor_tensor(xsp[:, k, 1, 0:cols], land[:, k, 1, 0:cols], xsp[:, k, 0, 0:cols].bitcast(F32), ALU.subtract)\
                        .then_inc(S["stage_used"], 1)

        def recurrent(i, last):
            own = Chain(dve, S["dve_step"], base, A_STEPS, i)
            for m in range(2):
                k, c = i * 2 + m, i * 4 + m

                def col(r, w=1, k=k):
                    return prm[:, bass.ds(k, 1), r:r + w].rearrange("p o n -> p (o n)")

                if m == 0:
                    dve.wait_ge(S["y_out1"], i * 16 + 16)
                evac(c, u[:, 3:3 + NT], m, last=S["psum_read"])
                dve.wait_ge(S["psum_read"], c + 3)
                oc = ocols[:, bass.ds(k, 1), :].rearrange("p o n -> p (o n)")
                own.step(dve.tensor_copy(oc[:, 0:11], u[:, SEQ:SEQ + 11]))
                v = cv[:, m, :]
                own.link(dve.tensor_scalar(v, u[:, 3:3 + NT], col(R_CW + 3), col(R_CB), ALU.mult, ALU.add))
                for tap in (2, 1, 0):
                    own.link(dve.scalar_tensor_tensor(out=v[:, 0:SEQ], in0=u[:, tap:tap + SEQ], scalar=col(R_CW + tap),
                                                      in1=v[:, 0:SEQ], op0=ALU.mult, op1=ALU.add))
                    op = dve.scalar_tensor_tensor(out=v[:, SEQ:NT], in0=col(R_SC, 3 * NB).rearrange("p (b w) -> p b w", w=3)[:, :, tap],
                                                  scalar=col(R_CW + tap), in1=v[:, SEQ:NT], op0=ALU.mult, op1=ALU.add)
                    if tap:
                        own.link(op)
                    else:
                        op.then_inc(S["cv_ready"], 1)
                dve.wait_ge(S["cv_ready"], i * 2 + m + 1)

            def conv_lo(g):
                dve.wait_ge(S["conv_hi"], i * 3 + g + 1)
                dve.tensor_tensor(csp[:, g % 2, 1, :, :], cv[:, :, grp(g)], csp[:, g % 2, 0, :, :].bitcast(F32), ALU.subtract)\
                    .then_inc(S["conv_lo"], 1)

            conv_lo(0)
            conv_lo(1)
            dve.wait_ge(S["y_out0"], i * 16 + 16)
            evac(i * 4 + 2, gs, 0)
            silu(i * 2, gs, 0)
            for g in range(GROUPS):
                for m in range(2):
                    dve.wait_ge(S["i_turned"], i * 6 + g * 2 + m + 1)
                    if g == 1 and m == 0:
                        conv_lo(2)
                    dve.scalar_tensor_tensor(out=cv[:, m, grp(g)], in0=ps[:, X1, 0:TG], scalar=1.0, in1=cv[:, m, grp(g)],
                                             op0=ALU.add, op1=ALU.mult).then_inc(S["i_read"], 1)
            dve.wait_ge(S["act_step"], i * 12 + 12)
            dve.tensor_scalar(h[:, :, :], h[:, :, :], TINY, None, ALU.max).then_inc(S["w_ready"], 1)
            if last:
                restage(0, NT, (0,))
            evac(i * 4 + 3, g1, 1)
            if last:
                restage(4, NT, (1,))
            dve.wait_ge(S["root"], i + 1)
            own.link(dve.scalar_tensor_tensor(out=h[:, :, :], in0=rc[:, :, :], scalar=1.0, in1=h[:, :, :], op0=ALU.add, op1=ALU.mult))
            own.step(dve.scalar_tensor_tensor(out=cv[:, :, :], in0=cv[:, :, :], scalar=0.5, in1=h[:, :, :], op0=ALU.mult, op1=ALU.mult))
            silu(i * 2 + 1, g1, 1)
            own.wait()
            if last:
                restage(8, NT, (2,))
            for m in range(2):
                k = i * 2 + m
                h0 = prm[:, bass.ds(k, 1), R_SH:R_SH + NB].rearrange("p o n -> p (o n)")
                own.link(dve.tensor_tensor(rc[:, m, SEQ:NT], rc[:, m, SEQ:NT], h0, ALU.mult))
                own.step(dve.tensor_tensor(h[:, m, SEQ:NT], cv[:, m, SEQ:NT], rc[:, m, SEQ:NT], ALU.add))
                own.link(dve.tensor_tensor_scan(h[:, m, 0:SEQ], rc[:, m, 0:SEQ], cv[:, m, 0:SEQ], 0.0, ALU.mult, ALU.add))
                oc = ocols[:, bass.ds(k, 1), :].rearrange("p o n -> p (o n)")
                dve.tensor_copy(oc[:, 11:20], h[:, m, SEQ - 1:NT]).then_inc(S["oc_ready"], 1)
                gate = (gs[:], g1)[m]
                dve.wait_ge(S["psum_read"], i * 4 + 6)
                dve.scalar_tensor_tensor(out=gate, in0=h[:, m, :], scalar=0.5, in1=gate, op0=ALU.mult, op1=ALU.mult)\
                    .then_inc(S["y_ready"], 1)
            if last:
                restage(12, NT, (3,), 2)
                for m in range(2):
                    k = KT - 2 + m
                    dve.wait_ge(S["stage_hi"], k + 1)
                    dve.tensor_tensor(xsp[:, k, 1, :], (gs[:], g1)[m], xsp[:, k, 0, :].bitcast(F32), ALU.subtract)\
                        .then_inc(S["stage_used"], 1)
            return own

        with dve.Fori(0, A_ITERS - 1) as i:
            recurrent(i, False)
        base = recurrent(A_ITERS - 1, True).end(A_ITERS)

        def out_phase(c_base, before):
            with dve.Fori(0, O_ITERS) as i:
                for m in range(2):
                    c = i * 2 + m
                    dve.wait_ge(S["psum_read"], c + c_base + 3)
                    dve.wait_ge(S["o_sq"], c + KT * before + 2)
                    dve.tensor_tensor(acc[:], acc[:], stg[:, m, 1, :], ALU.add).then_inc(S["o_sq"], 1)
            dve.wait_ge(S["o_sq"], KT * (before + 1) + 2)

        def clear_acc():
            own.link(dve.memset(acc[:], 0.0))

        def norm(n, summed):
            dve.wait_ge(*summed)
            for g in range(GROUPS):
                mean_eps(rstd[:, grp(g)], ps[:, 5 + g, 0:TG]).then_inc(S["root_in"], 1)
            for g in range(GROUPS):
                dve.wait_ge(S["root_done"], 3 + (n - 1) * GROUPS + g + 1)
                op = dve.reciprocal(rstd[:, grp(g)], rstd[:, grp(g)])
            op.then_inc(S["rstd_ready"], 1)
            dve.wait_ge(S["rstd_ready"], n + 1)

        own = Chain(dve, S["dve_step"], base)
        dve.wait_ge(S["y_out0"], 16 * A_ITERS)
        dve.wait_ge(S["y_out1"], 16 * A_ITERS)
        dve.wait_ge(S["stage_used"], KT)
        clear_acc()
        out_phase(C_O1, 0)
        dve.sem_inc(S["acc_ready"], 1)
        norm(1, (S["norm_mm"], 1))
        with dve.Fori(0, 4) as i:
            for s in range(4):
                k = i * 4 + s
                tile = land[:, bass.ds(k, 1), :, :]
                if X1_SLOTS[s] < 2:
                    dve.wait_ge(S[f"o_out{X1_SLOTS[s]}"], 16 * O_ITERS + 16)
                hold(dve, S["x1_scaled"], k + 1)
                hold(dve, S[f"x1_out{s}"], i * 16 + 16)
                dve.scalar_tensor_tensor(out=stg[:, X1_SLOTS[s], 0, :], in0=tile[:, :, 0, :].rearrange("p o n -> p (o n)"),
                                         scalar=prm[:, bass.ds(k, 1), R_GPOST:R_GPOST + 1].rearrange("p o n -> p (o n)"),
                                         in1=tile[:, :, 1, :].rearrange("p o n -> p (o n)"), op0=ALU.mult, op1=ALU.add)\
                    .then_inc(S["x1_ready"], 1)
            for s in range(4):
                k = i * 4 + s
                x = xsp[:, bass.ds(k, 1), :, :]
                dve.wait_ge(S["stage_hi"], k + KT + 1)
                dve.tensor_tensor(x[:, :, 1, :].rearrange("p o n -> p (o n)"), stg[:, X1_SLOTS[s], 0, :],
                                  x[:, :, 0, :].rearrange("p o n -> p (o n)").bitcast(F32), ALU.subtract)\
                    .then_inc(S["stage_used"], 1)
            dve.wait_ge(S["x1_sq"], i * 4 + 4)
            dve.wait_ge(S["stage_used"], i * 4 + KT + 4)
        norm(2, (S["x1_sum"], KT + 4))
        for s in range(4):
            dve.wait_ge(S[f"x1_out{s}"], 80)
        dve.sem_inc(S["b_used"], 2)

        def softmax_in(i, j, b):
            n = i * 32 + j * NBLK + b
            lo = BLK if b == 0 else 0
            bank = SETS[(ATT_AT[j] + 1) % 2]
            if b == 0:
                hold(dve, S[f"b_in{j % 2}"], i * 32 + 16 * (j // 2) + 16)
            hold(dve, S["s_done"], n + 1)
            for hf in range(2):
                op = dve.tensor_tensor_reduce(pp[:, b % 2, hf, lo:2 * BLK], ps[:, bank + hf, lo:2 * BLK],
                                              bb[:, j % 2, hf, lo:2 * BLK], 1.0, NEG, ALU.add, ALU.max, mx[:, 0, hf:hf + 1])
            op.then_inc(S["s_read"], 1)
            dve.wait_ge(S["s_read"], n + 2)
            sk = nsk[:, bass.ds(i * 8 + j * 2, 2)]
            own.link(dve.scalar_tensor_tensor(out=mx[:, 1, :], in0=mx[:, 0, :], scalar=-1.0, in1=sk, op0=ALU.mult, op1=ALU.min))
            dve.tensor_tensor(mx[:, 2, :], mx[:, 1, :], sk, ALU.subtract).then_inc(S["negm"], 1)
            if b == NBLK - 1:
                dve.sem_inc(S["b_used"], 1)

        def softmax_out(i, j, b):
            n = i * 32 + j * NBLK + b
            lo = BLK if b == 0 else 0
            dve.wait_ge(S["p_exp"], n + 1)
            own.link(dve.tensor_tensor(mx[:, 5, :], mx[:, 3, :], mx[:, 4, :], ALU.add))
            own.link(dve.reciprocal(mx[:, 5, :], mx[:, 5, :]))
            for hf in range(2):
                s = pp[:, b % 2, hf, lo:2 * BLK]
                op = dve.tensor_scalar(s, s, mx[:, 5, hf:hf + 1], None, ALU.mult)
            op.then_inc(S["p_ready"], 1)

        def output(i, j, b):
            n = i * 32 + j * NBLK + b
            dve.wait_ge(S["o_low"], n + 1)
            for hf in range(2):
                op = dve.tensor_tensor(q[hf * HD:hf * HD + HD, j % 2, b * BLK:(b + 1) * BLK],
                                       ps[0:HD, X1, hf * BLK:(hf + 1) * BLK], ol[0:HD, hf * BLK:(hf + 1) * BLK], ALU.add)
            op.then_inc(S["o_read"], 1)

        def probs_lo(i, j, b):
            dve.wait_ge(S["pt_ready"], i * 32 + j * NBLK + b + 2)
            lo = BLK if b == 0 else 0
            dve.tensor_tensor(ptl[:, :, lo:2 * BLK], ps[:, X0, :].rearrange("p (h c) -> p h c", h=2)[:, :, lo:2 * BLK],
                              pt[:, b % 2, :, lo:2 * BLK].bitcast(F32), ALU.subtract).then_inc(S["pt_lo"], 1)

        def values_lo(i):
            dve.wait_ge(S["v_hi"], i + 1)
            for n in range(2):
                v = vn[:, n * 4:n * 4 + 4]
                op = dve.tensor_tensor(v[:, :, :, 1, :], ps[:, X0 + n, :].rearrange("p (b e d) -> p b e d", e=2, d=HD),
                                       v[:, :, :, 0, :].bitcast(F32), ALU.subtract)
            op.then_inc(S["v_lo"], 1)

        def chunk_out(i, c):
            what, j = B_CHUNKS[c]
            cc = i * NBC + c + C_B
            if what == "k":
                evac(cc, k1, c % 2, last=S["psum_read"])
            elif what == "v":
                evac(cc, gb, c % 2, last=S["psum_read"])
            elif what == "q":
                dve.wait_ge(S[f"yb_out{j % 2}"], i * 32 + 16 * (j // 2) + 16)
                evac(cc, q[:, j % 2, :], c % 2, scale=0.125, last=S["psum_read"])
                dve.wait_ge(S["psum_read"], cc + 3)
                at = bass.ds(i * 4 + j, 1)
                own.step(dve.tensor_copy(qs[:, at, 0, :].rearrange("p o n -> p (o n)"), q[:, j % 2, SEQ:NT]))
                own.step(dve.tensor_copy(qs[0:HD, at, 1, :].rearrange("p o n -> p (o n)"), q[HD:P, j % 2, SEQ:NT]))
                own.step(dve.tensor_copy(qs[HD:P, at, 1, :].rearrange("p o n -> p (o n)"), q[0:HD, j % 2, SEQ:NT]))
            else:
                evac(cc, gb, c % 2)

        def gate_out(i, c, step):
            j = B_CHUNKS[c][1]
            if step == 0:
                silu(i * 4 + j + 2 * A_ITERS, gb, c % 2)
            else:
                dve.wait_ge(S["psum_read"], i * NBC + c + C_B + 3)
                own.step(dve.tensor_copy(gsm[:, bass.ds(i * 4 + j, 1), :].rearrange("p o n -> p (o n)"), gb[:, SEQ:NT]))
                dve.wait_ge(S["o_read"], i * 32 + j * NBLK + NBLK + 1)
                dve.scalar_tensor_tensor(out=q[:, j % 2, 0:SEQ], in0=q[:, j % 2, 0:SEQ], scalar=0.5, in1=gb[:, 0:SEQ],
                                         op0=ALU.mult, op1=ALU.mult).then_inc(S["y_ready"], 1)
                dve.wait_ge(S["y_ready"], i * 4 + j + 1 + 2 * A_ITERS)

        base = own.end()
        with dve.Fori(0, B_ITERS) as i:
            own = Chain(dve, S["dve_step"], base, 4 * 3 + 4 + 32 * 3, i)
            todo = [(c * 8 + 8, 0, lambda c=c: chunk_out(i, c)) for c in range(NBC)]
            todo.append((2 * 8 + 3, 0, lambda: values_lo(i)))
            for c in G_CHUNK:
                todo.append((c * 8 + 8, 4, lambda c=c: gate_out(i, c, 0)))
                todo.append((c * 8 + 9, 4, lambda c=c: gate_out(i, c, 1)))
            for j in range(4):
                at = ATT_AT[j] * 8
                for b in range(NBLK):
                    todo.append((at + b + 4, 1, lambda j=j, b=b: output(i, j, b)))
                    todo.append((at + b + 1, 2, lambda j=j, b=b: softmax_out(i, j, b)))
                    todo.append((at + b + 2, 2.5, lambda j=j, b=b: probs_lo(i, j, b)))
                    todo.append((at + b, 3, lambda j=j, b=b: softmax_in(i, j, b)))
            for _, _, f in sorted(todo, key=lambda x: x[:2]):
                f()
        own = Chain(dve, S["dve_step"], own.end(B_ITERS))

        own.link(dve.memset(qbd[:].rearrange("p c b e j v -> p (c b e j v)"), 0.0))
        for e in range(2):
            rows_e = slice(e * HD, e * HD + HD)
            for c in range(4):
                for j in range(2):
                    op = dve.tensor_copy(qbd[rows_e, c, :, e, j, :], qs[rows_e, 4 * c + 2 * e + j, :, :].rearrange("p v b -> p b v"))
        op.then_inc(S["smp_q"], 1)
        restage(32, SEQ, (1, 2))
        dve.wait_ge(S["yb_out0"], 32 * B_ITERS + 16)
        dve.wait_ge(S["yb_out1"], 32 * B_ITERS + 16)
        dve.wait_ge(S["smp_pe"], 12)
        sav = sa[:, :, :].rearrange("p n c -> p (n c)").rearrange("p (c e b t) -> p c e b t", c=4, e=2, b=NB)
        bsv = bsm[:].rearrange("p (c e t) -> p c e t", c=4, e=2)
        psv = ps[:, 3, 0:256].rearrange("p (c b e t) -> p c b e t", c=4, e=2, b=NB)
        for e in range(2):
            for b in range(NB):
                op = dve.tensor_tensor(sav[:, :, e, b, :], psv[:, :, b, e, :], bsv[:, :, e, :], ALU.add)
        op.then_inc(S["smp_dve"], 1)
        skv = skr[:].rearrange("p (h b t) -> p h b t", h=NKV, b=NB)
        for b in range(NB):
            op = dve.tensor_copy(skv[:, :, b, :], skp[:].rearrange("p (h t) -> p h t", h=NKV))
        op.then_inc(S["smp_dve"], 1)
        dve.wait_ge(S["smp_pe"], 13)
        own.step(dve.tensor_reduce(sx[:, 0, :], ps[:, 5, 0:256].rearrange("p (n c) -> p n c", n=2), AXX, ALU.max))
        own.link(dve.tensor_copy(sx[:, 5, :], ps[:, 6, 0:2]))
        own.link(dve.tensor_tensor(sx[:, 0, :], sx[:, 0, :], sx[:, 5, :], ALU.max))
        own.link(dve.tensor_scalar(sx[:, 1, :], sx[:, 0, :], -1.0, None, ALU.mult))
        dve.tensor_tensor(sx[:, 2, :], sx[:, 5, :], sx[:, 1, :], ALU.add).then_inc(S["smp_dve"], 1)
        dve.wait_ge(S["smp_act"], 9)
        own.link(dve.tensor_tensor(sx[:, 5, :], sx[:, 3, :], sx[:, 4, :], ALU.add))
        own.link(dve.reciprocal(sx[:, 5, :], sx[:, 5, :]))
        for n in range(2):
            op = dve.tensor_scalar(sbm[:, n, :], sbm[:, n, :], sx[:, 5, n:n + 1], None, ALU.mult)
        op.then_inc(S["smp_dve"], 1)
        dve.wait_ge(S["smp_pe"], 14)
        dve.tensor_copy(sa[:, :, :].rearrange("p n c -> p (n c)"), ps[:, 7, 0:256]).then_inc(S["smp_dve"], 1)
        dve.wait_ge(S["smp_pe"], 15)
        ov = ps[:, 0, 0:256].rearrange("p (c b e j w) -> p c e b j w", c=4, e=2, b=NB, j=2)
        qv = qs[:].rearrange("p (c e j) v b -> p c e j v b", c=4, e=2)
        for e in range(2):
            for w in range(2):
                hf = e ^ w
                for j in range(2):
                    own.step(dve.tensor_copy(qv[hf * HD:hf * HD + HD, :, e, j, 0, :], ov[e * HD:e * HD + HD, :, e, :, j, w]))
        own.wait()
        own.link(dve.scalar_tensor_tensor(out=qs[:, :, 0, :], in0=qs[:, :, 0, :], scalar=0.5, in1=gsm[:], op0=ALU.mult, op1=ALU.mult))
        chunk_done(dve, C_O2 - 1)
        dve.tensor_copy(xsp[:, :, 0, SEQ:NT], qs[:, :, 0, :]).then_inc(S["smp_split"], 1)
        dve.wait_ge(S["smp_split"], 1)
        dve.tensor_tensor(xsp[:, :, 1, SEQ:NT], qs[:, :, 0, :], xsp[:, :, 0, SEQ:NT].bitcast(F32), ALU.subtract)\
            .then_inc(S["smp_split"], 1)
        clear_acc()
        restage(40, SEQ, (3, 0))
        out_phase(C_O2, 1)
        dve.sem_inc(S["acc_ready"], 1)
        norm(3, (S["norm_mm"], 2))
        dve.wait_ge(S["x1_back"], 16)
        base = own.end()
        for kq in range(NQ):
            dve.wait_ge(LAND[kq], FIN_LANDED[kq])
            with dve.Fori(0, 2) as n:
                own = Chain(dve, S["dve_step"], base, 1, n + kq * 2)
                for odd in range(2):
                    k = n * 2 + (kq * QK + odd)
                    o = land[:, bass.ds(k, 1), 0, :].rearrange("p o n -> p (o n)")
                    if kq < NQ - 1:
                        x1 = land[:, bass.ds(k, 1), 1, :].rearrange("p o n -> p (o n)")
                    else:
                        x1 = stg[:, bass.ds(n + 2, 1), odd, :].rearrange("p o n -> p (o n)")
                    if odd:
                        hold(dve, S["x1_scaled"], n + (KT + kq * 2 + 1))
                    else:
                        own.step(dve.tensor_tensor(o, o, rstd[:], ALU.mult))
                        hold(dve, S["dve_step"], n + (base + kq * 2 + 1))
                    dve.scalar_tensor_tensor(out=o, in0=o, scalar=prm[:, bass.ds(k, 1), R_BPOST:R_BPOST + 1].rearrange("p o n -> p (o n)"),
                                             in1=x1, op0=ALU.mult, op1=ALU.add).then_inc(S["fin_ready"], 1)


_OUTS = [("y_prompt", (1, SEQ, D)), ("y_sample", (NB, 1, D)), ("prompt_conv", (1, 1, 3, D)), ("prompt_h", (1, 1, D)),
         ("prompt_k", (1, BLK, NKV, HD)), ("prompt_v", (1, BLK, NKV, HD)), ("sample_conv", (1, NB, 3, D)),
         ("sample_h", (1, NB, D)), ("sample_k", (NB, 1, NKV, HD)), ("sample_v", (NB, 1, NKV, HD))]


def kernel(**inputs):
    import concourse.bacc as bacc
    from concourse.bass_utils import run_bass_kernel_spmd

    nc = bacc.Bacc("TRN2", target_bir_lowering=False, num_devices=1)
    arrays, t = {}, {}
    for name, a in {**inputs, "ident": np.eye(P, dtype=np.float32), "onehot": bucket_one_hot()}.items():
        a = np.ascontiguousarray(a)
        arrays[f"in_{name}"] = a
        t[name] = nc.dram_tensor(f"in_{name}", a.shape, mybir.dt.from_np(a.dtype), kind="ExternalInput").ap()
    for name, shape in _OUTS:
        t[name] = nc.dram_tensor(f"out_{name}", shape, F32, kind="ExternalOutput").ap()
    build(nc, t)
    r = run_bass_kernel_spmd(nc, [arrays], core_ids=[0])
    return tuple(r.results[0][f"out_{name}"] for name, _ in _OUTS)
```
